# Optimizing a Trainium2 kernel written in Bass

```python
import jax
import jax.numpy as jnp
from jax import lax
import numpy as np

D_MODEL = 1024
BATCH = 1
SEQ = 512
DEPTH = 2

GRID_W = 64
CTX_LEN = 256
EPS = 1e-6
ROPE_BASE = 10000.0
NEG_INF = -1e30
N_ADA = 6
MIX_WIDTH = D_MODEL
RET_HEADS = 4
RET_V_DIM = MIX_WIDTH // (2 * RET_HEADS)
RET_QK_DIM = RET_V_DIM // 2
RET_CHUNK = 128
CONV_CH = MIX_WIDTH // 2
CONV_K = 3
ATT_HEADS = 16
ATT_HEAD_DIM = MIX_WIDTH // ATT_HEADS
ATT_KV_HEADS = 4
ATT_GROUP = ATT_HEADS // ATT_KV_HEADS
WINDOW = 128
ATT_BLOCK = 128
PEER_HEADS = 8
PEER_N_KEYS = 128
PEER_N_EXPERTS = PEER_N_KEYS * PEER_N_KEYS
PEER_D_KEY = 128
PEER_TOPK = 16
PEER_TOKEN_BLOCK = 128
N_EVEN = (DEPTH + 1) // 2
N_ODD = DEPTH // 2
RET_Q_W = RET_HEADS * RET_QK_DIM
RET_V_W = RET_HEADS * RET_V_DIM
EV_SPLITS = (RET_Q_W, 2 * RET_Q_W, 2 * RET_Q_W + RET_V_W, 2 * RET_Q_W + 2 * RET_V_W,
             2 * RET_Q_W + 2 * RET_V_W + CONV_CH, 2 * RET_Q_W + 2 * RET_V_W + 2 * CONV_CH)
EV_IN_COLS = 2 * RET_Q_W + 2 * RET_V_W + 3 * CONV_CH
ATT_Q_W = ATT_HEADS * ATT_HEAD_DIM
ATT_KV_W = ATT_KV_HEADS * ATT_HEAD_DIM
OD_IN_COLS = ATT_Q_W + 2 * ATT_KV_W

kernel_name = 'hybrid_retention_shortconv_swa_peer_dit'

def rmsnorm(x, gain):
    x32 = x.astype(jnp.float32)
    y = x32 * lax.rsqrt(jnp.mean(x32 * x32, axis=-1, keepdims=True) + EPS)
    return (y * gain.astype(jnp.float32)).astype(x.dtype)

def head_rmsnorm(y):
    y32 = y.astype(jnp.float32)
    return y32 * lax.rsqrt(jnp.mean(y32 * y32, axis=-1, keepdims=True) + EPS)

def modulate(x, shift, scale):
    return x * (1.0 + scale) + shift

def axial_rope_tables(n_tok, head_dim):
    n_rows = n_tok // GRID_W
    rows = jnp.broadcast_to(jnp.arange(n_rows, dtype=jnp.float32)[:, None], (n_rows, GRID_W)).reshape(-1)
    cols = jnp.broadcast_to(jnp.arange(GRID_W, dtype=jnp.float32)[None, :], (n_rows, GRID_W)).reshape(-1)
    n_freq = head_dim // 4
    inv_freq = ROPE_BASE ** (-jnp.arange(n_freq, dtype=jnp.float32) / n_freq)
    ang = jnp.concatenate([rows[:, None] * inv_freq, cols[:, None] * inv_freq], axis=-1)
    return jnp.cos(ang), jnp.sin(ang)

def _rotate_half(u, cos, sin):
    n = u.shape[-1] // 2
    u1, u2 = u[..., :n], u[..., n:]
    return jnp.concatenate([u1 * cos - u2 * sin, u2 * cos + u1 * sin], axis=-1)

def apply_axial_rope(x, cos, sin):
    n = x.shape[-1] // 4
    c = cos[None, :, None, :]
    s = sin[None, :, None, :]
    xr = _rotate_half(x[..., :2 * n], c[..., :n], s[..., :n])
    xc = _rotate_half(x[..., 2 * n:], c[..., n:], s[..., n:])
    return jnp.concatenate([xr, xc], axis=-1).astype(x.dtype)

def short_conv(u, w):
    t = u.shape[1]
    pad = CONV_K // 2
    up = jnp.pad(u, ((0, 0), (pad, pad), (0, 0)))
    return sum(w[i] * up[:, i:i + t] for i in range(CONV_K))

def retention_chunked(q, k, v, log_gamma, state0):
    b, t, h, dk = q.shape
    dv = v.shape[-1]
    n = t // RET_CHUNK
    qc = q.reshape(b, n, RET_CHUNK, h, dk)
    kc = k.reshape(b, n, RET_CHUNK, h, dk)
    vc = v.reshape(b, n, RET_CHUNK, h, dv)
    pos = jnp.arange(RET_CHUNK, dtype=jnp.float32)
    diff = pos[:, None] - pos[None, :]
    decay_in = jnp.where(diff[None] >= 0,
                         jnp.exp(log_gamma[:, None, None] * jnp.maximum(diff, 0.0)[None]), 0.0)
    scores = jnp.einsum('bnihd,bnjhd->bnhij', qc, kc) * decay_in
    inner = jnp.einsum('bnhij,bnjhe->bnihe', scores, vc)
    zeta = jnp.exp(log_gamma[:, None] * (RET_CHUNK - 1 - pos)[None])
    kv = jnp.einsum('bnjhd,bnjhe,hj->nbhde', kc, vc, zeta)
    chunk_decay = jnp.exp(log_gamma * RET_CHUNK)[None, :, None, None]

    def step(state, kv_i):
        return chunk_decay * state + kv_i, state

    state_final, state_prev = lax.scan(step, state0, kv)
    xi = jnp.exp(log_gamma[None, :] * (pos[:, None] + 1.0))
    cross = jnp.einsum('bnihd,nbhde->bnihe', qc, state_prev) * xi[None, None, :, :, None]
    return (inner + cross).reshape(b, t, h, dv), state_final

def retention_final_state(k, v, log_gamma):
    t = k.shape[1]
    pos = jnp.arange(t, dtype=jnp.float32)
    w = jnp.exp(log_gamma[:, None] * (t - 1 - pos)[None])
    return jnp.einsum('bthd,bthe,ht->bhde', k, v, w)

def bidirectional_retention(q_l, k_l, v_l, q_c, k_c, v_c, log_f, log_b):
    b, _, h, dk = k_c.shape
    dv = v_c.shape[-1]
    flip = lambda a: a[:, ::-1]
    zeros = jnp.zeros((b, h, dk, dv), jnp.float32)
    if q_c is not None:
        ctx_f, s_f = retention_chunked(q_c, k_c, v_c, log_f, zeros)
        ctx_b, s_b = retention_chunked(flip(q_c), flip(k_c), flip(v_c), log_b, zeros)
        out_ctx = ctx_f + flip(ctx_b)
    else:
        s_f = retention_final_state(k_c, v_c, log_f)
        s_b = retention_final_state(flip(k_c), flip(v_c), log_b)
        out_ctx = None
    lat_f, _ = retention_chunked(q_l, k_l, v_l, log_f, s_f)
    lat_b, _ = retention_chunked(flip(q_l), flip(k_l), flip(v_l), log_b, s_b)
    return lat_f + flip(lat_b), out_ctx

def even_output(ret, g, gb, gc, xt, conv_w, w_out):
    b, t = ret.shape[:2]
    y_ret = (head_rmsnorm(ret).reshape(b, t, RET_V_W) * jax.nn.silu(g.astype(jnp.float32))).astype(g.dtype)
    y_conv = gb * short_conv(gc * xt, conv_w)
    return jnp.concatenate([y_ret, y_conv], axis=-1) @ w_out

def even_mixer(a_lat, a_ctx, w_in, w_out, logit_f, logit_b, conv_w, need_ctx):
    b, n_lat, _ = a_lat.shape
    n_ctx = a_ctx.shape[1]
    k_scale = RET_QK_DIM ** -0.5
    log_f = jax.nn.log_sigmoid(logit_f.astype(jnp.float32))
    log_b = jax.nn.log_sigmoid(logit_b.astype(jnp.float32))
    cos, sin = axial_rope_tables(n_lat, RET_QK_DIM)
    q_l, k_l, v_l, g_l, gb_l, gc_l, x_l = jnp.split(a_lat @ w_in, EV_SPLITS, axis=-1)
    q_l = apply_axial_rope(q_l.reshape(b, n_lat, RET_HEADS, RET_QK_DIM), cos, sin)
    k_l = apply_axial_rope(k_l.reshape(b, n_lat, RET_HEADS, RET_QK_DIM), cos, sin) * k_scale
    v_l = v_l.reshape(b, n_lat, RET_HEADS, RET_V_DIM)
    if need_ctx:
        q_c, k_c, v_c, g_c, gb_c, gc_c, x_c = jnp.split(a_ctx @ w_in, EV_SPLITS, axis=-1)
        q_c = q_c.reshape(b, n_ctx, RET_HEADS, RET_QK_DIM)
    else:
        k_c, v_c = jnp.split(a_ctx @ w_in[:, RET_Q_W:2 * RET_Q_W + RET_V_W], (RET_Q_W,), axis=-1)
        q_c = None
    k_c = k_c.reshape(b, n_ctx, RET_HEADS, RET_QK_DIM) * k_scale
    v_c = v_c.reshape(b, n_ctx, RET_HEADS, RET_V_DIM)
    ret_l, ret_c = bidirectional_retention(q_l, k_l, v_l, q_c, k_c, v_c, log_f, log_b)
    out_lat = even_output(ret_l, g_l, gb_l, gc_l, x_l, conv_w, w_out)
    out_ctx = even_output(ret_c, g_c, gb_c, gc_c, x_c, conv_w, w_out) if need_ctx else None
    return out_lat, out_ctx

def odd_mixer(a_lat, a_ctx, w_in, w_out, sinks, need_ctx):
    b, n_lat, _ = a_lat.shape
    n_ctx = a_ctx.shape[1]
    scale = ATT_HEAD_DIM ** -0.5
    cos, sin = axial_rope_tables(n_lat, ATT_HEAD_DIM)
    q, k, v = jnp.split(a_lat @ w_in, (ATT_Q_W, ATT_Q_W + ATT_KV_W), axis=-1)
    q = apply_axial_rope(q.reshape(b, n_lat, ATT_HEADS, ATT_HEAD_DIM), cos, sin) * scale
    k = apply_axial_rope(k.reshape(b, n_lat, ATT_KV_HEADS, ATT_HEAD_DIM), cos, sin)
    v = v.reshape(b, n_lat, ATT_KV_HEADS, ATT_HEAD_DIM)
    if need_ctx:
        q_c, k_c, v_c = jnp.split(a_ctx @ w_in, (ATT_Q_W, ATT_Q_W + ATT_KV_W), axis=-1)
    else:
        k_c, v_c = jnp.split(a_ctx @ w_in[:, ATT_Q_W:], (ATT_KV_W,), axis=-1)
    k_c = k_c.reshape(b, n_ctx, ATT_KV_HEADS, ATT_HEAD_DIM)
    v_c = v_c.reshape(b, n_ctx, ATT_KV_HEADS, ATT_HEAD_DIM)
    sink = sinks.astype(jnp.float32).reshape(ATT_KV_HEADS, ATT_GROUP)

    span = ATT_BLOCK + 2 * WINDOW
    k_pad = jnp.pad(k, ((0, 0), (WINDOW, WINDOW), (0, 0), (0, 0)))
    v_pad = jnp.pad(v, ((0, 0), (WINDOW, WINDOW), (0, 0), (0, 0)))
    p_idx = jnp.arange(ATT_BLOCK)
    r_idx = jnp.arange(span)
    band = (r_idx[None, :] >= p_idx[:, None]) & (r_idx[None, :] <= p_idx[:, None] + 2 * WINDOW)

    def attend_block(blk):
        start = blk * ATT_BLOCK
        qb = lax.dynamic_slice_in_dim(q, start, ATT_BLOCK, axis=1).reshape(
            b, ATT_BLOCK, ATT_KV_HEADS, ATT_GROUP, ATT_HEAD_DIM)
        kb = lax.dynamic_slice_in_dim(k_pad, start, span, axis=1)
        vb = lax.dynamic_slice_in_dim(v_pad, start, span, axis=1)
        key_pos = start - WINDOW + r_idx
        valid = band & ((key_pos >= 0) & (key_pos < n_lat))[None, :]
        s_win = jnp.where(valid, jnp.einsum('bqkgd,bskd->bkgqs', qb, kb).astype(jnp.float32), NEG_INF)
        s_ctx = jnp.einsum('bqkgd,bskd->bkgqs', qb, k_c).astype(jnp.float32)
        s_sink = jnp.broadcast_to(sink[None, :, :, None, None], (b, ATT_KV_HEADS, ATT_GROUP, ATT_BLOCK, 1))
        probs = jax.nn.softmax(jnp.concatenate([s_win, s_ctx, s_sink], axis=-1), axis=-1).astype(v.dtype)
        o = (jnp.einsum('bkgqs,bskd->bqkgd', probs[..., :span], vb)
             + jnp.einsum('bkgqs,bskd->bqkgd', probs[..., span:span + n_ctx], v_c))
        return o.reshape(b, ATT_BLOCK, ATT_Q_W)

    o_lat = lax.map(attend_block, jnp.arange(n_lat // ATT_BLOCK))
    out_lat = jnp.moveaxis(o_lat, 0, 1).reshape(b, n_lat, ATT_Q_W) @ w_out
    if need_ctx:
        qc = q_c.reshape(b, n_ctx, ATT_KV_HEADS, ATT_GROUP, ATT_HEAD_DIM) * scale
        s = jnp.einsum('bqkgd,bskd->bkgqs', qc, k_c).astype(jnp.float32)
        s_sink = jnp.broadcast_to(sink[None, :, :, None, None], (b, ATT_KV_HEADS, ATT_GROUP, n_ctx, 1))
        probs = jax.nn.softmax(jnp.concatenate([s, s_sink], axis=-1), axis=-1).astype(v_c.dtype)
        o_c = jnp.einsum('bkgqs,bskd->bqkgd', probs[..., :n_ctx], v_c)
        out_ctx = o_c.reshape(b, n_ctx, ATT_Q_W) @ w_out
    else:
        out_ctx = None
    return out_lat, out_ctx

def peer_ffn(xn, wq, keys1, keys2, u_tab, v_tab):
    t, d = xn.shape
    half = PEER_D_KEY // 2
    q = (xn @ wq).reshape(t, PEER_HEADS, PEER_D_KEY)
    s1 = jnp.einsum('thd,hkd->thk', q[..., :half], keys1).astype(jnp.float32)
    s2 = jnp.einsum('thd,hkd->thk', q[..., half:], keys2).astype(jnp.float32)
    v1, i1 = lax.top_k(s1, PEER_TOPK)
    v2, i2 = lax.top_k(s2, PEER_TOPK)
    cand = (v1[..., :, None] + v2[..., None, :]).reshape(t, PEER_HEADS, PEER_TOPK * PEER_TOPK)
    cs, ci = lax.top_k(cand, PEER_TOPK)
    e1 = jnp.take_along_axis(i1, ci // PEER_TOPK, axis=-1)
    e2 = jnp.take_along_axis(i2, ci % PEER_TOPK, axis=-1)
    expert = e1 * PEER_N_KEYS + e2
    gate = jax.nn.softmax(cs, axis=-1).astype(xn.dtype)
    nb = t // PEER_TOKEN_BLOCK

    def block(args):
        xb, eb, gb = args
        ub = u_tab[eb]
        vb = v_tab[eb]
        act = jax.nn.gelu(jnp.einsum('td,thkd->thk', xb, ub), approximate=False)
        return jnp.einsum('thk,thkd->td', gb * act, vb)

    out = lax.map(block, (xn.reshape(nb, PEER_TOKEN_BLOCK, d),
                          expert.reshape(nb, PEER_TOKEN_BLOCK, PEER_HEADS, PEER_TOPK),
                          gate.reshape(nb, PEER_TOKEN_BLOCK, PEER_HEADS, PEER_TOPK)))
    return out.reshape(t, d)

def setup_inputs(seed: int = 0) -> dict:
    key = jax.random.key(seed)
    ks = jax.random.split(key, 24)
    f32 = jnp.float32
    nrm = lambda k, shape, s: jax.random.normal(k, shape, f32) * s
    ret_base = jnp.log(2.0 ** (5.0 + jnp.arange(RET_HEADS, dtype=f32)) - 1.0)
    return {
        'x': nrm(ks[0], (BATCH, SEQ, D_MODEL), 1.0),
        'c': nrm(ks[1], (BATCH, D_MODEL), 1.0),
        'ctx': nrm(ks[2], (BATCH, CTX_LEN, D_MODEL), 1.0),
        'c_ctx': nrm(ks[3], (D_MODEL,), 1.0),
        'ada_w': nrm(ks[4], (DEPTH, D_MODEL, N_ADA * D_MODEL), 0.5 * D_MODEL ** -0.5),
        'ada_b': nrm(ks[5], (DEPTH, N_ADA * D_MODEL), 0.01),
        'mix_norm_g': 1.0 + nrm(ks[6], (DEPTH, D_MODEL), 0.02),
        'ffn_norm_g': 1.0 + nrm(ks[7], (DEPTH, D_MODEL), 0.02),
        'ev_w_in': nrm(ks[8], (N_EVEN, D_MODEL, EV_IN_COLS), D_MODEL ** -0.5),
        'ev_w_out': nrm(ks[9], (N_EVEN, MIX_WIDTH, D_MODEL), MIX_WIDTH ** -0.5),
        'ret_decay_logit_f': ret_base[None] + nrm(ks[10], (N_EVEN, RET_HEADS), 0.1),
        'ret_decay_logit_b': ret_base[None] + nrm(ks[11], (N_EVEN, RET_HEADS), 0.1),
        'conv_w': nrm(ks[12], (N_EVEN, CONV_K, CONV_CH), CONV_K ** -0.5),
        'od_w_in': nrm(ks[13], (N_ODD, D_MODEL, OD_IN_COLS), D_MODEL ** -0.5),
        'od_w_out': nrm(ks[14], (N_ODD, MIX_WIDTH, D_MODEL), MIX_WIDTH ** -0.5),
        'attn_sinks': nrm(ks[15], (N_ODD, ATT_HEADS), 0.5),
        'peer_wq': nrm(ks[16], (DEPTH, D_MODEL, PEER_HEADS * PEER_D_KEY), D_MODEL ** -0.5),
        'peer_keys1': nrm(ks[17], (DEPTH, PEER_HEADS, PEER_N_KEYS, PEER_D_KEY // 2), (PEER_D_KEY // 2) ** -0.5),
        'peer_keys2': nrm(ks[18], (DEPTH, PEER_HEADS, PEER_N_KEYS, PEER_D_KEY // 2), (PEER_D_KEY // 2) ** -0.5),
        'peer_u': nrm(ks[19], (DEPTH, PEER_N_EXPERTS, D_MODEL), D_MODEL ** -0.5),
        'peer_v': nrm(ks[20], (DEPTH, PEER_N_EXPERTS, D_MODEL), PEER_HEADS ** -0.5),
        'final_norm_g': 1.0 + nrm(ks[21], (D_MODEL,), 0.02),
    }

def reference(x, c, ctx, c_ctx, ada_w, ada_b, mix_norm_g, ffn_norm_g, ev_w_in, ev_w_out,
              ret_decay_logit_f, ret_decay_logit_b, conv_w, od_w_in, od_w_out, attn_sinks,
              peer_wq, peer_keys1, peer_keys2, peer_u, peer_v, final_norm_g):
    h_lat, h_ctx = x, ctx
    silu_c = jax.nn.silu(c)
    silu_cc = jax.nn.silu(c_ctx)
    for layer in range(DEPTH):
        need_ctx = layer < DEPTH - 1
        j = layer // 2
        mod_lat = (silu_c @ ada_w[layer] + ada_b[layer])[:, None, :]
        mod_ctx = silu_cc @ ada_w[layer] + ada_b[layer]
        sh1, sc1, g1, sh2, sc2, g2 = jnp.split(mod_lat, N_ADA, axis=-1)
        csh1, csc1, cg1, csh2, csc2, cg2 = jnp.split(mod_ctx, N_ADA, axis=-1)
        a_lat = modulate(rmsnorm(h_lat, mix_norm_g[layer]), sh1, sc1)
        a_ctx = modulate(rmsnorm(h_ctx, mix_norm_g[layer]), csh1, csc1)
        if layer % 2 == 0:
            m_lat, m_ctx = even_mixer(a_lat, a_ctx, ev_w_in[j], ev_w_out[j], ret_decay_logit_f[j],
                                      ret_decay_logit_b[j], conv_w[j], need_ctx)
        else:
            m_lat, m_ctx = odd_mixer(a_lat, a_ctx, od_w_in[j], od_w_out[j], attn_sinks[j], need_ctx)
        h_lat = h_lat + g1 * m_lat
        f_lat = modulate(rmsnorm(h_lat, ffn_norm_g[layer]), sh2, sc2)
        if need_ctx:
            h_ctx = h_ctx + cg1 * m_ctx
            f_ctx = modulate(rmsnorm(h_ctx, ffn_norm_g[layer]), csh2, csc2)
            n_ctx_tok = f_ctx.shape[0] * f_ctx.shape[1]
            tokens = jnp.concatenate([f_ctx.reshape(-1, D_MODEL), f_lat.reshape(-1, D_MODEL)], axis=0)
            y = peer_ffn(tokens, peer_wq[layer], peer_keys1[layer], peer_keys2[layer], peer_u[layer], peer_v[layer])
            h_ctx = h_ctx + cg2 * y[:n_ctx_tok].reshape(h_ctx.shape)
            y_lat = y[n_ctx_tok:].reshape(h_lat.shape)
        else:
            y_lat = peer_ffn(f_lat.reshape(-1, D_MODEL), peer_wq[layer], peer_keys1[layer], peer_keys2[layer],
                             peer_u[layer], peer_v[layer]).reshape(h_lat.shape)
        h_lat = h_lat + g2 * y_lat
    return rmsnorm(h_lat, final_norm_g)


_drawn_inputs = setup_inputs


def setup_inputs(seed=0):
    import zlib

    import numpy as np

    out = dict(_drawn_inputs(seed))
    spreads = {}
    factors = {'ada_b': 3.265,
     'mix_norm_g': 4.074,
     'ffn_norm_g': 36.648,
     'attn_sinks': 8.0,
     'final_norm_g': 20.172,
     'ret_decay_logit_f': 28.528,
     'ret_decay_logit_b': 28.968}
    for name, (base, spread) in spreads.items():
        noise = np.random.default_rng([zlib.crc32(name.encode()), seed]).standard_normal(out[name].shape)
        drawn = base * np.exp(spread * noise) if base else spread * noise
        out[name] = jnp.asarray(drawn.astype(out[name].dtype))
    for name, factor in factors.items():
        out[name] = (out[name] * factor).astype(out[name].dtype)
    return out
```

```python
from contextlib import ExitStack

import numpy as np

import concourse.bass as bass
from concourse import mybir

ALU = mybir.AluOpType
ACT = mybir.ActivationFunctionType
AX = mybir.AxisListType
F32 = mybir.dt.float32
U32 = mybir.dt.uint32

P = 128
D = 1024
KC = D // P
CTX, SEQ = 256, 512
CT, LT = CTX // P, SEQ // P
NT = CT + LT
TOK = CTX + SEQ
DEPTH = 2
EPS = 1e-6
HALF = 512
RET_HEADS, RET_V = 4, 128
HD = 64
ATT_HEADS, KV_HEADS = 16, 4
SCALE = HD ** -0.5
GRID_W, ROPE_BASE = 64, 10000.0
NEG = -1e30
NH, NK, TOPK = 8, 128, 16
EXPERTS = NK * NK
RING = 8
PAIR = 2
PAIRS = TOPK // PAIR
LAG = 2
TAKEN = -3.0e38


def kind(t):
    return int(t >= CT)


class Sems:

    def __init__(self, nc, ctx):
        self.nc, self.ctx, self.made = nc, ctx, {}

    def __call__(self, name):
        if name not in self.made:
            self.made[name] = self.ctx.enter_context(self.nc.semaphore(name))
        return self.made[name]


def modulation_stage(nc, S, A, h, ident, mod_d, strips):
    n_chunk, ring = DEPTH * 12, 3
    with ExitStack() as ctx:
        def sb(name, shape, dt=F32):
            return ctx.enter_context(nc.sbuf_tensor(name, shape, dt))
        crow = sb("crow", [P, 2, KC])
        silu = sb("silu", [P, 2, KC])
        ada = sb("ada", [P, ring, KC, HALF])
        bias = sb("ada_bias", [2, DEPTH * 6 * D])
        gain = sb("norm_gain", [2, DEPTH * 2 * D])
        row = sb("mod_row", [2, 4, HALF])
        tmp = sb("mod_tmp", [2, 2, HALF])
        lg = sb("decay_log", [P, 5, 2 * RET_HEADS])
        dist = sb("distance", [P, 3, SL])
        cdist = sb("ctx_distance", [P, 2, SC])
        dec = sb("decays", [P, 2, SL])
        ps = ctx.enter_context(nc.psum_tensor("mod_ps", [2, 4, HALF], F32))
        block = ctx.enter_context(nc.Block())

        def chunk(n):
            layer, c = divmod(n, 12)
            return layer, c // 6, (c % 6) // 2, c % 2

        @block.sync
        def _(sp):
            sp.dma_start(crow[:, 0, :], A["c_ctx"].rearrange("(p k) -> p k", p=P)).then_inc(S("c_loaded"), 16)
            sp.dma_start(crow[:, 1, :], A["c"].rearrange("a (p k) -> p (a k)", p=P)).then_inc(S("c_loaded"), 16)
            sp.dma_start(lg[:, 0, 0:RET_HEADS], A["ret_decay_logit_f"].broadcast_to([P, RET_HEADS])).then_inc(S("logits"), 16)
            sp.dma_start(lg[:, 0, RET_HEADS:], A["ret_decay_logit_b"].broadcast_to([P, RET_HEADS])).then_inc(S("logits"), 16)
            sp.dma_start(bias[:], A["ada_b"].rearrange("(a l) n -> a (l n)", a=1).broadcast_to([2, DEPTH * 6 * D])
                         ).then_inc(S("rows_loaded"), 16)
            sp.dma_start(gain[:], A["gains"].rearrange("(a l) n -> a (l n)", a=1).broadcast_to([2, DEPTH * 2 * D])
                         ).then_inc(S("rows_loaded"), 16)
            for n in range(n_chunk):
                layer, half, sec, ch = chunk(n)
                if n >= ring:
                    sp.wait_ge(S("mod_mm"), n - ring + 1)
                col = ((half * 3 + sec) * 2 + ch) * HALF
                sp.dma_start(ada[:, n % ring], A["ada_w"][layer].rearrange("(p k) n -> p k n", p=P)[:, :, col:col + HALF]
                             ).then_inc(S(f"ada_loaded{n % ring}"), 16)
                if n == 4:
                    sp.dma_start(h[:, 0:CT], A["ctx"][0].rearrange("(t p) d -> p t d", p=P)).then_inc(S("h_loaded"), 16)
                    sp.dma_start(h[:, CT:NT], A["x"][0].rearrange("(t p) d -> p t d", p=P)).then_inc(S("h_loaded"), 16)
            sp.wait_ge(S("h_loaded"), 32)

        @block.gpsimd
        def _(pool):
            pool.memset(ident[:], 0.0).then_inc(S("ident_zero"), 1)
            pool.wait_ge(S("ident_zero"), 1)
            pool.affine_select(out=ident[:], in_=ident[:], compare_op=ALU.not_equal, fill=1.0, base=0,
                               pattern=[[-1, P]], channel_multiplier=1).then_inc(S("ident_ready"), 1)
            few = dict(allow_small_or_imprecise_dtypes=True)
            pool.iota(dist[:, 0], [[1, SL]], base=-3 * P, channel_multiplier=-1, **few).then_inc(S("distances"), 1)
            pool.iota(cdist[:, 0], [[1, SC]], base=CTX - P, channel_multiplier=-1, **few).then_inc(S("distances"), 1)
            pool.iota(cdist[:, 1], [[-1, SC]], base=SEQ + P, channel_multiplier=1, **few).then_inc(S("distances"), 1)

        @block.scalar
        def _(act):
            act.wait_ge(S("c_loaded"), 32)
            act.activation(silu[:], crow[:], ACT.Silu).then_inc(S("silu_ready"), 1)
            act.wait_ge(S("logits_abs"), 1)
            act.activation(lg[:, 2], lg[:, 1], ACT.Exp, scale=-1.0).then_inc(S("logits_exp"), 1)
            act.wait_ge(S("logits_exp"), 1)
            act.activation(lg[:, 3], lg[:, 2], ACT.Ln, bias=1.0).then_inc(S("logits_ln"), 1)
            act.wait_ge(S("log_gamma"), 1)
            act.wait_ge(S("distances"), 3)
            for m in range(2 * RET_HEADS):
                hd, cross = m // 2, m % 2
                for way in range(2):
                    if m:
                        act.wait_ge(S("strip"), m)
                    src = cdist[:, way] if cross else dist[:, 1 + way]
                    dst = dec[:, way, 0:SC] if cross else dec[:, way]
                    act.activation(dst, src, ACT.Exp, scale=lg[:, 4, way * RET_HEADS + hd:way * RET_HEADS + hd + 1]
                                   ).then_inc(S("decay"), 1)
            for n in range(n_chunk):
                layer, half, sec, ch = chunk(n)
                act.wait_ge(S("mod_row"), n + 1)
                act.dma_start(mod_d[layer, half, :, sec, ch * HALF:(ch + 1) * HALF], row[:, n % 4]
                              ).then_inc(S(f"mod_stored{n % 4}"), 16)
            for b in range(4):
                act.wait_ge(S(f"mod_stored{b}"), 16 * (n_chunk // 4))

        @block.tensor
        def _(pe):
            pe.wait_ge(S("silu_ready"), 1)
            for n in range(n_chunk):
                pe.wait_ge(S(f"ada_loaded{n % ring}"), 16 * (n // ring + 1))
                if n >= 4:
                    pe.wait_ge(S("mod_row"), n - 3)
                for k in range(KC):
                    ins = pe.matmul(ps[:, n % 4], silu[:, :, k], ada[:, n % ring, k], start=k == 0, stop=k == KC - 1)
                ins.then_inc(S("mod_mm"), 1)

        @block.vector
        def _(dve):
            dve.wait_ge(S("logits"), 32)
            dve.scalar_tensor_tensor(lg[:, 1], lg[:, 0], -1.0, lg[:, 0], ALU.mult, ALU.max).then_inc(S("logits_abs"), 1)
            dve.wait_ge(S("distances"), 3)
            dve.tensor_scalar(dist[:, 1], dist[:, 0], 0.0, None, ALU.max).then_inc(S("clamped"), 1)
            dve.tensor_scalar(dist[:, 2], dist[:, 0], -1.0, 0.0, ALU.mult, ALU.max).then_inc(S("clamped"), 1)
            dve.wait_ge(S("clamped"), 2)
            dve.wait_ge(S("logits_ln"), 1)
            dve.scalar_tensor_tensor(lg[:, 4], lg[:, 0], 0.0, lg[:, 3], ALU.min, ALU.subtract).then_inc(S("log_gamma"), 1)
            for m in range(2 * RET_HEADS):
                hd, cross = m // 2, m % 2
                dve.wait_ge(S("decay"), 2 * (m + 1))
                if cross:
                    dve.tensor_tensor(strips[:, hd, SL:SL + SC], dec[:, 0, 0:SC], dec[:, 1, 0:SC], ALU.add).then_inc(S("strip"), 1)
                    continue
                for way, op in enumerate((ALU.is_ge, ALU.is_le)):
                    dve.scalar_tensor_tensor(dec[:, way], dist[:, 0], 0.0, dec[:, way], op, ALU.mult).then_inc(S("masked"), 1)
                dve.wait_ge(S("masked"), m + 2)
                dve.tensor_tensor(strips[:, hd, 0:SL], dec[:, 0], dec[:, 1], ALU.add).then_inc(S("strip"), 1)
            dve.wait_ge(S("rows_loaded"), 32)
            scaled = 0
            for n in range(n_chunk):
                layer, half, sec, ch = chunk(n)
                dve.wait_ge(S("mod_mm"), n + 1)
                if n >= 4:
                    dve.wait_ge(S(f"mod_stored{n % 4}"), 16 * (n // 4))
                b = bias[:, (layer * 12 + n % 12) * HALF:(layer * 12 + n % 12 + 1) * HALF]
                if sec != 1:
                    dve.tensor_tensor(row[:, n % 4], ps[:, n % 4], b, ALU.add).then_inc(S("mod_row"), 1)
                    continue
                g = gain[:, ((layer * 2 + half) * 2 + ch) * HALF:((layer * 2 + half) * 2 + ch + 1) * HALF]
                dve.tensor_tensor(tmp[:, ch], ps[:, n % 4], b, ALU.add).then_inc(S("mod_scale"), 1)
                scaled += 1
                dve.wait_ge(S("mod_scale"), scaled)
                dve.scalar_tensor_tensor(row[:, n % 4], tmp[:, ch], 1.0, g, ALU.add, ALU.mult).then_inc(S("mod_row"), 1)


def norm_squares(act, S, tag, h, junk, ss):
    for t in range(NT):
        act.activation(junk, h[:, t], ACT.Square, accum_out=ss[:, 0, t:t + 1]).then_inc(S(tag + "_squares"), 1)
        act.wait_ge(S(tag + "_squares"), t + 1)
    act.wait_ge(S(tag + "_ms"), 1)
    act.activation(ss[:, 2], ss[:, 1], ACT.Sqrt).then_inc(S(tag + "_root"), 1)


def norm_modulate(dve, S, tag, h, a, ss, rows):
    dve.wait_ge(S(tag + "_squares"), NT)
    dve.tensor_scalar(ss[:, 1], ss[:, 0], 1.0 / D, EPS, ALU.mult, ALU.add).then_inc(S(tag + "_ms"), 1)
    dve.wait_ge(S(tag + "_root"), 1)
    dve.reciprocal(ss[:, 3], ss[:, 2]).then_inc(S(tag + "_rstd"), 1)
    dve.wait_ge(S(tag + "_rstd"), 1)
    dve.wait_ge(S(tag + "_rows"), 32)
    for t in range(NT):
        if t >= 2:
            dve.wait_ge(S(tag + "_aT_ps"), t - 1)
        dve.scalar_tensor_tensor(a[:, t % 2], h[:, t], ss[:, 3, t:t + 1], rows[:, kind(t), 1], ALU.mult, ALU.mult)\
            .then_inc(S(tag + "_scaled"), 1)
        dve.wait_ge(S(tag + "_scaled"), t + 1)
        dve.tensor_tensor(a[:, t % 2], a[:, t % 2], rows[:, kind(t), 0], ALU.add).then_inc(S(tag + "_a"), 1)


def norm_transpose(pe, S, tag, PS, a, ident):
    pe.wait_ge(S("ident_ready"), 1)
    for t in range(NT):
        pe.wait_ge(S(tag + "_a"), t + 1)
        if t >= 2:
            pe.wait_ge(S(tag + "_aT"), t - 1)
        for k in range(KC):
            ins = pe.transpose(PS[:, 2 * (t % 2) + k // 4, (k % 4) * P:(k % 4 + 1) * P], a[:, t % 2, k * P:(k + 1) * P], ident[:])
        ins.then_inc(S(tag + "_aT_ps"), 1)


def norm_evacuate(act, S, tag, PS, aT):
    for t in range(NT):
        act.wait_ge(S(tag + "_aT_ps"), t + 1)
        act.activation(aT[:, :, t * P:(t + 1) * P],
                       PS[:, 2 * (t % 2):2 * (t % 2) + 2].rearrange("p b (k n) -> p (b k) n", k=4), ACT.Copy
                       ).then_inc(S(tag + "_aT"), 1)


def residual(dve, S, tag, h, PS, rows, tmp, tiles):
    for n in range(2 * len(tiles)):
        c, t = n // len(tiles), tiles[n % len(tiles)]
        dve.wait_ge(S(tag + "_out"), n + 1)
        if n >= 2:
            dve.wait_ge(S(tag + "_added"), n - 1)
        cols = slice(c * HALF, (c + 1) * HALF)
        dve.tensor_tensor(tmp[:, n % 2], PS[:, 6 + n % 2], rows[:, kind(t), 2, cols], ALU.mult).then_inc(S(tag + "_out_read"), 1)
        dve.wait_ge(S(tag + "_out_read"), n + 1)
        dve.tensor_tensor(h[:, t, cols], h[:, t, cols], tmp[:, n % 2], ALU.add).then_inc(S(tag + "_added"), 1)


def rope(dve, S, tag, n, outs, ps, t1, t2, cos, sin, heads):
    w = heads * HD

    def halves(x):
        return x.rearrange("p (g a n) -> p g a n", g=2 * heads, a=2)

    def by_head(x):
        return x.rearrange("p (h n) -> p h n", h=heads)

    if n:
        dve.wait_ge(S(tag + "_rope_out"), n)
    dve.tensor_tensor(by_head(t1[:, 0:w]), by_head(ps), cos.rearrange("p (o n) -> p o n", o=1).broadcast_to([P, heads, HD]),
                      ALU.mult).then_inc(S(tag + "_rope"), 1)
    for a in range(2):
        table = sin.rearrange("p (x a n) -> p x a n", x=2, a=2)[:, :, a]
        for x in range(2):
            o = t2[:, 0:w].rearrange("p (h x a n) -> p h x a n", h=heads, x=2, a=2)[:, :, x, a]
            u = ps.rearrange("p (h x a n) -> p h x a n", h=heads, x=2, a=2)[:, :, x, 1 - a]
            s = table[:, x].rearrange("p (o n) -> p o n", o=1).broadcast_to([P, heads, 16])
            dve.tensor_tensor(o, u, s, ALU.mult).then_inc(S(tag + "_rope"), 1)
    dve.wait_ge(S(tag + "_rope"), 5 * (n + 1))
    for m, o in enumerate(outs):
        ins = dve.tensor_tensor(o, by_head(t1[:, 0:w]), by_head(t2[:, 0:w]), ALU.add)
        if m < len(outs) - 1:
            ins.then_inc(S(tag + "_rope_dup"), 1)
    return ins.then_inc(S(tag + "_rope_out"), 1)


def load_rows(sp, S, mod_d, rows, layer, half, name):
    for kd in range(2):
        sp.dma_start(rows[:, kd], mod_d[layer, half, kd].rearrange("(o s) d -> o s d", o=1).broadcast_to([P, 3, D])
                     ).then_inc(S(name), 16)


SL = 3 * P + SEQ
SC = P + SEQ


def mixer0_stage(nc, S, A, h, ident, mod_d, strips):
    n_in, ring = 6, 2
    with ExitStack() as ctx:
        def sb(name, shape, dt=F32):
            return ctx.enter_context(nc.sbuf_tensor("m0_" + name, shape, dt))
        rows = sb("rows", [P, 2, 3, D])
        aT = sb("aT", [P, KC, TOK])
        w = sb("w", [P, ring, KC, HALF])
        v = sb("v", [P, NT, HALF])
        sg = sb("sg", [P, NT, HALF])
        qT = sb("qT", [P, 2, TOK])
        kT = sb("kT", [P, 2, TOK])
        gb = sb("gb", [P, 4, TOK])
        u = sb("u", [P, 4, TOK])
        cos = sb("cos", [P, LT, HD])
        sin = sb("sin", [P, LT, HD])
        cw = sb("cw", [P, 4, 3])
        ss = sb("ss", [P, 4, NT])
        hs = sb("hs", [P, 4, 2 * RET_HEADS, LT])
        a = sb("a", [P, 2, D])
        sq = sb("sq", [P, D])
        PS = ctx.enter_context(nc.psum_tensor("m0_ps", [P, 8, HALF], F32))
        block = ctx.enter_context(nc.Block())
        PT = a[:].rearrange("p a (b n) -> p (a b) n", b=2)
        yr = aT[:, 0:4].rearrange("p k n -> p (k n)").rearrange("p (t n) -> p t n", t=NT)
        yc = aT[:, 4:8]
        yrT = v[:].rearrange("p t n -> p (t n)").rearrange("p (k n) -> p k n", k=4)
        T = "m0"
        n_tok, n_ch = 3 * NT, 8

        items = []
        for hd in range(RET_HEADS):
            items += [(hd, 0, j) for j in range(CT)] + [(hd, 1, j) for j in range(NT)]

        @block.sync
        def _(sp):
            load_rows(sp, S, mod_d, rows, 0, 0, "m0_rows")
            sp.dma_start(cos[:], A["rope_cos"].rearrange("(t p) n -> p t n", p=P)).then_inc(S("m0_tabs"), 16)
            sp.dma_start(sin[:], A["rope_sin"].rearrange("(t p) n -> p t n", p=P)).then_inc(S("m0_tabs"), 16)
            sp.dma_start(cw[:], A["conv_wT"].rearrange("(m p) i -> p m i", p=P)).then_inc(S("m0_tabs"), 16)
            for n in range(n_in + 2):
                if n >= ring:
                    c = n - ring
                    sp.wait_ge(S("m0_proj"), NT * (c + 1) if c < 3 else n_tok + n_ch * (c - 2))
                src = A["ev_w_in"][0] if n < n_in else A["ev_w_out"][0]
                c = (n if n < n_in else n - n_in) * HALF
                sp.dma_start(w[:, n % ring], src.rearrange("(k p) n -> p k n", p=P)[:, :, c:c + HALF]
                             ).then_inc(S(f"m0_w{n % ring}"), 16)

        @block.scalar
        def _(act):
            norm_squares(act, S, T, h, sq[:], ss)
            norm_evacuate(act, S, T, PS, aT)
            for n in range(NT, n_tok):
                c, t = divmod(n, NT)
                act.wait_ge(S("m0_proj"), n + 1)
                dst = v if c == 1 else sg
                act.activation(dst[:, t], PS[:, 4 + n % 4], ACT.Copy if c == 1 else ACT.Silu).then_inc(S("m0_ev"), 1)
                if n == 2 * NT - 1:
                    for t in range(NT):
                        act.wait_ge(S("m0_qkT_ps"), t + 1)
                        blk = PS[:, t % 2].rearrange("p (b n) -> p b n", b=4)
                        act.activation(qT[:, :, t * P:(t + 1) * P], blk[:, 0:2], ACT.Copy).then_inc(S("m0_qT"), 1)
                        act.activation(kT[:, :, t * P:(t + 1) * P], blk[:, 2:4], ACT.Copy, scale=SCALE).then_inc(S("m0_qT"), 1)
            for i in range(2 * n_ch):
                n = n_tok + i
                m, th = divmod(i % n_ch, 2)
                act.wait_ge(S("m0_proj"), n + 1)
                act.activation((gb if i < n_ch else u)[:, m, th * 3 * P:(th + 1) * 3 * P], PS[:, 4 + n % 4, 0:3 * P], ACT.Copy
                               ).then_inc(S("m0_ev"), 1)
            for g in range(2 * RET_HEADS):
                nt = LT if g % 2 else CT
                act.wait_ge(S("m0_pv"), g // 2 * (CT + NT) + (CT + NT if g % 2 else CT))
                if g:
                    act.wait_ge(S("m0_ret_ss"), g)
                act.activation(sq[:, 0:nt * P], PS[:, 4 + g % 2, 0:nt * P], ACT.Square).then_inc(S("m0_ret_sq"), 1)
                act.wait_ge(S("m0_ret_ms"), g + 1)
                act.activation(hs[:, 2, g, 0:nt], hs[:, 1, g, 0:nt], ACT.Sqrt).then_inc(S("m0_ret_root"), 1)
            for t in range(NT):
                act.wait_ge(S("m0_yT_ps"), t + 1)
                act.activation(yrT[:, :, t * P:(t + 1) * P], PS[:, t % 2].rearrange("p (b n) -> p b n", b=4), ACT.Copy
                               ).then_inc(S("m0_yT"), 1)

        @block.tensor
        def _(pe):
            def bank_free(n):
                if n < NT:
                    pe.wait_ge(S("m0_qk"), n + 1)
                elif n < n_tok + 2 * n_ch:
                    pe.wait_ge(S("m0_ev"), n - NT + 1)
                else:
                    pe.wait_ge(S("m0_u"), n - n_tok - 2 * n_ch + 1)

            norm_transpose(pe, S, T, PS, a, ident)
            pe.wait_ge(S("m0_aT"), NT)
            n = 0
            for c in range(3):
                pe.wait_ge(S(f"m0_w{c % ring}"), 16 * (c // ring + 1))
                for t in range(NT):
                    if n >= 4:
                        bank_free(n - 4)
                    for k in range(KC):
                        ins = pe.matmul(PS[:, 4 + n % 4], aT[:, k, t * P:(t + 1) * P], w[:, c % ring, k], start=k == 0, stop=k == KC - 1)
                    ins.then_inc(S("m0_proj"), 1)
                    n += 1
                if c == 1:
                    for t in range(NT):
                        pe.wait_ge(S("m0_qk"), t + 1)
                        if t >= 2:
                            pe.wait_ge(S("m0_qT"), 2 * (t - 1))
                        for m in range(4):
                            ins = pe.transpose(PS[:, t % 2, m * P:(m + 1) * P], sg[:, t, m * P:(m + 1) * P], ident[:])
                        ins.then_inc(S("m0_qkT_ps"), 1)
            for c in range(3, 6):
                pe.wait_ge(S(f"m0_w{c % ring}"), 16 * (c // ring + 1))
                for m in range(4):
                    for th in range(2):
                        bank_free(n - 4)
                        for k in range(KC):
                            ins = pe.matmul(PS[:, 4 + n % 4, 0:3 * P], w[:, c % ring, k, m * P:(m + 1) * P],
                                            aT[:, k, th * 3 * P:(th + 1) * 3 * P], start=k == 0, stop=k == KC - 1)
                        ins.then_inc(S("m0_proj"), 1)
                        n += 1
            for m in range(n - 4, n):
                bank_free(m)
            pe.wait_ge(S("m0_qT"), 2 * NT)

            def scores(i):
                hd, kd, j = items[i]
                p0 = (hd % 2) * HD
                if i >= 2:
                    pe.wait_ge(S("m0_P"), i - 1)
                lo, hi = (CTX, TOK) if kd else (0, CTX)
                pe.matmul(PS[:, 2 + i % 2, 0:hi - lo], kT[p0:p0 + HD, hd // 2, j * P:(j + 1) * P],
                          qT[p0:p0 + HD, hd // 2, lo:hi], start=True, stop=True).then_inc(S("m0_S"), 1)

            def values(i):
                hd, kd, j = items[i]
                nt, last = (LT, NT - 1) if kd else (CT, CT - 1)
                pe.wait_ge(S("m0_P"), i + 1)
                if j == 0 and hd >= 1:
                    pe.wait_ge(S("m0_ret_y"), 2 * (hd - 1) + kd + 1)
                for it in range(nt):
                    ins = pe.matmul(PS[:, 4 + kd, it * P:(it + 1) * P], PT[:, i % 4, it * P:(it + 1) * P],
                                    v[:, j, hd * RET_V:(hd + 1) * RET_V], start=j == 0 and it == 0, stop=j == last,
                                    skip_group_check=True)
                ins.then_inc(S("m0_pv"), 1)

            for i in range(len(items)):
                scores(i)
                if i >= 1:
                    values(i - 1)
            values(len(items) - 1)
            pe.wait_ge(S("m0_ret_y"), 2 * RET_HEADS)
            for t in range(NT):
                if t >= 2:
                    pe.wait_ge(S("m0_yT"), t - 1)
                for m in range(4):
                    ins = pe.transpose(PS[:, t % 2, m * P:(m + 1) * P], yr[:, t, m * P:(m + 1) * P], ident[:])
                ins.then_inc(S("m0_yT_ps"), 1)
            pe.wait_ge(S("m0_yT"), NT)
            pe.wait_ge(S("m0_conv_out"), 4)
            for n in range(2 * NT):
                c, t = divmod(n, NT)
                q = n_in + c
                if t == 0:
                    pe.wait_ge(S(f"m0_w{q % ring}"), 16 * (q // ring + 1))
                if n >= 2:
                    pe.wait_ge(S("m0_out_read"), n - 1)
                for k in range(KC):
                    y = yrT[:, k, t * P:(t + 1) * P] if k < 4 else yc[:, k - 4, t * P:(t + 1) * P]
                    ins = pe.matmul(PS[:, 6 + n % 2], y, w[:, q % ring, k], start=k == 0, stop=k == KC - 1)
                ins.then_inc(S("m0_out"), 1)

        @block.vector
        def _(dve):
            norm_modulate(dve, S, T, h, a, ss, rows)
            dve.wait_ge(S("m0_tabs"), 48)
            dve.wait_ge(S("m0_aT_ps"), NT)
            for t in range(NT):
                dve.wait_ge(S("m0_proj"), t + 1)
                if t < CT:
                    dve.tensor_copy(sg[:, t], PS[:, 4 + t % 4]).then_inc(S("m0_qk"), 1)
                else:
                    rope(dve, S, T, t - CT, [sg[:, t].rearrange("p (h n) -> p h n", h=8)], PS[:, 4 + t % 4], a[:, 0, 0:HALF],
                         a[:, 0, HALF:D], cos[:, t - CT], sin[:, t - CT], 8)
                    dve.wait_ge(S("m0_rope_out"), t - CT + 1)
                    dve.sem_inc(S("m0_qk"), 1)
            for i in range(n_ch):
                n = n_tok + 2 * n_ch + i
                m, th = divmod(i, 2)
                dve.wait_ge(S("m0_proj"), n + 1)
                dve.wait_ge(S("m0_ev"), 2 * NT + n_ch + i + 1)
                seg = u[:, m, th * 3 * P:(th + 1) * 3 * P]
                dve.tensor_tensor(seg, seg, PS[:, 4 + n % 4, 0:3 * P], ALU.mult).then_inc(S("m0_u"), 1)
            dve.wait_ge(S("m0_u"), n_ch)
            links = 0

            def link(ins):
                nonlocal links
                links += 1
                ins.then_inc(S("m0_link"), 1)
                dve.wait_ge(S("m0_link"), links)

            def conv(m):
                link(dve.tensor_scalar(yc[:, m], u[:, m], cw[:, m, 1:2], None, ALU.mult))
                for lo, hi in ((0, CTX), (CTX, TOK)):
                    link(dve.scalar_tensor_tensor(yc[:, m, lo + 1:hi], u[:, m, lo:hi - 1], cw[:, m, 0:1], yc[:, m, lo + 1:hi],
                                                  ALU.mult, ALU.add))
                    link(dve.scalar_tensor_tensor(yc[:, m, lo:hi - 1], u[:, m, lo + 1:hi], cw[:, m, 2:3], yc[:, m, lo:hi - 1],
                                                  ALU.mult, ALU.add))
                dve.tensor_tensor(yc[:, m], yc[:, m], gb[:, m], ALU.mult).then_inc(S("m0_conv_out"), 1)

            def head_norm(hd, kd):
                g = 2 * hd + kd
                nt, t0 = (LT, CT) if kd else (CT, 0)
                dve.wait_ge(S("m0_ret_sq"), g + 1)
                dve.tensor_reduce(hs[:, 0, g, 0:nt], sq[:, 0:nt * P].rearrange("p (t n) -> p t n", t=nt), AX.X, ALU.add
                                  ).then_inc(S("m0_ret_ss"), 1)
                dve.wait_ge(S("m0_ret_ss"), g + 1)
                dve.tensor_scalar(hs[:, 1, g, 0:nt], hs[:, 0, g, 0:nt], 1.0 / RET_V, EPS, ALU.mult, ALU.add
                                  ).then_inc(S("m0_ret_ms"), 1)
                dve.wait_ge(S("m0_ret_root"), g + 1)
                link(dve.reciprocal(hs[:, 3, g, 0:nt], hs[:, 2, g, 0:nt]))
                for it in range(nt):
                    cols = slice(hd * RET_V, (hd + 1) * RET_V)
                    ins = dve.scalar_tensor_tensor(yr[:, t0 + it, cols], PS[:, 4 + kd, it * P:(it + 1) * P], hs[:, 3, g, it:it + 1],
                                                   sg[:, t0 + it, cols], ALU.mult, ALU.mult)
                    if it < nt - 1:
                        ins.then_inc(S("m0_ret_part"), 1)
                ins.then_inc(S("m0_ret_y"), 1)

            for i, (hd, kd, j) in enumerate(items):
                dve.wait_ge(S("m0_S"), i + 1)
                if i >= 4:
                    dve.wait_ge(S("m0_pv"), i - 3)
                if kd == 0:
                    x, nq = 3 * P - j * P, CTX
                elif j < CT:
                    x, nq = SL + P - j * P, SEQ
                else:
                    x, nq = 3 * P - (j - CT) * P, SEQ
                dve.tensor_tensor(PT[:, i % 4, 0:nq], PS[:, 2 + i % 2, 0:nq], strips[:, hd, x:x + nq], ALU.mult
                                  ).then_inc(S("m0_P"), 1)
                if kd == 0 and j == CT - 1 and hd:
                    conv(hd - 1)
                    head_norm(hd - 1, 1)
                if kd == 1 and j == 2:
                    head_norm(hd, 0)
            conv(RET_HEADS - 1)
            head_norm(RET_HEADS - 1, 1)
            dve.wait_ge(S("m0_P"), len(items))
            dve.wait_ge(S("m0_pv"), len(items))
            residual(dve, S, T, h, PS, rows, PT, list(range(NT)))


def mixer1_stage(nc, S, A, h, ident, mod_d):
    ring = 3
    BAND = P + 2 * 128
    chunks = [("od_w_in", 0), ("od_w_in", 1), ("od_w_in", 2), ("od_w_out", 0), ("od_w_out", 1)]
    with ExitStack() as ctx:
        def sb(name, shape, dt=F32):
            return ctx.enter_context(nc.sbuf_tensor("m1_" + name, shape, dt))
        rows = sb("rows", [P, 2, 3, D])
        aT = sb("aT", [P, KC, TOK])
        w = sb("w", [P, ring, KC, HALF])
        qT = sb("qT", [P, ATT_HEADS // 2, SEQ])
        kT = sb("kT", [P, KV_HEADS, TOK])
        v = sb("v", [P, NT, KV_HEADS * HD])
        qtok = sb("qtok", [P, 2, HALF])
        ktok = sb("ktok", [P, 2, KV_HEADS, 2, HD])
        cos = sb("cos", [P, LT, HD])
        sin = sb("sin", [P, LT, HD])
        ss = sb("ss", [P, 4, NT])
        a = sb("a", [P, 2, D])
        sq = sb("sq", [P, D])
        mask = sb("mask", [P, BAND])
        sink = sb("sink", [P, ATT_HEADS])
        lgt = sb("logits", [P, 2, CTX + BAND + 1])
        pr = sb("probs", [P, 2, CTX + BAND + 1])
        pT = sb("probsT", [P, 2, CTX + BAND])
        st = sb("stats", [P, 4, LT * ATT_HEADS])
        otok = sb("otok", [P, 2, D])
        PS = ctx.enter_context(nc.psum_tensor("m1_ps", [P, 8, HALF], F32))
        block = ctx.enter_context(nc.Block())
        T = "m1"
        oT = aT[:].rearrange("p k n -> p (k n)")[:, 0:KC * SEQ].rearrange("p (k n) -> p k n", k=KC)
        n_q = 2 * LT
        items = [(b, hd) for b in range(LT) for hd in range(ATT_HEADS)]

        def window(b):
            return max(b - 1, 0), min(b + 2, LT)

        def keys(b):
            lo, hi = window(b)
            return CTX + lo * P, (hi - lo) * P

        def key_tiles(b):
            lo, hi = window(b)
            return list(range(CT)) + [CT + j for j in range(lo, hi)]

        def OT(b):
            return otok[:, b] if b < 2 else a[:, b - 2]

        @block.sync
        def _(sp):
            load_rows(sp, S, mod_d, rows, 1, 0, "m1_rows")
            sp.dma_start(cos[:], A["rope_cos"].rearrange("(t p) n -> p t n", p=P)).then_inc(S("m1_tabs"), 16)
            sp.dma_start(sin[:], A["rope_sin"].rearrange("(t p) n -> p t n", p=P)).then_inc(S("m1_tabs"), 16)
            sp.dma_start(sink[:], A["attn_sinks"].broadcast_to([P, ATT_HEADS])).then_inc(S("m1_tabs"), 16)
            for n, (name, c) in enumerate(chunks):
                if n >= ring:
                    sp.wait_ge(S("m1_proj"), LT * (n - ring + 1))
                sp.dma_start(w[:, n % ring], A[name][0].rearrange("(k p) n -> p k n", p=P)[:, :, c * HALF:(c + 1) * HALF]
                             ).then_inc(S(f"m1_w{n % ring}"), 16)

        @block.gpsimd
        def _(pool):
            pool.memset(mask[:], 0.0).then_inc(S("m1_mask"), 1)
            pool.wait_ge(S("m1_mask"), 1)
            pool.affine_select(out=mask[:], in_=mask[:], compare_op=ALU.is_ge, fill=NEG, base=0, pattern=[[1, BAND]],
                               channel_multiplier=-1).then_inc(S("m1_mask"), 1)
            pool.wait_ge(S("m1_mask"), 2)
            pool.affine_select(out=mask[:], in_=mask[:], compare_op=ALU.is_ge, fill=NEG, base=2 * 128, pattern=[[-1, BAND]],
                               channel_multiplier=1).then_inc(S("m1_mask"), 1)

        @block.scalar
        def _(act):
            norm_squares(act, S, T, h, sq[:], ss)
            norm_evacuate(act, S, T, PS, aT)
            for n in range(n_q):
                act.wait_ge(S("m1_qT_ps"), n + 1)
                c, t = divmod(n, LT)
                act.activation(qT[:, 4 * c:4 * c + 4, t * P:(t + 1) * P], PS[:, n % 2].rearrange("p (m n) -> p m n", m=4), ACT.Copy
                               ).then_inc(S("m1_qT"), 1)
            for t in range(NT):
                act.wait_ge(S("m1_kT_ps"), t + 1)
                act.activation(kT[:, :, t * P:(t + 1) * P], PS[:, t % 2].rearrange("p (m n) -> p m n", m=4), ACT.Copy
                               ).then_inc(S("m1_kT"), 1)

            def probs(i):
                b, hd = items[i]
                w_all = CTX + keys(b)[1] + 1
                act.wait_ge(S("m1_negm"), i + 1)
                if i >= 2:
                    act.wait_ge(S("m1_pT_ps"), i - 1)
                act.activation(pr[:, i % 2, 0:w_all], lgt[:, i % 2, 0:w_all], ACT.Exp, bias=st[:, 1, i:i + 1],
                               accum_out=st[:, 2, i:i + 1]).then_inc(S("m1_probs"), 1)

            def transposed(i):
                b, hd = items[i]
                n = CTX + keys(b)[1]
                act.wait_ge(S("m1_pT_ps"), i + 1)
                if i >= 2:
                    act.wait_ge(S("m1_o"), i - 1)
                act.activation(pT[:, i % 2, 0:n], PS[:, 4:6].rearrange("p b n -> p (b n)")[:, 0:n], ACT.Copy).then_inc(S("m1_pT"), 1)

            for i in range(len(items)):
                probs(i)
                if i >= 1:
                    transposed(i - 1)
            transposed(len(items) - 1)
            for b in range(LT):
                act.wait_ge(S("m1_oT_ps"), b + 1)
                act.activation(oT[:, :, b * P:(b + 1) * P], PS[:, 0:2].rearrange("p b (k n) -> p (b k) n", k=4), ACT.Copy
                               ).then_inc(S("m1_oT"), 1)

        @block.tensor
        def _(pe):
            norm_transpose(pe, S, T, PS, a, ident)
            pe.wait_ge(S("m1_aT"), NT)

            def q_transpose(n):
                pe.wait_ge(S("m1_rope_out"), n + 1)
                if n >= 2:
                    pe.wait_ge(S("m1_qT"), n - 1)
                for m in range(4):
                    ins = pe.transpose(PS[:, n % 2, m * P:(m + 1) * P], qtok[:, n % 2, m * P:(m + 1) * P], ident[:])
                ins.then_inc(S("m1_qT_ps"), 1)

            def k_transpose(t):
                pe.wait_ge(S("m1_k"), t + 1)
                if t >= 2:
                    pe.wait_ge(S("m1_kT"), t - 1)
                else:
                    pe.wait_ge(S("m1_qT"), n_q - 1 + t)
                for m in range(4):
                    ins = pe.transpose(PS[:, t % 2, m * P:(m + 1) * P], ktok[:, t % 2, m].rearrange("p a n -> p (a n)"), ident[:])
                ins.then_inc(S("m1_kT_ps"), 1)

            for n in range(n_q + NT):
                c, t = (n // LT, CT + n % LT) if n < n_q else (2, n - n_q)
                if n in (0, LT, n_q):
                    pe.wait_ge(S(f"m1_w{c % ring}"), 16 * (c // ring + 1))
                if n >= 4:
                    if n - 4 < n_q:
                        pe.wait_ge(S("m1_rope_out"), n - 3)
                    else:
                        pe.wait_ge(S("m1_v"), n - 4 - n_q + 1)
                for k in range(KC):
                    ins = pe.matmul(PS[:, 4 + n % 4], aT[:, k, t * P:(t + 1) * P], w[:, c % ring, k], start=k == 0, stop=k == KC - 1)
                ins.then_inc(S("m1_proj"), 1)
                if 1 <= n <= n_q:
                    q_transpose(n - 1)
                elif n > n_q:
                    k_transpose(n - n_q - 1)
            k_transpose(NT - 1)
            pe.wait_ge(S("m1_kT"), NT)
            pe.wait_ge(S("m1_v"), NT)

            def scores(i):
                b, hd = items[i]
                kv, p0, s0 = hd // (ATT_HEADS // KV_HEADS), (hd % 2) * HD, 2 * (i % 2)
                at, n = keys(b)
                if i >= 2:
                    pe.wait_ge(S("m1_logits"), i - 1)
                q = qT[p0:p0 + HD, hd // 2, b * P:(b + 1) * P]
                pe.matmul(PS[:, s0, 0:CTX], q, kT[p0:p0 + HD, kv, 0:CTX], start=True, stop=True)
                pe.matmul(PS[:, s0 + 1, 0:n], q, kT[p0:p0 + HD, kv, at:at + n], start=True, stop=True).then_inc(S("m1_S"), 1)

            def transposes(i):
                b, hd = items[i]
                pe.wait_ge(S("m1_probs"), i + 1)
                if i >= 1:
                    pe.wait_ge(S("m1_pT"), i)
                for m in range(len(key_tiles(b))):
                    ins = pe.transpose(PS[:, 4 + m // 4, (m % 4) * P:(m % 4 + 1) * P], pr[:, i % 2, m * P:(m + 1) * P], ident[:])
                ins.then_inc(S("m1_pT_ps"), 1)

            def values(i):
                b, hd = items[i]
                kv, tiles = hd // (ATT_HEADS // KV_HEADS), key_tiles(b)
                pe.wait_ge(S("m1_pT"), i + 1)
                if i >= 2:
                    pe.wait_ge(S("m1_otok"), i - 1)
                for m, t in enumerate(tiles):
                    ins = pe.matmul(PS[:, 6 + i % 2, 0:HD], pT[:, i % 2, m * P:(m + 1) * P], v[:, t, kv * HD:(kv + 1) * HD],
                                    start=m == 0, stop=m == len(tiles) - 1)
                ins.then_inc(S("m1_o"), 1)

            for i in range(len(items) + 2):
                if i < len(items):
                    scores(i)
                if 1 <= i <= len(items):
                    transposes(i - 1)
                if i >= 2:
                    values(i - 2)
            pe.wait_ge(S("m1_logits"), len(items))
            pe.wait_ge(S("m1_otok"), len(items))
            for b in range(LT):
                pe.wait_ge(S("m1_otok_kept"), b + 1)
                if b >= 1:
                    pe.wait_ge(S("m1_oT"), b)
                for k in range(KC):
                    ins = pe.transpose(PS[:, k // 4, (k % 4) * P:(k % 4 + 1) * P], OT(b)[:, k * P:(k + 1) * P], ident[:])
                ins.then_inc(S("m1_oT_ps"), 1)
            pe.wait_ge(S("m1_oT"), LT)
            for n in range(2 * LT):
                c, t = divmod(n, LT)
                q = 3 + c
                if t == 0:
                    pe.wait_ge(S(f"m1_w{q % ring}"), 16 * (q // ring + 1))
                if n >= 2:
                    pe.wait_ge(S("m1_out_read"), n - 1)
                for k in range(KC):
                    ins = pe.matmul(PS[:, 6 + n % 2], oT[:, k, t * P:(t + 1) * P], w[:, q % ring, k], start=k == 0, stop=k == KC - 1)
                ins.then_inc(S("m1_out"), 1)

        @block.vector
        def _(dve):
            norm_modulate(dve, S, T, h, a, ss, rows)
            dve.wait_ge(S("m1_tabs"), 48)
            dve.wait_ge(S("m1_aT_ps"), NT)
            t1, t2 = a[:, 0, 0:HALF], a[:, 0, HALF:D]
            for n in range(n_q):
                dve.wait_ge(S("m1_proj"), n + 1)
                if n >= 2:
                    dve.wait_ge(S("m1_qT_ps"), n - 1)
                rope(dve, S, T, n, [qtok[:, n % 2].rearrange("p (h n) -> p h n", h=8)], PS[:, 4 + n % 4], t1, t2,
                     cos[:, n % LT], sin[:, n % LT], 8)
            for t in range(NT):
                n = n_q + t
                ps = PS[:, 4 + n % 4]
                dve.wait_ge(S("m1_proj"), n + 1)
                if t >= 2:
                    dve.wait_ge(S("m1_kT_ps"), t - 1)
                outs = [ktok[:, t % 2, :, x] for x in range(2)]
                if t < CT:
                    for x, o in enumerate(outs):
                        ins = dve.tensor_copy(o, ps[:, 0:KV_HEADS * HD].rearrange("p (h n) -> p h n", h=KV_HEADS))
                        ins.then_inc(S("m1_k" if x else "m1_k_dup"), 1)
                else:
                    rope(dve, S, T, n_q + t - CT, outs, ps[:, 0:KV_HEADS * HD], t1, t2, cos[:, t - CT], sin[:, t - CT], KV_HEADS)
                    dve.wait_ge(S("m1_rope_out"), n_q + t - CT + 1)
                    dve.sem_inc(S("m1_k"), 1)
                dve.tensor_copy(v[:, t], ps[:, KV_HEADS * HD:HALF]).then_inc(S("m1_v"), 1)
            dve.wait_ge(S("m1_mask"), 3)

            def logits(i):
                b, hd = items[i]
                n = keys(b)[1]
                m0 = P if b == 0 else 0
                dve.wait_ge(S("m1_S"), i + 1)
                if i >= 2:
                    dve.wait_ge(S("m1_probs"), i - 1)
                L = lgt[:, i % 2]
                dve.tensor_scalar(L[:, 0:CTX], PS[:, 2 * (i % 2), 0:CTX], SCALE, None, ALU.mult).then_inc(S("m1_logits_part"), 1)
                dve.tensor_copy(L[:, CTX + n:CTX + n + 1], sink[:, hd:hd + 1]).then_inc(S("m1_logits_part"), 1)
                dve.scalar_tensor_tensor(L[:, CTX:CTX + n], PS[:, 2 * (i % 2) + 1, 0:n], SCALE, mask[:, m0:m0 + n], ALU.mult, ALU.add
                                         ).then_inc(S("m1_logits"), 1)
                dve.wait_ge(S("m1_logits"), i + 1)
                dve.tensor_reduce(st[:, 0, i:i + 1], L[:, 0:CTX + n + 1], AX.X, ALU.max).then_inc(S("m1_max"), 1)
                dve.wait_ge(S("m1_max"), i + 1)
                dve.tensor_scalar(st[:, 1, i:i + 1], st[:, 0, i:i + 1], -1.0, None, ALU.mult).then_inc(S("m1_negm"), 1)

            def output(i):
                b, hd = items[i]
                dve.wait_ge(S("m1_probs"), i + 1)
                dve.reciprocal(st[:, 3, i:i + 1], st[:, 2, i:i + 1]).then_inc(S("m1_recip"), 1)
                dve.wait_ge(S("m1_recip"), i + 1)
                dve.wait_ge(S("m1_o"), i + 1)
                dve.tensor_scalar(OT(b)[:, hd * HD:(hd + 1) * HD], PS[:, 6 + i % 2, 0:HD], st[:, 3, i:i + 1], None, ALU.mult
                                  ).then_inc(S("m1_otok"), 1)
                if hd == ATT_HEADS - 1:
                    dve.wait_ge(S("m1_otok"), i + 1)
                    dve.sem_inc(S("m1_otok_kept"), 1)

            for i in range(len(items) + 3):
                if i < len(items):
                    logits(i)
                if i >= 3:
                    output(i - 3)
            residual(dve, S, T, h, PS, rows, qtok, [CT + t for t in range(LT)])


R_LINKS = 19
R_PIECES = 4

PAIRS_T = NH * PAIRS
ACT_SQUARE, DVE_MEAN, ACT_ROOT, DVE_MOD = 1, 3, 4, 6
PE_F_T, ACT_F_T, PE_Q, ACT_Q, PE_Q_T, ACT_Q_T, PE_S, ACT_S = 8, 10, 12, 22, 24, 26, 28, 32
ROUTE_NOW = {3: 6, 8: 7}
ROUTE_FIRST = {4 * n: LAG + n for n in range(NH - LAG)}
ROUTE_NEXT = {33 + 4 * n: n for n in range(NH - LAG)}


def peer_stage(nc, S, A, h, ident, mod_d, layer, t0, first, n_tiles):
    T = f"peer{layer}_"
    TS = NH * TOPK
    with ExitStack() as ctx:
        def sb(name, shape, dt=F32):
            return ctx.enter_context(nc.sbuf_tensor(T + name, shape, dt))

        def sem(name):
            return S("peer_" + name)

        rows = sb("rows", [P, 2, 3, D])
        ring = sb("ring", [P, RING, 2 * D])
        wq = sb("wq", [P, KC, D])
        keys = sb("keys", [P, NH, NK])
        f = sb("f", [P, D])
        fn = sb("fn", [P, D])
        fT = sb("fT", [P, KC, P])
        q = sb("q", [P, D])
        qT = sb("qT", [P, NH, P])
        sc = sb("scores", [P, 2, 2, NH // 2, NK])
        y = sb("y", [P, D])
        diag = sb("diag", [P, RING, P])
        ss = sb("ss", [P, 4])
        iota = sb("iota", [P, TOPK])
        top = sb("top", [P, 2, TOPK])
        topi = sb("topi", [P, 2, TOPK], U32)
        topf = sb("topf", [P, 2, TOPK])
        cand = sb("cand", [P, TOPK, TOPK])
        cs = sb("cs", [P, NH, TOPK])
        ci = sb("ci", [P, TOPK], U32)
        ab = sb("ab", [P, 2, TOPK], U32)
        abf = sb("abf", [P, 2, TOPK])
        hot = sb("hot", [P, 2, TOPK, TOPK])
        e12 = sb("e12", [P, 2, TOPK])
        ef = sb("ef", [P, TOPK])
        idx = sb("idx", [P, NH, TOPK], U32)
        negm = sb("negm", [P, NH])
        gexp = sb("gexp", [P, NH, TOPK])
        gsum = sb("gsum", [P, NH])
        grec = sb("grec", [P, NH])
        u = sb("u", [P, 4, PAIR])
        gel = sb("gel", [P, 4, PAIR])
        coef = sb("coef", [P, 4, PAIR])
        PY = ctx.enter_context(nc.psum_tensor(T + "py", [P, 2, 2, HALF], F32))
        PB = ctx.enter_context(nc.psum_tensor(T + "pb", [P, 4, HALF], F32))
        block = ctx.enter_context(nc.Block())

        shift = first - t0

        def wait_apart(eng, which, value):
            eng.wait_ge(which, value)
            eng.sem_inc(sem("passed_" + ("pool" if eng is nc.gpsimd else "dve")), 1)

        def row_kind(t):
            return (t - shift + CT) // LT if t0 < CT else 1

        def tiles(eng, body):
            body(first, ROUTE_FIRST, ROUTE_NEXT)
            with eng.Fori(first + 1, first + n_tiles - 1) as i:
                body(i, ROUTE_NOW, ROUTE_NEXT)
            body(first + n_tiles - 1, ROUTE_NOW, {})

        def heads_at(g, table):
            return [table[g]] if g in table else []

        @block.sync
        def _(sp):
            load_rows(sp, S, mod_d, rows, layer, 1, "peer_rows")
            sp.dma_start(wq[:], A["peer_wq"][layer].rearrange("(k p) n -> p k n", p=P)).then_inc(sem("wq"), 16)
            sp.dma_start(keys[:], A["keysT"][layer]).then_inc(sem("keys"), 16)

        @block.gpsimd
        def _(pool):
            pool.iota(iota[:], [[1, TOPK]], base=0, channel_multiplier=0, allow_small_or_imprecise_dtypes=True
                      ).then_inc(sem("iota"), 1)

            def body(i, now, nxt):
                for hd in range(NH):
                    pool.wait_ge(sem("idx"), i * NH + hd + 1)
                    for j in range(TOPK):
                        s = hd * TOPK + j
                        wait_apart(pool, sem("slot_free"), i * TS + s + 1)
                        pool.indirect_dma_start(ring[:, s % RING], None, A["uv"], bass.IndirectOffsetOnAxis(idx[:, hd, j:j + 1], 0)
                                                ).then_inc(sem(f"landed{s % RING}"), 16)
            tiles(pool, body)

        @block.scalar
        def _(act):
            def prep(i, step):
                if step == "square":
                    act.activation(q[:], h[:, i - shift], ACT.Square, accum_out=ss[:, 0:1]).then_inc(sem("square"), 1)
                elif step == "root":
                    act.wait_ge(sem("mean"), i + 1)
                    act.activation(ss[:, 2:3], ss[:, 1:2], ACT.Sqrt).then_inc(sem("root"), 1)
                elif step == "fT":
                    act.wait_ge(sem("fT_ps"), i + 1)
                    act.activation(fT[:], PB[:, 0:2].rearrange("p b (k n) -> p (b k) n", k=4), ACT.Copy).then_inc(sem("fT"), 1)
                elif step == "q":
                    act.wait_ge(sem("q_ps"), i + 1)
                    act.activation(q[:], PB[:, 2:4].rearrange("p b n -> p (b n)"), ACT.Copy).then_inc(sem("q"), 1)
                elif step == "qT":
                    act.wait_ge(sem("qT_ps"), i + 1)
                    act.activation(qT[:], PB[:, 0:2].rearrange("p b (k n) -> p (b k) n", k=4), ACT.Copy).then_inc(sem("qT"), 1)
                elif step == "s":
                    act.wait_ge(sem("s_ps"), i + 1)
                    if i is not first or first:
                        act.wait_ge(sem("idx"), i * NH)
                    act.activation(sc[:].rearrange("p g a h n -> p (g a h n)"), PB[:].rearrange("p b n -> p (b n)"), ACT.Copy
                                   ).then_inc(sem("s"), 1)

            def gate(i, hd):
                act.wait_ge(sem("negm"), i * NH + hd + 1)
                act.activation(gexp[:, hd], cs[:, hd], ACT.Exp, bias=negm[:, hd:hd + 1], accum_out=gsum[:, hd:hd + 1]
                               ).then_inc(sem("gexp"), 1)

            for step in ("square", "root", "fT", "q", "qT", "s"):
                prep(first, step)
            for hd in range(LAG):
                gate(first, hd)

            def body(i, now, nxt):
                for g in range(PAIRS_T):
                    act.wait_ge(sem("dot"), i * TS + PAIR * (g + 1))
                    act.activation(gel[:, g % 4], u[:, g % 4], ACT.Gelu).then_inc(sem("gelu"), 1)
                    act.wait_ge(sem("coef"), i * PAIRS_T + g + 1)
                    for j in range(PAIR):
                        act.activation(diag[:, (PAIR * g + j) % RING], ident[:], ACT.Copy, scale=coef[:, g % 4, j:j + 1]
                                       ).then_inc(sem("diag"), 1)
                    for hd in heads_at(g - R_PIECES, now):
                        gate(i, hd)
                    for hd in heads_at(g - R_PIECES, nxt):
                        gate(i + 1, hd)
                    if not nxt:
                        continue
                    for at, step in ((ACT_SQUARE, "square"), (ACT_ROOT, "root"), (ACT_F_T, "fT"), (ACT_Q, "q"),
                                     (ACT_Q_T, "qT"), (ACT_S, "s")):
                        if g == at:
                            prep(i + 1, step)
            tiles(act, body)

        @block.tensor
        def _(pe):
            def f_transposes(i):
                pe.wait_ge(sem("fn"), i + 1)
                for k in range(KC):
                    ins = pe.transpose(PB[:, k // 4, (k % 4) * P:(k % 4 + 1) * P], fn[:, k * P:(k + 1) * P], ident[:])
                ins.then_inc(sem("fT_ps"), 1)

            def queries(i, k):
                if k == 0:
                    pe.wait_ge(sem("fT"), i + 1)
                for b in range(2):
                    ins = pe.matmul(PB[:, 2 + b], fT[:, k], wq[:, k, b * HALF:(b + 1) * HALF], start=k == 0, stop=k == KC - 1)
                if k == KC - 1:
                    ins.then_inc(sem("q_ps"), 1)

            def q_transposes(i):
                pe.wait_ge(sem("q"), i + 1)
                for k in range(KC):
                    ins = pe.transpose(PB[:, k // 4, (k % 4) * P:(k % 4 + 1) * P], q[:, k * P:(k + 1) * P], ident[:])
                ins.then_inc(sem("qT_ps"), 1)

            def scores(i, part):
                if part == 0:
                    pe.wait_ge(sem("qT"), i + 1)
                for hd in range(4 * part, 4 * part + 4):
                    for half in range(2):
                        rng = slice(half * 64, half * 64 + 64)
                        ins = pe.matmul(PB[:, 2 * part + half, (hd % 4) * NK:(hd % 4 + 1) * NK], qT[rng, hd], keys[rng, hd],
                                        start=True, stop=True, skip_group_check=True)
                if part == 1:
                    ins.then_inc(sem("s_ps"), 1)

            if layer == 0:
                pe.sem_inc(sem("slot_free"), RING)
            pe.wait_ge(S("ident_ready"), 1)
            f_transposes(first)
            pe.wait_ge(sem("wq"), 16 * (layer + 1))
            for k in range(KC):
                queries(first, k)
            q_transposes(first)
            pe.wait_ge(sem("keys"), 16 * (layer + 1))
            scores(first, 0)
            scores(first, 1)

            def body(i, now, nxt):
                for g in range(PAIRS_T):
                    hd = g // PAIRS
                    if g % PAIRS == 0:
                        pe.wait_ge(sem("y_free"), i * NH + hd + 1)
                    for j in range(PAIR):
                        s = PAIR * g + j
                        pe.wait_ge(sem("diag"), i * TS + s + 1)
                        for b in range(2):
                            ins = pe.matmul(PY[:, hd % 2, b], diag[:, s % RING], ring[:, s % RING, D + b * HALF:D + (b + 1) * HALF],
                                            start=s % TOPK == 0, stop=s % TOPK == TOPK - 1)
                        ins.then_inc(sem("slot_free"), 1)
                    if not nxt:
                        continue
                    if g == PE_F_T:
                        f_transposes(i + 1)
                    if PE_Q <= g < PE_Q + KC:
                        queries(i + 1, g - PE_Q)
                    if g == PE_Q_T:
                        q_transposes(i + 1)
                    if PE_S <= g < PE_S + 2:
                        scores(i + 1, g - PE_S)
            tiles(pe, body)

        @block.vector
        def _(dve):
            def mean(i):
                dve.wait_ge(sem("square"), i + 1)
                dve.tensor_scalar(ss[:, 1:2], ss[:, 0:1], 1.0 / D, EPS, ALU.mult, ALU.add).then_inc(sem("mean"), 1)

            def modulate(i):
                dve.wait_ge(sem("root"), i + 1)
                dve.reciprocal(ss[:, 3:4], ss[:, 2:3]).then_inc(sem("rstd"), 1)
                dve.wait_ge(sem("rstd"), i + 1)
                dve.scalar_tensor_tensor(fn[:], h[:, i - shift], ss[:, 3:4], rows[:, row_kind(i), 1], ALU.mult, ALU.mult
                                         ).then_inc(sem("fn_scaled"), 1)
                dve.wait_ge(sem("fn_scaled"), i + 1)
                dve.tensor_tensor(fn[:], fn[:], rows[:, row_kind(i), 0], ALU.add).then_inc(sem("fn"), 1)

            def route(i, hd, piece):
                links = (0, 4, 8, 13)[piece]

                def link(ins):
                    nonlocal links
                    links += 1
                    ins.then_inc(sem("link"), 1)
                    wait_apart(dve, sem("link"), (i * NH + hd) * R_LINKS + links)

                def top16(out, where, values):
                    link(dve.max(out[:, 0:8], values))
                    dve.max_index(where[:, 0:8], out[:, 0:8], values).then_inc(sem("places"), 1)
                    link(dve.match_replace(values, out[:, 0:8], values, TAKEN))
                    link(dve.max(out[:, 8:16], values))
                    link(dve.max_index(where[:, 8:16], out[:, 8:16], values))

                if piece == 0:
                    wait_apart(dve, sem("s"), i + 1)
                if piece < 2:
                    top16(top[:, piece], topi[:, piece], sc[:, hd // 4, piece, hd % 4])
                    return
                if piece == 2:
                    dve.tensor_copy(topf[:], topi[:]).then_inc(sem("places"), 1)
                    link(dve.tensor_tensor(cand[:], top[:, 0].rearrange("p (a b) -> p a b", b=1).broadcast_to([P, TOPK, TOPK]),
                                           top[:, 1].rearrange("p (a b) -> p a b", a=1).broadcast_to([P, TOPK, TOPK]), ALU.add))
                    top16(cs[:, hd], ci, cand[:].rearrange("p a b -> p (a b)"))
                    dve.tensor_scalar(negm[:, hd:hd + 1], cs[:, hd, 0:1], -1.0, None, ALU.mult).then_inc(sem("negm"), 1)
                    return
                dve.tensor_scalar(ab[:, 0], ci[:], 4, None, ALU.logical_shift_right).then_inc(sem("places"), 1)
                link(dve.tensor_scalar(ab[:, 1], ci[:], 15, None, ALU.bitwise_and))
                link(dve.tensor_copy(abf[:], ab[:]))
                link(dve.tensor_tensor(hot[:], abf[:].rearrange("p c (k o) -> p c k o", o=1).broadcast_to([P, 2, TOPK, TOPK]),
                                       iota[:].rearrange("p (a b m) -> p a b m", a=1, b=1).broadcast_to([P, 2, TOPK, TOPK]), ALU.is_equal))
                link(dve.tensor_tensor(hot[:], hot[:], topf[:].rearrange("p c (o m) -> p c o m", o=1).broadcast_to([P, 2, TOPK, TOPK]),
                                       ALU.mult))
                link(dve.tensor_reduce(e12[:], hot[:], AX.X, ALU.add))
                link(dve.scalar_tensor_tensor(ef[:], e12[:, 0], float(NK), e12[:, 1], ALU.mult, ALU.add))
                dve.tensor_scalar(idx[:, hd], ef[:], float(layer * EXPERTS), None, ALU.add).then_inc(sem("idx"), 1)
                dve.wait_ge(sem("idx"), i * NH + hd + 1)
                assert links == R_LINKS, links

            def denominator(i, hd):
                dve.wait_ge(sem("gexp"), i * NH + hd + 1)
                dve.reciprocal(grec[:, hd:hd + 1], gsum[:, hd:hd + 1]).then_inc(sem("grec"), 1)

            def coefficients(i, g):
                hd, at = g // PAIRS, PAIR * (g % PAIRS)
                dve.wait_ge(sem("gelu"), i * PAIRS_T + g + 1)
                if g % PAIRS == 0:
                    dve.wait_ge(sem("grec"), i * NH + hd + 1)
                dve.scalar_tensor_tensor(coef[:, g % 4], gel[:, g % 4], grec[:, hd:hd + 1], gexp[:, hd, at:at + PAIR],
                                         ALU.mult, ALU.mult).then_inc(sem("coef"), 1)

            def head_sum(i, hd):
                dve.wait_ge(sem("slot_free"), i * TS + RING + (hd + 1) * TOPK)
                ps = PY[:, hd % 2].rearrange("p b n -> p (b n)")
                if hd == 0:
                    dve.tensor_copy(y[:], ps).then_inc(sem("y_free"), 1)
                else:
                    dve.tensor_tensor(y[:], y[:], ps, ALU.add).then_inc(sem("y_free"), 1)

            if layer == 0:
                dve.sem_inc(sem("y_free"), 2)
            dve.wait_ge(sem("rows"), 32 * (layer + 1))
            mean(first)
            modulate(first)
            dve.wait_ge(sem("iota"), layer + 1)
            for hd in range(LAG):
                for piece in range(R_PIECES):
                    route(first, hd, piece)
            for hd in range(LAG):
                denominator(first, hd)

            def body(i, now, nxt):
                dve.wait_ge(sem("fn"), i + 1)
                dve.tensor_copy(f[:], fn[:]).then_inc(sem("f"), 1)
                dve.wait_ge(sem("f"), i + 1)
                for g in range(PAIRS_T):
                    for j in range(PAIR):
                        s = PAIR * g + j
                        dve.wait_ge(sem(f"landed{s % RING}"), 16 * (i * (TS // RING) + s // RING + 1))
                        x = ring[:, s % RING, 0:D]
                        dve.tensor_tensor_reduce(x, x, f[:], 1.0, 0.0, ALU.mult, ALU.add, u[:, g % 4, j:j + 1]).then_inc(sem("dot"), 1)
                        if j == 0 and g:
                            coefficients(i, g - 1)
                    if g % PAIRS == 3 and g >= PAIRS:
                        dve.wait_ge(sem("y_free"), i * NH + g // PAIRS + 1)
                        head_sum(i, g // PAIRS - 1)
                    for ahead, table in ((0, now), (1, nxt)):
                        for piece in range(R_PIECES):
                            for hd in heads_at(g - piece, table):
                                route(i + ahead, hd, piece)
                        for hd in heads_at(g - R_PIECES - 2, table):
                            denominator(i + ahead, hd)
                    if not nxt:
                        continue
                    if g == DVE_MEAN:
                        mean(i + 1)
                    if g == DVE_MOD:
                        modulate(i + 1)
                coefficients(i, PAIRS_T - 1)
                dve.wait_ge(sem("y_free"), i * NH + NH + 1)
                head_sum(i, NH - 1)
                dve.wait_ge(sem("y_free"), i * NH + NH + 2)
                dve.tensor_tensor(y[:], y[:], rows[:, row_kind(i), 2], ALU.mult).then_inc(sem("gated"), 1)
                dve.wait_ge(sem("gated"), i + 1)
                dve.tensor_tensor(h[:, i - shift], h[:, i - shift], y[:], ALU.add).then_inc(sem("h"), 1)
                dve.wait_ge(sem("h"), i + 1)
            tiles(dve, body)


def final_stage(nc, S, A, h, out):
    with ExitStack() as ctx:
        gain = ctx.enter_context(nc.sbuf_tensor("fin_gain", [P, D], F32))
        o = ctx.enter_context(nc.sbuf_tensor("fin_o", [P, LT, D], F32))
        ss = ctx.enter_context(nc.sbuf_tensor("fin_ss", [P, 4, LT], F32))
        block = ctx.enter_context(nc.Block())

        @block.sync
        def _(sp):
            sp.dma_start(gain[:], A["final_norm_g"].rearrange("(a n) -> a n", a=1).broadcast_to([P, D])).then_inc(S("fin_gain"), 16)
            for t in range(LT):
                sp.wait_ge(S("fin_o"), t + 1)
                sp.dma_start(out[0].rearrange("(t p) d -> p t d", p=P)[:, t], o[:, t]).then_inc(S("stored"), 16)
            sp.wait_ge(S("stored"), 16 * LT)

        @block.scalar
        def _(act):
            for t in range(LT):
                act.activation(o[:, t], h[:, CT + t], ACT.Square, accum_out=ss[:, 0, t:t + 1]).then_inc(S("fin_sq"), 1)
            act.wait_ge(S("fin_ms"), 1)
            act.activation(ss[:, 2], ss[:, 1], ACT.Sqrt).then_inc(S("fin_root"), 1)

        @block.vector
        def _(dve):
            dve.wait_ge(S("fin_sq"), LT)
            dve.tensor_scalar(ss[:, 1], ss[:, 0], 1.0 / D, EPS, ALU.mult, ALU.add).then_inc(S("fin_ms"), 1)
            dve.wait_ge(S("fin_root"), 1)
            dve.reciprocal(ss[:, 3], ss[:, 2]).then_inc(S("fin_rstd"), 1)
            dve.wait_ge(S("fin_rstd"), 1)
            dve.wait_ge(S("fin_gain"), 16)
            for t in range(LT):
                dve.scalar_tensor_tensor(o[:, t], h[:, CT + t], ss[:, 3, t:t + 1], gain[:], ALU.mult, ALU.mult
                                         ).then_inc(S("fin_o"), 1)


def backbone(nc, A, out):
    with ExitStack() as ctx:
        S = Sems(nc, ctx)
        mod_d = nc.dram_tensor("mod_rows", (DEPTH, 2, 2, 3, D), F32).ap()
        h = ctx.enter_context(nc.sbuf_tensor("h", [P, NT, D], F32))
        ident = ctx.enter_context(nc.sbuf_tensor("ident", [P, P], F32))
        with nc.sbuf_tensor("strips", [P, RET_HEADS, SL + SC], F32) as strips:
            modulation_stage(nc, S, A, h, ident, mod_d, strips)
            mixer0_stage(nc, S, A, h, ident, mod_d, strips)
        peer_stage(nc, S, A, h, ident, mod_d, 0, 0, 0, NT)
        mixer1_stage(nc, S, A, h, ident, mod_d)
        peer_stage(nc, S, A, h, ident, mod_d, 1, CT, NT, LT)
        final_stage(nc, S, A, h, out)


def _rope_tables():
    n = HD // 4
    rows, cols = np.divmod(np.arange(SEQ), GRID_W)
    inv = (np.float32(ROPE_BASE) ** (-np.arange(n, dtype=np.float32) / np.float32(n))).astype(np.float32)
    ang = np.stack([rows.astype(np.float32)[:, None] * inv, cols.astype(np.float32)[:, None] * inv], axis=1)
    cos, sin = np.cos(ang), np.sin(ang)
    return (np.stack([cos, cos], axis=2).reshape(SEQ, HD).astype(np.float32),
            np.stack([-sin, sin], axis=2).reshape(SEQ, HD).astype(np.float32))


def _lay_out(inputs):
    a = {k: np.asarray(v) for k, v in inputs.items()}
    a["rope_cos"], a["rope_sin"] = _rope_tables()
    a["gains"] = np.stack([a.pop("mix_norm_g"), a.pop("ffn_norm_g")], axis=1).reshape(DEPTH, 2 * D)
    a["conv_wT"] = a.pop("conv_w")[0].T
    keys = np.concatenate([a.pop("peer_keys1"), a.pop("peer_keys2")], axis=-1)
    a["keysT"] = keys.transpose(0, 3, 1, 2)
    a["uv"] = np.concatenate([a.pop("peer_u"), a.pop("peer_v")], axis=-1).reshape(DEPTH * EXPERTS, 2 * D)
    return {k: np.ascontiguousarray(v) for k, v in a.items()}


def kernel(**inputs):
    import concourse.bacc as _bacc
    from concourse.bass_utils import run_bass_kernel_spmd as _run

    nc = _bacc.Bacc("TRN2", target_bir_lowering=False, num_devices=1)
    arrays, args = {}, {}
    for name, a in _lay_out(inputs).items():
        arrays[f"in_{name}_dram"] = a
        args[name] = nc.dram_tensor(f"in_{name}_dram", a.shape, mybir.dt.from_np(a.dtype), kind="ExternalInput").ap()
    out = nc.dram_tensor("out_0_dram", (1, SEQ, D), F32, kind="ExternalOutput").ap()
    backbone(nc, args, out)
    r = _run(nc, [arrays], core_ids=[0])
    return r.results[0]["out_0_dram"]
```

```python
from contextlib import ExitStack

import numpy as np

import concourse.bass as bass
from concourse import mybir

ALU = mybir.AluOpType
ACT = mybir.ActivationFunctionType
AX = mybir.AxisListType
F32 = mybir.dt.float32
U32 = mybir.dt.uint32

P = 128
D = 1024
KC = D // P
CTX, SEQ = 256, 512
CT, LT = CTX // P, SEQ // P
NT = CT + LT
TOK = CTX + SEQ
DEPTH = 2
EPS = 1e-6
HALF = 512
RET_HEADS, RET_V = 4, 128
HD = 64
ATT_HEADS, KV_HEADS = 16, 4
SCALE = HD ** -0.5
GRID_W, ROPE_BASE = 64, 10000.0
NEG = -1e30
NH, NK, TOPK = 8, 128, 16
EXPERTS = NK * NK
RING = 8
PAIR = 2
PAIRS = TOPK // PAIR
LAG = 2
TAKEN = -3.0e38


def kind(t):
    return int(t >= CT)


class Sems:

    def __init__(self, nc, ctx):
        self.nc, self.ctx, self.made = nc, ctx, {}

    def __call__(self, name):
        if name not in self.made:
            self.made[name] = self.ctx.enter_context(self.nc.semaphore(name))
        return self.made[name]


class Arena:

    def __init__(self, tensor):
        self.flat, self.at = tensor[:], 0

    def cut(self, *shape):
        size = int(np.prod(shape))
        assert self.at + size <= self.flat.shape[1], (self.at, size)
        part = self.flat[:, self.at:self.at + size]
        self.at += size
        if len(shape) == 1:
            return part
        names = "abcd"[:len(shape)]
        sizes = dict(zip(names[1:], shape[1:]))
        return part.rearrange(f"p ({' '.join(names)}) -> p {' '.join(names)}", **sizes)


def modulation_stage(nc, S, A, h, ident, mod_d, strips, arena, rows):
    n_chunk, ring = DEPTH * 12, 3
    with ExitStack() as ctx:
        def sb(name, shape, dt=F32):
            return ctx.enter_context(nc.sbuf_tensor(name, shape, dt))
        crow = sb("crow", [P, 2, KC])
        silu = sb("silu", [P, 2, KC])
        bufs, spare = Arena(arena), Arena(rows)
        ada = [bufs.cut(KC, HALF), bufs.cut(KC, HALF), spare.cut(KC, HALF)]
        bias = sb("ada_bias", [2, DEPTH * 6 * D])
        gain = sb("norm_gain", [2, DEPTH * 2 * D])
        row = sb("mod_row", [2, 4, HALF])
        tmp = sb("mod_tmp", [2, 2, HALF])
        lg = sb("decay_log", [P, 5, 2 * RET_HEADS])
        dist = sb("distance", [P, 3, SL])
        cdist = sb("ctx_distance", [P, 2, SC])
        dec = sb("decays", [P, 2, SL])
        ps = ctx.enter_context(nc.psum_tensor("mod_ps", [2, 4, HALF], F32))
        block = ctx.enter_context(nc.Block())

        def chunk(n):
            layer, c = divmod(n, 12)
            return layer, c // 6, (c % 6) // 2, c % 2

        @block.sync
        def _(sp):
            sp.dma_start(crow[:, 0, :], A["c_ctx"].rearrange("(p k) -> p k", p=P)).then_inc(S("c_loaded"), 16)
            sp.dma_start(crow[:, 1, :], A["c"].rearrange("a (p k) -> p (a k)", p=P)).then_inc(S("c_loaded"), 16)
            sp.dma_start(lg[:, 0, 0:RET_HEADS], A["ret_decay_logit_f"].broadcast_to([P, RET_HEADS])).then_inc(S("logits"), 16)
            sp.dma_start(lg[:, 0, RET_HEADS:], A["ret_decay_logit_b"].broadcast_to([P, RET_HEADS])).then_inc(S("logits"), 16)
            sp.dma_start(bias[:], A["ada_b"].rearrange("(a l) n -> a (l n)", a=1).broadcast_to([2, DEPTH * 6 * D])
                         ).then_inc(S("rows_loaded"), 16)
            sp.dma_start(gain[:], A["gains"].rearrange("(a l) n -> a (l n)", a=1).broadcast_to([2, DEPTH * 2 * D])
                         ).then_inc(S("rows_loaded"), 16)
            for n in range(n_chunk):
                layer, half, sec, ch = chunk(n)
                if n >= ring:
                    sp.wait_ge(S("mod_mm"), n - ring + 1)
                col = ((half * 3 + sec) * 2 + ch) * HALF
                sp.dma_start(ada[n % ring], A["ada_w"][layer].rearrange("(p k) n -> p k n", p=P)[:, :, col:col + HALF]
                             ).then_inc(S(f"ada_loaded{n % ring}"), 16)
                if n == 4:
                    sp.dma_start(h[:, 0:CT], A["ctx"][0].rearrange("(t p) d -> p t d", p=P)).then_inc(S("h_loaded"), 16)
                    sp.dma_start(h[:, CT:NT], A["x"][0].rearrange("(t p) d -> p t d", p=P)).then_inc(S("h_loaded"), 16)
            sp.wait_ge(S("h_loaded"), 32)

        @block.gpsimd
        def _(pool):
            pool.memset(ident[:], 0.0).then_inc(S("ident_zero"), 1)
            pool.wait_ge(S("ident_zero"), 1)
            pool.affine_select(out=ident[:], in_=ident[:], compare_op=ALU.not_equal, fill=1.0, base=0,
                               pattern=[[-1, P]], channel_multiplier=1).then_inc(S("ident_ready"), 1)
            few = dict(allow_small_or_imprecise_dtypes=True)
            pool.iota(dist[:, 0], [[1, SL]], base=-3 * P, channel_multiplier=-1, **few).then_inc(S("distances"), 1)
            pool.iota(cdist[:, 0], [[1, SC]], base=CTX - P, channel_multiplier=-1, **few).then_inc(S("distances"), 1)
            pool.iota(cdist[:, 1], [[-1, SC]], base=SEQ + P, channel_multiplier=1, **few).then_inc(S("distances"), 1)

        @block.scalar
        def _(act):
            act.wait_ge(S("c_loaded"), 32)
            act.activation(silu[:], crow[:], ACT.Silu).then_inc(S("silu_ready"), 1)
            act.wait_ge(S("logits_abs"), 1)
            act.activation(lg[:, 2], lg[:, 1], ACT.Exp, scale=-1.0).then_inc(S("logits_log"), 1)
            act.wait_ge(S("logits_log"), 1)
            act.activation(lg[:, 3], lg[:, 2], ACT.Ln, bias=1.0).then_inc(S("logits_log"), 1)
            act.wait_ge(S("log_gamma"), 1)
            act.wait_ge(S("distances"), 3)
            for m in range(2 * RET_HEADS):
                hd, cross = m // 2, m % 2
                for way in range(2):
                    if m:
                        act.wait_ge(S("strip"), m)
                    src = cdist[:, way] if cross else dist[:, 1 + way]
                    dst = dec[:, way, 0:SC] if cross else dec[:, way]
                    act.activation(dst, src, ACT.Exp, scale=lg[:, 4, way * RET_HEADS + hd:way * RET_HEADS + hd + 1]
                                   ).then_inc(S("decay"), 1)
            for n in range(n_chunk):
                layer, half, sec, ch = chunk(n)
                act.wait_ge(S("mod_row"), n + 1)
                act.dma_start(mod_d[layer, half, :, sec, ch * HALF:(ch + 1) * HALF], row[:, n % 4]
                              ).then_inc(S(f"mod_stored{n % 4}"), 16)
            for b in range(4):
                act.wait_ge(S(f"mod_stored{b}"), 16 * (n_chunk // 4))

        @block.tensor
        def _(pe):
            pe.wait_ge(S("silu_ready"), 1)
            for n in range(n_chunk):
                pe.wait_ge(S(f"ada_loaded{n % ring}"), 16 * (n // ring + 1))
                if n >= 4:
                    pe.wait_ge(S("mod_row"), n - 3)
                for k in range(KC):
                    ins = pe.matmul(ps[:, n % 4], silu[:, :, k], ada[n % ring][:, k], start=k == 0, stop=k == KC - 1)
                ins.then_inc(S("mod_mm"), 1)

        @block.vector
        def _(dve):
            dve.wait_ge(S("logits"), 32)
            dve.scalar_tensor_tensor(lg[:, 1], lg[:, 0], -1.0, lg[:, 0], ALU.mult, ALU.max).then_inc(S("logits_abs"), 1)
            dve.wait_ge(S("distances"), 3)
            dve.tensor_scalar(dist[:, 1], dist[:, 0], 0.0, None, ALU.max).then_inc(S("clamped"), 1)
            dve.tensor_scalar(dist[:, 2], dist[:, 0], -1.0, 0.0, ALU.mult, ALU.max).then_inc(S("clamped"), 1)
            dve.wait_ge(S("clamped"), 2)
            dve.wait_ge(S("logits_log"), 2)
            dve.scalar_tensor_tensor(lg[:, 4], lg[:, 0], 0.0, lg[:, 3], ALU.min, ALU.subtract).then_inc(S("log_gamma"), 1)
            for m in range(2 * RET_HEADS):
                hd, cross = m // 2, m % 2
                dve.wait_ge(S("decay"), 2 * (m + 1))
                if cross:
                    dve.tensor_tensor(strips[:, hd, SL:SL + SC], dec[:, 0, 0:SC], dec[:, 1, 0:SC], ALU.add).then_inc(S("strip"), 1)
                    continue
                for way, op in enumerate((ALU.is_ge, ALU.is_le)):
                    dve.scalar_tensor_tensor(dec[:, way], dist[:, 0], 0.0, dec[:, way], op, ALU.mult).then_inc(S("masked"), 1)
                dve.wait_ge(S("masked"), m + 2)
                dve.tensor_tensor(strips[:, hd, 0:SL], dec[:, 0], dec[:, 1], ALU.add).then_inc(S("strip"), 1)
            dve.wait_ge(S("rows_loaded"), 32)
            scaled = 0
            for n in range(n_chunk):
                layer, half, sec, ch = chunk(n)
                dve.wait_ge(S("mod_mm"), n + 1)
                if n >= 4:
                    dve.wait_ge(S(f"mod_stored{n % 4}"), 16 * (n // 4))
                b = bias[:, (layer * 12 + n % 12) * HALF:(layer * 12 + n % 12 + 1) * HALF]
                if sec != 1:
                    dve.tensor_tensor(row[:, n % 4], ps[:, n % 4], b, ALU.add).then_inc(S("mod_row"), 1)
                    continue
                g = gain[:, ((layer * 2 + half) * 2 + ch) * HALF:((layer * 2 + half) * 2 + ch + 1) * HALF]
                dve.tensor_tensor(tmp[:, ch], ps[:, n % 4], b, ALU.add).then_inc(S("mod_scale"), 1)
                scaled += 1
                dve.wait_ge(S("mod_scale"), scaled)
                dve.scalar_tensor_tensor(row[:, n % 4], tmp[:, ch], 1.0, g, ALU.add, ALU.mult).then_inc(S("mod_row"), 1)


def norm_squares(act, S, tag, h, junk, ss):
    for t in range(NT):
        act.activation(junk, h[:, t], ACT.Square, accum_out=ss[:, 0, t:t + 1]).then_inc(S(tag + "_squares"), 1)
        act.wait_ge(S(tag + "_squares"), t + 1)
    act.wait_ge(S(tag + "_stats"), 1)
    act.activation(ss[:, 2], ss[:, 1], ACT.Sqrt).then_inc(S(tag + "_root"), 1)


def norm_modulate(dve, S, tag, h, a, ss, rows):
    dve.wait_ge(S(tag + "_squares"), NT)
    dve.tensor_scalar(ss[:, 1], ss[:, 0], 1.0 / D, EPS, ALU.mult, ALU.add).then_inc(S(tag + "_stats"), 1)
    dve.wait_ge(S(tag + "_root"), 1)
    dve.reciprocal(ss[:, 3], ss[:, 2]).then_inc(S(tag + "_stats"), 1)
    dve.wait_ge(S(tag + "_stats"), 2)
    dve.wait_ge(S(tag + "_rows"), 32)
    for t in range(NT):
        if t >= 2:
            dve.wait_ge(S(tag + "_aT_ps"), t - 1)
        dve.scalar_tensor_tensor(a[:, t % 2], h[:, t], ss[:, 3, t:t + 1], rows[:, kind(t), 1], ALU.mult, ALU.mult)\
            .then_inc(S(tag + "_scaled"), 1)
        dve.wait_ge(S(tag + "_scaled"), t + 1)
        dve.tensor_tensor(a[:, t % 2], a[:, t % 2], rows[:, kind(t), 0], ALU.add).then_inc(S(tag + "_a"), 1)


def norm_transpose(pe, S, tag, PS, a, ident):
    pe.wait_ge(S("ident_ready"), 1)
    for t in range(NT):
        pe.wait_ge(S(tag + "_a"), t + 1)
        if t >= 2:
            pe.wait_ge(S(tag + "_aT"), t - 1)
        for k in range(KC):
            ins = pe.transpose(PS[:, 2 * (t % 2) + k // 4, (k % 4) * P:(k % 4 + 1) * P], a[:, t % 2, k * P:(k + 1) * P], ident[:])
        ins.then_inc(S(tag + "_aT_ps"), 1)


def norm_evacuate(act, S, tag, PS, aT):
    for t in range(NT):
        act.wait_ge(S(tag + "_aT_ps"), t + 1)
        act.activation(aT[:, :, t * P:(t + 1) * P],
                       PS[:, 2 * (t % 2):2 * (t % 2) + 2].rearrange("p b (k n) -> p (b k) n", k=4), ACT.Copy
                       ).then_inc(S(tag + "_aT"), 1)


def residual(dve, S, tag, h, PS, rows, tmp, tiles):
    for n in range(2 * len(tiles)):
        c, t = n // len(tiles), tiles[n % len(tiles)]
        dve.wait_ge(S(tag + "_out"), n + 1)
        if n >= 2:
            dve.wait_ge(S(tag + "_added"), n - 1)
        cols = slice(c * HALF, (c + 1) * HALF)
        dve.tensor_tensor(tmp[:, n % 2], PS[:, 6 + n % 2], rows[:, kind(t), 2, cols], ALU.mult).then_inc(S(tag + "_out_read"), 1)
        dve.wait_ge(S(tag + "_out_read"), n + 1)
        dve.tensor_tensor(h[:, t, cols], h[:, t, cols], tmp[:, n % 2], ALU.add).then_inc(S(tag + "_added"), 1)


def rope(dve, S, tag, n, outs, ps, t1, t2, cos, sin, heads):
    w = heads * HD

    def halves(x):
        return x.rearrange("p (g a n) -> p g a n", g=2 * heads, a=2)

    def by_head(x):
        return x.rearrange("p (h n) -> p h n", h=heads)

    if n:
        dve.wait_ge(S(tag + "_rope_out"), n)
    dve.tensor_tensor(by_head(t1[:, 0:w]), by_head(ps), cos.rearrange("p (o n) -> p o n", o=1).broadcast_to([P, heads, HD]),
                      ALU.mult).then_inc(S(tag + "_rope"), 1)
    for a in range(2):
        table = sin.rearrange("p (x a n) -> p x a n", x=2, a=2)[:, :, a]
        for x in range(2):
            o = t2[:, 0:w].rearrange("p (h x a n) -> p h x a n", h=heads, x=2, a=2)[:, :, x, a]
            u = ps.rearrange("p (h x a n) -> p h x a n", h=heads, x=2, a=2)[:, :, x, 1 - a]
            s = table[:, x].rearrange("p (o n) -> p o n", o=1).broadcast_to([P, heads, 16])
            dve.tensor_tensor(o, u, s, ALU.mult).then_inc(S(tag + "_rope"), 1)
    dve.wait_ge(S(tag + "_rope"), 5 * (n + 1))
    for m, o in enumerate(outs):
        ins = dve.tensor_tensor(o, by_head(t1[:, 0:w]), by_head(t2[:, 0:w]), ALU.add)
    return ins.then_inc(S(tag + "_rope_out"), 1)


def load_rows(sp, S, mod_d, rows, layer, half, name, kinds=(0, 1), parts=slice(0, 3)):
    for kd in kinds:
        sp.dma_start(rows[:, kd, parts], mod_d[layer, half, kd, parts].rearrange("(o s) d -> o s d", o=1)
                     .broadcast_to([P, parts.stop - parts.start, D])).then_inc(S(name), 16)


def peer_kinds(layer):
    return (0, 1) if layer < DEPTH - 1 else (1,)


def peer_buffers(arena):
    cuts = Arena(arena)
    return cuts.cut(KC, D), cuts.cut(NH, NK)


def load_ahead_for_peer(sp, S, A, mod_d, arena, layer):
    wq, keys = peer_buffers(arena)
    sp.dma_start(wq, A["peer_wq"][layer].rearrange("(k p) n -> p k n", p=P)).then_inc(S("peer_wq"), 16)
    sp.dma_start(keys, A["keysT"][layer]).then_inc(S("peer_keys"), 16)


SL = 3 * P + SEQ
SC = P + SEQ


def mixer0_stage(nc, S, A, h, ident, mod_d, strips, arena, rows):
    n_in, ring = 6, 2
    with ExitStack() as ctx:
        def sb(name, shape, dt=F32):
            return ctx.enter_context(nc.sbuf_tensor("m0_" + name, shape, dt))
        aT = sb("aT", [P, KC, TOK])
        w = sb("w", [P, ring, KC, HALF])
        v = sb("v", [P, NT, HALF])
        sg = sb("sg", [P, NT, HALF])
        cuts = Arena(arena)
        qT = cuts.cut(2, TOK)
        kT = cuts.cut(2, TOK)
        gb = cuts.cut(4, TOK)
        u = cuts.cut(4, TOK)
        cos = sb("cos", [P, LT, HD])
        sin = sb("sin", [P, LT, HD])
        cw = sb("cw", [P, 4, 3])
        tapped = sb("tapped", [P, TOK])
        ss = sb("ss", [P, 4, NT])
        hs = sb("hs", [P, 4, 2 * RET_HEADS, LT])
        a = sb("a", [P, 2, D])
        sq = sb("sq", [P, D])
        PS = ctx.enter_context(nc.psum_tensor("m0_ps", [P, 8, HALF], F32))
        block = ctx.enter_context(nc.Block())
        PT = a[:].rearrange("p a (b n) -> p (a b) n", b=2)
        yr = aT[:, 0:4].rearrange("p k n -> p (k n)").rearrange("p (t n) -> p t n", t=NT)
        yc = aT[:, 4:8]
        yrT = v[:].rearrange("p t n -> p (t n)").rearrange("p (k n) -> p k n", k=4)
        T = "m0"
        n_tok, n_ch = 3 * NT, 8

        items = []
        for hd in range(RET_HEADS):
            items += [(hd, 0, j) for j in range(CT)] + [(hd, 1, j) for j in range(NT)]

        @block.sync
        def _(sp):
            load_rows(sp, S, mod_d, rows, 0, 0, "m0_rows")
            sp.dma_start(cos[:], A["rope_cos"].rearrange("(t p) n -> p t n", p=P)).then_inc(S("m0_tabs"), 16)
            sp.dma_start(sin[:], A["rope_sin"].rearrange("(t p) n -> p t n", p=P)).then_inc(S("m0_tabs"), 16)
            sp.dma_start(cw[:], A["conv_wT"].rearrange("(m p) i -> p m i", p=P)).then_inc(S("m0_tabs"), 16)
            for n in range(n_in + 2):
                if n >= ring:
                    c = n - ring
                    sp.wait_ge(S("m0_proj"), NT * (c + 1) if c < 3 else n_tok + n_ch * (c - 2))
                src = A["ev_w_in"][0] if n < n_in else A["ev_w_out"][0]
                c = (n if n < n_in else n - n_in) * HALF
                sp.dma_start(w[:, n % ring], src.rearrange("(k p) n -> p k n", p=P)[:, :, c:c + HALF]
                             ).then_inc(S(f"m0_w{n % ring}"), 16)
            sp.wait_ge(S("m0_a"), NT)
            load_rows(sp, S, mod_d, rows, 0, 1, "peer_rows", parts=slice(0, 2))
            sp.wait_ge(S("m0_conv_out"), 4)
            sp.wait_ge(S("m0_S"), len(items))
            load_ahead_for_peer(sp, S, A, mod_d, arena, 0)

        @block.gpsimd
        def _(pool):
            pool.wait_ge(S("m0_tabs"), 48)
            pool.wait_ge(S("m0_u"), n_ch)
            pool.wait_ge(S("m0_ev"), 2 * NT + 2 * n_ch)
            pool.wait_ge(S("m0_proj"), n_tok + 3 * n_ch)
            links = 0
            for m in range(4):
                y = yc[:, m]
                pool.tensor_scalar(y, u[:, m], cw[:, m, 1:2], None, ALU.mult).then_inc(S("m0_conv"), 1)
                links += 1
                for tap, out, src in ((0, slice(1, 0), slice(0, -1)), (2, slice(0, -1), slice(1, 0))):
                    pool.wait_ge(S("m0_conv"), links)
                    pool.tensor_scalar(tapped[:], u[:, m], cw[:, m, tap:tap + 1], None, ALU.mult).then_inc(S("m0_conv"), 1)
                    links += 1
                    pool.wait_ge(S("m0_conv"), links)
                    for lo, hi in ((0, CTX), (CTX, TOK)):
                        y_at, u_at = y[:, lo + out.start:hi + out.stop], tapped[:, lo + src.start:hi + src.stop]
                        pool.tensor_tensor(y_at, y_at, u_at, ALU.add).then_inc(S("m0_conv"), 1)
                    links += 2
                pool.wait_ge(S("m0_conv"), links)
                pool.tensor_tensor(y, y, gb[:, m], ALU.mult).then_inc(S("m0_conv_out"), 1)

        @block.scalar
        def _(act):
            norm_squares(act, S, T, h, sq[:], ss)
            norm_evacuate(act, S, T, PS, aT)
            for n in range(NT, n_tok):
                c, t = divmod(n, NT)
                act.wait_ge(S("m0_proj"), n + 1)
                dst = v if c == 1 else sg
                act.activation(dst[:, t], PS[:, 4 + n % 4], ACT.Copy if c == 1 else ACT.Silu).then_inc(S("m0_ev"), 1)
                if n == 2 * NT - 1:
                    for t in range(NT):
                        act.wait_ge(S("m0_qkT_ps"), t + 1)
                        blk = PS[:, t % 2].rearrange("p (b n) -> p b n", b=4)
                        act.activation(qT[:, :, t * P:(t + 1) * P], blk[:, 0:2], ACT.Copy).then_inc(S("m0_qT"), 1)
                        act.activation(kT[:, :, t * P:(t + 1) * P], blk[:, 2:4], ACT.Copy, scale=SCALE).then_inc(S("m0_qT"), 1)
            for i in range(2 * n_ch):
                n = n_tok + i
                m, th = divmod(i % n_ch, 2)
                act.wait_ge(S("m0_proj"), n + 1)
                act.activation((gb if i < n_ch else u)[:, m, th * 3 * P:(th + 1) * 3 * P], PS[:, 4 + n % 4, 0:3 * P], ACT.Copy
                               ).then_inc(S("m0_ev"), 1)
            for g in range(2 * RET_HEADS):
                nt = LT if g % 2 else CT
                act.wait_ge(S("m0_pv"), g // 2 * (CT + NT) + (CT + NT if g % 2 else CT))
                if g:
                    act.wait_ge(S("m0_ret_ss"), g)
                act.activation(sq[:, 0:nt * P], PS[:, 4 + g % 2, 0:nt * P], ACT.Square).then_inc(S("m0_ret_sq"), 1)
                act.wait_ge(S("m0_ret_ms"), g + 1)
                act.activation(hs[:, 2, g, 0:nt], hs[:, 1, g, 0:nt], ACT.Sqrt).then_inc(S("m0_ret_root"), 1)
            for t in range(NT):
                act.wait_ge(S("m0_yT_ps"), t + 1)
                act.activation(yrT[:, :, t * P:(t + 1) * P], PS[:, t % 2].rearrange("p (b n) -> p b n", b=4), ACT.Copy
                               ).then_inc(S("m0_yT"), 1)

        @block.tensor
        def _(pe):
            def bank_free(n):
                if n < NT:
                    pe.wait_ge(S("m0_qk"), n + 1)
                elif n < n_tok + 2 * n_ch:
                    pe.wait_ge(S("m0_ev"), n - NT + 1)
                else:
                    pe.wait_ge(S("m0_u"), n - n_tok - 2 * n_ch + 1)

            norm_transpose(pe, S, T, PS, a, ident)
            pe.wait_ge(S("m0_aT"), NT)
            n = 0
            for c in range(3):
                pe.wait_ge(S(f"m0_w{c % ring}"), 16 * (c // ring + 1))
                for t in range(NT):
                    if n >= 4:
                        bank_free(n - 4)
                    for k in range(KC):
                        ins = pe.matmul(PS[:, 4 + n % 4], aT[:, k, t * P:(t + 1) * P], w[:, c % ring, k], start=k == 0, stop=k == KC - 1)
                    ins.then_inc(S("m0_proj"), 1)
                    n += 1
                if c == 1:
                    for t in range(NT):
                        pe.wait_ge(S("m0_qk"), t + 1)
                        if t >= 2:
                            pe.wait_ge(S("m0_qT"), 2 * (t - 1))
                        for m in range(4):
                            ins = pe.transpose(PS[:, t % 2, m * P:(m + 1) * P], sg[:, t, m * P:(m + 1) * P], ident[:])
                        ins.then_inc(S("m0_qkT_ps"), 1)
            for c in range(3, 6):
                pe.wait_ge(S(f"m0_w{c % ring}"), 16 * (c // ring + 1))
                for m in range(4):
                    for th in range(2):
                        bank_free(n - 4)
                        for k in range(KC):
                            ins = pe.matmul(PS[:, 4 + n % 4, 0:3 * P], w[:, c % ring, k, m * P:(m + 1) * P],
                                            aT[:, k, th * 3 * P:(th + 1) * 3 * P], start=k == 0, stop=k == KC - 1)
                        ins.then_inc(S("m0_proj"), 1)
                        n += 1
            for m in range(n - 4, n):
                bank_free(m)
            pe.wait_ge(S("m0_qT"), 2 * NT)

            def scores(i):
                hd, kd, j = items[i]
                p0 = (hd % 2) * HD
                if i >= 2:
                    pe.wait_ge(S("m0_P"), i - 1)
                lo, hi = (CTX, TOK) if kd else (0, CTX)
                pe.matmul(PS[:, 2 + i % 2, 0:hi - lo], kT[p0:p0 + HD, hd // 2, j * P:(j + 1) * P],
                          qT[p0:p0 + HD, hd // 2, lo:hi], start=True, stop=True).then_inc(S("m0_S"), 1)

            def values(i):
                hd, kd, j = items[i]
                nt, last = (LT, NT - 1) if kd else (CT, CT - 1)
                pe.wait_ge(S("m0_P"), i + 1)
                if j == 0 and hd >= 1:
                    pe.wait_ge(S("m0_ret_y"), 2 * (hd - 1) + kd + 1)
                for it in range(nt):
                    ins = pe.matmul(PS[:, 4 + kd, it * P:(it + 1) * P], PT[:, i % 4, it * P:(it + 1) * P],
                                    v[:, j, hd * RET_V:(hd + 1) * RET_V], start=j == 0 and it == 0, stop=j == last,
                                    skip_group_check=True)
                ins.then_inc(S("m0_pv"), 1)

            for i in range(len(items)):
                scores(i)
                if i >= 1:
                    values(i - 1)
            values(len(items) - 1)
            pe.wait_ge(S("m0_ret_y"), 2 * RET_HEADS)
            for t in range(NT):
                if t >= 2:
                    pe.wait_ge(S("m0_yT"), t - 1)
                for m in range(4):
                    ins = pe.transpose(PS[:, t % 2, m * P:(m + 1) * P], yr[:, t, m * P:(m + 1) * P], ident[:])
                ins.then_inc(S("m0_yT_ps"), 1)
            pe.wait_ge(S("m0_yT"), NT)
            pe.wait_ge(S("m0_conv_out"), 4)
            for n in range(2 * NT):
                c, t = divmod(n, NT)
                q = n_in + c
                if t == 0:
                    pe.wait_ge(S(f"m0_w{q % ring}"), 16 * (q // ring + 1))
                if n >= 2:
                    pe.wait_ge(S("m0_out_read"), n - 1)
                for k in range(KC):
                    y = yrT[:, k, t * P:(t + 1) * P] if k < 4 else yc[:, k - 4, t * P:(t + 1) * P]
                    ins = pe.matmul(PS[:, 6 + n % 2], y, w[:, q % ring, k], start=k == 0, stop=k == KC - 1)
                ins.then_inc(S("m0_out"), 1)

        @block.vector
        def _(dve):
            norm_modulate(dve, S, T, h, a, ss, rows)
            dve.wait_ge(S("m0_tabs"), 48)
            dve.wait_ge(S("m0_aT_ps"), NT)
            for t in range(NT):
                dve.wait_ge(S("m0_proj"), t + 1)
                if t < CT:
                    dve.tensor_copy(sg[:, t], PS[:, 4 + t % 4]).then_inc(S("m0_qk"), 1)
                else:
                    rope(dve, S, T, t - CT, [sg[:, t].rearrange("p (h n) -> p h n", h=8)], PS[:, 4 + t % 4], a[:, 0, 0:HALF],
                         a[:, 0, HALF:D], cos[:, t - CT], sin[:, t - CT], 8)
                    dve.wait_ge(S("m0_rope_out"), t - CT + 1)
                    dve.sem_inc(S("m0_qk"), 1)
            for i in range(n_ch):
                n = n_tok + 2 * n_ch + i
                m, th = divmod(i, 2)
                dve.wait_ge(S("m0_proj"), n + 1)
                dve.wait_ge(S("m0_ev"), 2 * NT + n_ch + i + 1)
                seg = u[:, m, th * 3 * P:(th + 1) * 3 * P]
                dve.tensor_tensor(seg, seg, PS[:, 4 + n % 4, 0:3 * P], ALU.mult).then_inc(S("m0_u"), 1)
            links = 0

            def link(ins):
                nonlocal links
                links += 1
                ins.then_inc(S("m0_link"), 1)
                dve.wait_ge(S("m0_link"), links)

            def head_norm(hd, kd):
                g = 2 * hd + kd
                nt, t0 = (LT, CT) if kd else (CT, 0)
                dve.wait_ge(S("m0_ret_sq"), g + 1)
                dve.tensor_reduce(hs[:, 0, g, 0:nt], sq[:, 0:nt * P].rearrange("p (t n) -> p t n", t=nt), AX.X, ALU.add
                                  ).then_inc(S("m0_ret_ss"), 1)
                dve.wait_ge(S("m0_ret_ss"), g + 1)
                dve.tensor_scalar(hs[:, 1, g, 0:nt], hs[:, 0, g, 0:nt], 1.0 / RET_V, EPS, ALU.mult, ALU.add
                                  ).then_inc(S("m0_ret_ms"), 1)
                dve.wait_ge(S("m0_ret_root"), g + 1)
                link(dve.reciprocal(hs[:, 3, g, 0:nt], hs[:, 2, g, 0:nt]))
                for it in range(nt):
                    cols = slice(hd * RET_V, (hd + 1) * RET_V)
                    ins = dve.scalar_tensor_tensor(yr[:, t0 + it, cols], PS[:, 4 + kd, it * P:(it + 1) * P], hs[:, 3, g, it:it + 1],
                                                   sg[:, t0 + it, cols], ALU.mult, ALU.mult)
                ins.then_inc(S("m0_ret_y"), 1)

            for i, (hd, kd, j) in enumerate(items):
                dve.wait_ge(S("m0_S"), i + 1)
                if i >= 4:
                    dve.wait_ge(S("m0_pv"), i - 3)
                if kd == 0:
                    x, nq = 3 * P - j * P, CTX
                elif j < CT:
                    x, nq = SL + P - j * P, SEQ
                else:
                    x, nq = 3 * P - (j - CT) * P, SEQ
                dve.tensor_tensor(PT[:, i % 4, 0:nq], PS[:, 2 + i % 2, 0:nq], strips[:, hd, x:x + nq], ALU.mult
                                  ).then_inc(S("m0_P"), 1)
                if kd == 0 and j == CT - 1 and hd:
                    head_norm(hd - 1, 1)
                if kd == 1 and j == 2:
                    head_norm(hd, 0)
            head_norm(RET_HEADS - 1, 1)
            dve.wait_ge(S("m0_P"), len(items))
            dve.wait_ge(S("m0_pv"), len(items))
            residual(dve, S, T, h, PS, rows, PT, list(range(NT)))


def mixer1_stage(nc, S, A, h, ident, mod_d, arena, rows):
    ring = 3
    BAND = P + 2 * 128
    chunks = [("od_w_in", 0), ("od_w_in", 1), ("od_w_in", 2), ("od_w_out", 0), ("od_w_out", 1)]
    with ExitStack() as ctx:
        def sb(name, shape, dt=F32):
            return ctx.enter_context(nc.sbuf_tensor("m1_" + name, shape, dt))
        aT = sb("aT", [P, KC, TOK])
        w01 = sb("w", [P, 2, KC, HALF])
        cuts = Arena(arena)
        w = [w01[:, 0], w01[:, 1], cuts.cut(KC, HALF)]
        qT = sb("qT", [P, ATT_HEADS // 2, SEQ])
        kT = sb("kT", [P, KV_HEADS, TOK])
        v = sb("v", [P, NT, KV_HEADS, 2, HD])
        qtok = sb("qtok", [P, 2, HALF])
        ktok = cuts.cut(2, KV_HEADS, 2 * HD)
        cos = cuts.cut(LT, HD)
        sin = cuts.cut(LT, HD)
        ss = sb("ss", [P, 4, NT])
        a = cuts.cut(2, D)
        sq = cuts.cut(D)
        mask = sb("mask", [P, BAND])
        sink = sb("sink", [P, ATT_HEADS])
        lgt = sb("logits", [P, 2, CTX + BAND + 1])
        pr = sb("probs", [P, 3, CTX + BAND + 1])
        dg = sb("inverse_sums", [P, 2, P])
        pT = sb("probsT", [P, 2, CTX + BAND])
        st = sb("stats", [P, 4, LT * ATT_HEADS])
        PS = ctx.enter_context(nc.psum_tensor("m1_ps", [P, 8, HALF], F32))
        block = ctx.enter_context(nc.Block())
        T = "m1"
        oT = aT[:].rearrange("p k n -> p (k n)")[:, 0:KC * SEQ].rearrange("p (k n) -> p k n", k=KC)
        n_q = 2 * LT
        items = [(b, hd) for b in range(LT) for hd in range(ATT_HEADS)]

        def window(b):
            return max(b - 1, 0), min(b + 2, LT)

        def keys(b):
            lo, hi = window(b)
            return CTX + lo * P, (hi - lo) * P

        def key_tiles(b):
            lo, hi = window(b)
            return list(range(CT)) + [CT + j for j in range(lo, hi)]

        @block.sync
        def _(sp):
            load_rows(sp, S, mod_d, rows, 1, 0, "m1_rows")
            sp.dma_start(cos, A["rope_cos"].rearrange("(t p) n -> p t n", p=P)).then_inc(S("m1_tabs"), 16)
            sp.dma_start(sin, A["rope_sin"].rearrange("(t p) n -> p t n", p=P)).then_inc(S("m1_tabs"), 16)
            sp.dma_start(sink[:], A["attn_sinks"].broadcast_to([P, ATT_HEADS])).then_inc(S("m1_tabs"), 16)
            for n, (name, c) in enumerate(chunks):
                if n >= ring:
                    sp.wait_ge(S("m1_proj"), LT * (n - ring + 1))
                sp.dma_start(w[n % ring], A[name][0].rearrange("(k p) n -> p k n", p=P)[:, :, c * HALF:(c + 1) * HALF]
                             ).then_inc(S(f"m1_w{n % ring}"), 16)
            sp.wait_ge(S("m1_a"), NT)
            load_rows(sp, S, mod_d, rows, 1, 1, "peer_rows", peer_kinds(1), slice(0, 2))
            sp.wait_ge(S("m1_kT"), NT)
            sp.wait_ge(S("m1_v"), NT)
            load_ahead_for_peer(sp, S, A, mod_d, arena, 1)

        @block.gpsimd
        def _(pool):
            pool.memset(mask[:], 0.0).then_inc(S("m1_mask"), 1)
            pool.wait_ge(S("m1_mask"), 1)
            pool.affine_select(out=mask[:], in_=mask[:], compare_op=ALU.is_ge, fill=NEG, base=0, pattern=[[1, BAND]],
                               channel_multiplier=-1).then_inc(S("m1_mask"), 1)
            pool.wait_ge(S("m1_mask"), 2)
            pool.affine_select(out=mask[:], in_=mask[:], compare_op=ALU.is_ge, fill=NEG, base=2 * 128, pattern=[[-1, BAND]],
                               channel_multiplier=1).then_inc(S("m1_mask"), 1)

        @block.scalar
        def _(act):
            norm_squares(act, S, T, h, sq, ss)
            norm_evacuate(act, S, T, PS, aT)
            for n in range(n_q):
                act.wait_ge(S("m1_qT_ps"), n + 1)
                c, t = divmod(n, LT)
                act.activation(qT[:, 4 * c:4 * c + 4, t * P:(t + 1) * P], PS[:, n % 2].rearrange("p (m n) -> p m n", m=4), ACT.Copy
                               ).then_inc(S("m1_qT"), 1)
            for t in range(NT):
                act.wait_ge(S("m1_kT_ps"), t + 1)
                act.activation(kT[:, :, t * P:(t + 1) * P], PS[:, t % 2].rearrange("p (m n) -> p m n", m=4), ACT.Copy
                               ).then_inc(S("m1_kT"), 1)

            def probs(i):
                b, hd = items[i]
                w_all = CTX + keys(b)[1] + 1
                act.wait_ge(S("m1_negm"), i + 1)
                if i >= 3:
                    act.wait_ge(S("m1_pT_ps"), i - 2)
                act.activation(pr[:, i % 3, 0:w_all], lgt[:, i % 2, 0:w_all], ACT.Exp, bias=st[:, 1, i:i + 1],
                               accum_out=st[:, 2, i:i + 1]).then_inc(S("m1_probs"), 1)

            def inverse_sums(i):
                act.wait_ge(S("m1_recip"), i + 1)
                if i >= 2:
                    act.wait_ge(S("m1_pT_ps"), i - 1)
                act.activation(dg[:, i % 2], ident[:], ACT.Copy, scale=st[:, 3, i:i + 1]).then_inc(S("m1_diag"), 1)

            def transposed(i):
                b, hd = items[i]
                n = CTX + keys(b)[1]
                act.wait_ge(S("m1_pT_ps"), i + 1)
                if i >= 2:
                    act.wait_ge(S("m1_o"), i - 1)
                act.activation(pT[:, i % 2, 0:n], PS[:, 4:6].rearrange("p b n -> p (b n)")[:, 0:n], ACT.Copy).then_inc(S("m1_pT"), 1)

            for i in range(len(items) + 2):
                if 1 <= i <= len(items):
                    inverse_sums(i - 1)
                if i >= 2:
                    transposed(i - 2)
                if i < len(items):
                    probs(i)

        @block.tensor
        def _(pe):
            norm_transpose(pe, S, T, PS, a, ident)
            pe.wait_ge(S("m1_aT"), NT)

            def q_transpose(n):
                pe.wait_ge(S("m1_rope_out"), n + 1)
                if n >= 2:
                    pe.wait_ge(S("m1_qT"), n - 1)
                for m in range(4):
                    ins = pe.transpose(PS[:, n % 2, m * P:(m + 1) * P], qtok[:, n % 2, m * P:(m + 1) * P], ident[:])
                ins.then_inc(S("m1_qT_ps"), 1)

            def k_transpose(t):
                pe.wait_ge(S("m1_k"), t + 1)
                if t >= 2:
                    pe.wait_ge(S("m1_kT"), t - 1)
                else:
                    pe.wait_ge(S("m1_qT"), n_q - 1 + t)
                for m in range(4):
                    ins = pe.transpose(PS[:, t % 2, m * P:(m + 1) * P], ktok[:, t % 2, m], ident[:])
                ins.then_inc(S("m1_kT_ps"), 1)

            for n in range(n_q + NT):
                c, t = (n // LT, CT + n % LT) if n < n_q else (2, n - n_q)
                if n in (0, LT, n_q):
                    pe.wait_ge(S(f"m1_w{c % ring}"), 16 * (c // ring + 1))
                if n >= 4:
                    if n - 4 < n_q:
                        pe.wait_ge(S("m1_rope_out"), n - 3)
                    else:
                        pe.wait_ge(S("m1_v"), n - 4 - n_q + 1)
                for k in range(KC):
                    ins = pe.matmul(PS[:, 4 + n % 4], aT[:, k, t * P:(t + 1) * P], w[c % ring][:, k], start=k == 0, stop=k == KC - 1)
                ins.then_inc(S("m1_proj"), 1)
                if 1 <= n <= n_q:
                    q_transpose(n - 1)
                elif n > n_q:
                    k_transpose(n - n_q - 1)
            k_transpose(NT - 1)
            pe.wait_ge(S("m1_kT"), NT)
            pe.wait_ge(S("m1_v"), NT)

            def scores(i):
                b, hd = items[i]
                kv, p0, s0 = hd // (ATT_HEADS // KV_HEADS), (hd % 2) * HD, 2 * (i % 2)
                at, n = keys(b)
                if i >= 2:
                    pe.wait_ge(S("m1_logits"), i - 1)
                q = qT[p0:p0 + HD, hd // 2, b * P:(b + 1) * P]
                pe.matmul(PS[:, s0, 0:CTX], q, kT[p0:p0 + HD, kv, 0:CTX], start=True, stop=True)
                pe.matmul(PS[:, s0 + 1, 0:n], q, kT[p0:p0 + HD, kv, at:at + n], start=True, stop=True).then_inc(S("m1_S"), 1)

            def transposes(i):
                b, hd = items[i]
                pe.wait_ge(S("m1_probs"), i + 1)
                pe.wait_ge(S("m1_diag"), i + 1)
                if i >= 1:
                    pe.wait_ge(S("m1_pT"), i)
                for m in range(len(key_tiles(b))):
                    ins = pe.matmul(PS[:, 4 + m // 4, (m % 4) * P:(m % 4 + 1) * P], pr[:, i % 3, m * P:(m + 1) * P], dg[:, i % 2],
                                    start=True, stop=True, skip_group_check=True)
                ins.then_inc(S("m1_pT_ps"), 1)

            def values(i):
                b, hd = items[i]
                kv, tiles = hd // (ATT_HEADS // KV_HEADS), key_tiles(b)
                pe.wait_ge(S("m1_pT"), i + 1)
                if i >= 2:
                    pe.wait_ge(S("m1_oT"), i - 1)
                for m, t in enumerate(tiles):
                    ins = pe.matmul(PS[:, 6 + i % 2, 0:P], v[:, t, kv].rearrange("p a n -> p (a n)"), pT[:, i % 2, m * P:(m + 1) * P],
                                    start=m == 0, stop=m == len(tiles) - 1)
                ins.then_inc(S("m1_o"), 1)

            for i in range(len(items) + 3):
                if i < len(items):
                    scores(i)
                if 2 <= i <= len(items) + 1:
                    transposes(i - 2)
                if i >= 3:
                    values(i - 3)
            pe.wait_ge(S("m1_oT"), len(items))
            for n in range(2 * LT):
                c, t = divmod(n, LT)
                q = 3 + c
                if t == 0:
                    pe.wait_ge(S(f"m1_w{q % ring}"), 16 * (q // ring + 1))
                if n >= 2:
                    pe.wait_ge(S("m1_out_read"), n - 1)
                for k in range(KC):
                    ins = pe.matmul(PS[:, 6 + n % 2], oT[:, k, t * P:(t + 1) * P], w[q % ring][:, k], start=k == 0, stop=k == KC - 1)
                ins.then_inc(S("m1_out"), 1)

        @block.vector
        def _(dve):
            norm_modulate(dve, S, T, h, a, ss, rows)
            dve.wait_ge(S("m1_tabs"), 48)
            dve.wait_ge(S("m1_aT_ps"), NT)
            t1, t2 = a[:, 0, 0:HALF], a[:, 0, HALF:D]
            for n in range(n_q):
                dve.wait_ge(S("m1_proj"), n + 1)
                if n >= 2:
                    dve.wait_ge(S("m1_qT_ps"), n - 1)
                rope(dve, S, T, n, [qtok[:, n % 2].rearrange("p (h n) -> p h n", h=8)], PS[:, 4 + n % 4], t1, t2,
                     cos[:, n % LT], sin[:, n % LT], 8)
            for t in range(NT):
                n = n_q + t
                ps = PS[:, 4 + n % 4]
                dve.wait_ge(S("m1_proj"), n + 1)
                if t >= 2:
                    dve.wait_ge(S("m1_kT_ps"), t - 1)
                outs = [ktok[:, t % 2, :, x * HD:(x + 1) * HD] for x in range(2)]
                if t < CT:
                    for x, o in enumerate(outs):
                        ins = dve.tensor_copy(o, ps[:, 0:KV_HEADS * HD].rearrange("p (h n) -> p h n", h=KV_HEADS))
                    ins.then_inc(S("m1_k"), 1)
                else:
                    rope(dve, S, T, n_q + t - CT, outs, ps[:, 0:KV_HEADS * HD], t1, t2, cos[:, t - CT], sin[:, t - CT], KV_HEADS)
                    dve.wait_ge(S("m1_rope_out"), n_q + t - CT + 1)
                    dve.sem_inc(S("m1_k"), 1)
                dve.tensor_copy(v[:, t], ps[:, KV_HEADS * HD:HALF].rearrange("p (h o n) -> p h o n", h=KV_HEADS, o=1)
                                .broadcast_to([P, KV_HEADS, 2, HD])).then_inc(S("m1_v"), 1)
            dve.wait_ge(S("m1_mask"), 3)

            def logits(i):
                b, hd = items[i]
                n = keys(b)[1]
                m0 = P if b == 0 else 0
                dve.wait_ge(S("m1_S"), i + 1)
                if i >= 2:
                    dve.wait_ge(S("m1_probs"), i - 1)
                L = lgt[:, i % 2]
                dve.tensor_scalar(L[:, 0:CTX], PS[:, 2 * (i % 2), 0:CTX], SCALE, None, ALU.mult)
                dve.tensor_copy(L[:, CTX + n:CTX + n + 1], sink[:, hd:hd + 1])
                dve.scalar_tensor_tensor(L[:, CTX:CTX + n], PS[:, 2 * (i % 2) + 1, 0:n], SCALE, mask[:, m0:m0 + n], ALU.mult, ALU.add
                                         ).then_inc(S("m1_logits"), 1)
                if i >= 1:
                    inverse(i - 1)
                dve.wait_ge(S("m1_logits"), i + 1)
                dve.tensor_reduce(st[:, 0, i:i + 1], L[:, 0:CTX + n + 1], AX.X, ALU.max).then_inc(S("m1_max"), 1)
                dve.wait_ge(S("m1_max"), i + 1)
                dve.tensor_scalar(st[:, 1, i:i + 1], st[:, 0, i:i + 1], -1.0, None, ALU.mult).then_inc(S("m1_negm"), 1)

            def inverse(i):
                dve.wait_ge(S("m1_probs"), i + 1)
                dve.reciprocal(st[:, 3, i:i + 1], st[:, 2, i:i + 1]).then_inc(S("m1_recip"), 1)

            def output(i):
                b, hd = items[i]
                p0 = (hd % 2) * HD
                dve.wait_ge(S("m1_o"), i + 1)
                dve.tensor_copy(oT[p0:p0 + HD, hd // 2, b * P:(b + 1) * P], PS[p0:p0 + HD, 6 + i % 2, 0:P]).then_inc(S("m1_oT"), 1)

            for i in range(len(items) + 4):
                if i < len(items):
                    logits(i)
                if i == len(items):
                    inverse(i - 1)
                if i >= 4:
                    output(i - 4)
            residual(dve, S, T, h, PS, rows, qtok, [CT + t for t in range(LT)])


R_LINKS = 19
R_PIECES = 4

PAIRS_T = NH * PAIRS
ACT_SQUARE, DVE_MEAN, ACT_ROOT, DVE_MOD = 1, 3, 4, 6
PE_F_T, ACT_F_T, PE_Q, ACT_Q, PE_Q_T, ACT_Q_T, PE_S, ACT_S = 8, 10, 12, 22, 24, 26, 28, 32
ROUTE_NOW = {3: 6, 8: 7}
ROUTE_FIRST = {4 * n: LAG + n for n in range(NH - LAG)}
ROUTE_NEXT = {33 + 4 * n: n for n in range(NH - LAG)}


def peer_stage(nc, S, A, h, ident, mod_d, arena, rows, layer, t0, first, n_tiles):
    T = f"peer{layer}_"
    TS = NH * TOPK
    with ExitStack() as ctx:
        def sb(name, shape, dt=F32):
            return ctx.enter_context(nc.sbuf_tensor(T + name, shape, dt))

        def sem(name):
            return S("peer_" + name)

        ring = sb("ring", [P, RING, 2 * D])
        wq, keys = peer_buffers(arena)
        f = sb("f", [P, D])
        fn = sb("fn", [P, D])
        fT = sb("fT", [P, KC, P])
        q = sb("q", [P, D])
        qT = sb("qT", [P, NH, P])
        sc = sb("scores", [P, 2, 2, NH // 2, NK])
        y = sb("y", [P, D])
        diag = sb("diag", [P, RING, P])
        ss = sb("ss", [P, 4])
        iota = sb("iota", [P, TOPK])
        top = sb("top", [P, 2, TOPK])
        topi = sb("topi", [P, 2, TOPK], U32)
        topf = sb("topf", [P, 2, TOPK])
        cand = sb("cand", [P, TOPK, TOPK])
        cs = sb("cs", [P, NH, TOPK])
        ci = sb("ci", [P, TOPK], U32)
        ab = sb("ab", [P, 2, TOPK], U32)
        abf = sb("abf", [P, 2, TOPK])
        hot = sb("hot", [P, 2, TOPK, TOPK])
        e12 = sb("e12", [P, 2, TOPK])
        ef = sb("ef", [P, TOPK])
        idx = sb("idx", [P, NH, TOPK], U32)
        negm = sb("negm", [P, NH])
        gexp = sb("gexp", [P, NH, TOPK])
        gsum = sb("gsum", [P, NH])
        grec = sb("grec", [P, NH])
        u = sb("u", [P, 4, PAIR])
        gel = sb("gel", [P, 4, PAIR])
        coef = sb("coef", [P, 4, PAIR])
        PY = ctx.enter_context(nc.psum_tensor(T + "py", [P, 2, 2, HALF], F32))
        PB = ctx.enter_context(nc.psum_tensor(T + "pb", [P, 4, HALF], F32))
        block = ctx.enter_context(nc.Block())

        rows_loads = sum(len(peer_kinds(l)) for l in range(layer + 1))
        shift = first - t0

        def wait_apart(eng, which, value):
            eng.wait_ge(which, value)
            eng.sem_inc(sem("passed_" + ("pool" if eng is nc.gpsimd else "dve")), 1)

        def row_kind(t):
            return (t - shift + CT) // LT if t0 < CT else 1

        def tiles(eng, body):
            body(first, ROUTE_FIRST, ROUTE_NEXT)
            with eng.Fori(first + 1, first + n_tiles - 1) as i:
                body(i, ROUTE_NOW, ROUTE_NEXT)
            body(first + n_tiles - 1, ROUTE_NOW, {})

        def heads_at(g, table):
            return [table[g]] if g in table else []

        @block.sync
        def _(sp):
            load_rows(sp, S, mod_d, rows, layer, 1, "peer_gates", peer_kinds(layer), slice(2, 3))

        @block.gpsimd
        def _(pool):
            pool.iota(iota[:], [[1, TOPK]], base=0, channel_multiplier=0, allow_small_or_imprecise_dtypes=True
                      ).then_inc(sem("iota"), 1)

            def body(i, now, nxt):
                for hd in range(NH):
                    pool.wait_ge(sem("idx"), i * NH + hd + 1)
                    for j in range(TOPK):
                        s = hd * TOPK + j
                        wait_apart(pool, sem("slot_free"), i * TS + s + 1)
                        pool.indirect_dma_start(ring[:, s % RING], None, A["uv"], bass.IndirectOffsetOnAxis(idx[:, hd, j:j + 1], 0)
                                                ).then_inc(sem(f"landed{s % RING}"), 16)
            tiles(pool, body)

        @block.scalar
        def _(act):
            def prep(i, step):
                if step == "square":
                    act.activation(q[:], h[:, i - shift], ACT.Square, accum_out=ss[:, 0:1]).then_inc(sem("square"), 1)
                elif step == "root":
                    act.wait_ge(sem("mean"), i + 1)
                    act.activation(ss[:, 2:3], ss[:, 1:2], ACT.Sqrt).then_inc(sem("root"), 1)
                elif step == "fT":
                    act.wait_ge(sem("fT_ps"), i + 1)
                    act.activation(fT[:], PB[:, 0:2].rearrange("p b (k n) -> p (b k) n", k=4), ACT.Copy).then_inc(sem("fT"), 1)
                elif step == "q":
                    act.wait_ge(sem("q_ps"), i + 1)
                    act.activation(q[:], PB[:, 2:4].rearrange("p b n -> p (b n)"), ACT.Copy).then_inc(sem("q"), 1)
                elif step == "qT":
                    act.wait_ge(sem("qT_ps"), i + 1)
                    act.activation(qT[:], PB[:, 0:2].rearrange("p b (k n) -> p (b k) n", k=4), ACT.Copy).then_inc(sem("qT"), 1)
                elif step == "s":
                    act.wait_ge(sem("s_ps"), i + 1)
                    if i is not first or first:
                        act.wait_ge(sem("idx"), i * NH)
                    act.activation(sc[:].rearrange("p g a h n -> p (g a h n)"), PB[:].rearrange("p b n -> p (b n)"), ACT.Copy
                                   ).then_inc(sem("s"), 1)

            def prep_first(part):
                def said(name):
                    return (name, i + 1) if part else ("first_" + name, layer + 1)
                i, cols, hds = first, slice(part * HALF, (part + 1) * HALF), slice(4 * part, 4 * part + 4)
                ps_name, count = said("q_ps")
                act.wait_ge(sem(ps_name), count)
                act.activation(q[:, cols], PB[:, 2 + part], ACT.Copy).then_inc(sem(said("q")[0]), 1)
                ps_name, count = said("qT_ps")
                act.wait_ge(sem(ps_name), count)
                act.activation(qT[:, hds], PB[:, 2 * part].rearrange("p (k n) -> p k n", k=4), ACT.Copy
                               ).then_inc(sem(said("qT")[0]), 1)
                ps_name, count = said("s_ps")
                act.wait_ge(sem(ps_name), count)
                if first:
                    act.wait_ge(sem("idx"), first * NH)
                act.activation(sc[:, part].rearrange("p g h n -> p (g h n)"), PB[:, 2 * part:2 * part + 2].rearrange("p b n -> p (b n)"),
                               ACT.Copy).then_inc(sem(said("s")[0]), 1)

            def gate(i, hd):
                act.wait_ge(sem("negm"), i * NH + hd + 1)
                act.activation(gexp[:, hd], cs[:, hd], ACT.Exp, bias=negm[:, hd:hd + 1], accum_out=gsum[:, hd:hd + 1]
                               ).then_inc(sem("gexp"), 1)

            for step in ("square", "root", "fT"):
                prep(first, step)
            for part in range(2):
                prep_first(part)
            for hd in range(LAG):
                gate(first, hd)

            def body(i, now, nxt):
                for g in range(PAIRS_T):
                    act.wait_ge(sem("dot"), i * TS + PAIR * (g + 1))
                    act.activation(gel[:, g % 4], u[:, g % 4], ACT.Gelu).then_inc(sem("gelu"), 1)
                    act.wait_ge(sem("coef"), i * PAIRS_T + g + 1)
                    for j in range(PAIR):
                        act.activation(diag[:, (PAIR * g + j) % RING], ident[:], ACT.Copy, scale=coef[:, g % 4, j:j + 1]
                                       ).then_inc(sem("diag"), 1)
                    for hd in heads_at(g - R_PIECES, now):
                        gate(i, hd)
                    for hd in heads_at(g - R_PIECES, nxt):
                        gate(i + 1, hd)
                    if not nxt:
                        continue
                    for at, step in ((ACT_SQUARE, "square"), (ACT_ROOT, "root"), (ACT_F_T, "fT"), (ACT_Q, "q"),
                                     (ACT_Q_T, "qT"), (ACT_S, "s")):
                        if g == at:
                            prep(i + 1, step)
            tiles(act, body)

        @block.tensor
        def _(pe):
            def f_transposes(i):
                pe.wait_ge(sem("fn"), i + 1)
                for k in range(KC):
                    ins = pe.transpose(PB[:, k // 4, (k % 4) * P:(k % 4 + 1) * P], fn[:, k * P:(k + 1) * P], ident[:])
                ins.then_inc(sem("fT_ps"), 1)

            def queries(i, k):
                if k == 0:
                    pe.wait_ge(sem("fT"), i + 1)
                for b in range(2):
                    ins = pe.matmul(PB[:, 2 + b], fT[:, k], wq[:, k, b * HALF:(b + 1) * HALF], start=k == 0, stop=k == KC - 1)
                if k == KC - 1:
                    ins.then_inc(sem("q_ps"), 1)

            def q_transposes(i):
                pe.wait_ge(sem("q"), i + 1)
                for k in range(KC):
                    ins = pe.transpose(PB[:, k // 4, (k % 4) * P:(k % 4 + 1) * P], q[:, k * P:(k + 1) * P], ident[:])
                ins.then_inc(sem("qT_ps"), 1)

            def scores(i, part):
                if part == 0 and i is not first:
                    pe.wait_ge(sem("qT"), i + 1)
                for hd in range(4 * part, 4 * part + 4):
                    for half in range(2):
                        rng = slice(half * 64, half * 64 + 64)
                        ins = pe.matmul(PB[:, 2 * part + half, (hd % 4) * NK:(hd % 4 + 1) * NK], qT[rng, hd], keys[rng, hd],
                                        start=True, stop=True, skip_group_check=True)
                if part == 1:
                    ins.then_inc(sem("s_ps"), 1)
                elif i is first:
                    ins.then_inc(sem("first_s_ps"), 1)

            if layer == 0:
                pe.sem_inc(sem("slot_free"), RING)
            pe.wait_ge(S("ident_ready"), 1)
            f_transposes(first)
            pe.wait_ge(sem("wq"), 16 * (layer + 1))
            pe.wait_ge(sem("keys"), 16 * (layer + 1))
            pe.wait_ge(sem("fT"), first + 1)
            for part in range(2):
                for k in range(KC):
                    ins = pe.matmul(PB[:, 2 + part], fT[:, k], wq[:, k, part * HALF:(part + 1) * HALF], start=k == 0, stop=k == KC - 1)
                ins.then_inc(sem("q_ps" if part else "first_q_ps"), 1)
                if part:
                    pe.wait_ge(sem("q"), first + 1)
                else:
                    pe.wait_ge(sem("first_q"), layer + 1)
                for k in range(4):
                    ins = pe.transpose(PB[:, 2 * part, k * P:(k + 1) * P], q[:, part * HALF + k * P:part * HALF + (k + 1) * P], ident[:])
                ins.then_inc(sem("qT_ps" if part else "first_qT_ps"), 1)
                if part:
                    pe.wait_ge(sem("qT"), first + 1)
                else:
                    pe.wait_ge(sem("first_qT"), layer + 1)
                scores(first, part)

            def body(i, now, nxt):
                for g in range(PAIRS_T):
                    hd = g // PAIRS
                    if g % PAIRS == 0:
                        pe.wait_ge(sem("y_free"), i * NH + hd + 1)
                    for j in range(PAIR):
                        s = PAIR * g + j
                        pe.wait_ge(sem("diag"), i * TS + s + 1)
                        for b in range(2):
                            ins = pe.matmul(PY[:, hd % 2, b], diag[:, s % RING], ring[:, s % RING, D + b * HALF:D + (b + 1) * HALF],
                                            start=s % TOPK == 0, stop=s % TOPK == TOPK - 1)
                        ins.then_inc(sem("slot_free"), 1)
                    if not nxt:
                        continue
                    if g == PE_F_T:
                        f_transposes(i + 1)
                    if PE_Q <= g < PE_Q + KC:
                        queries(i + 1, g - PE_Q)
                    if g == PE_Q_T:
                        q_transposes(i + 1)
                    if PE_S <= g < PE_S + 2:
                        scores(i + 1, g - PE_S)
            tiles(pe, body)

        @block.vector
        def _(dve):
            def mean(i):
                dve.wait_ge(sem("square"), i + 1)
                dve.tensor_scalar(ss[:, 1:2], ss[:, 0:1], 1.0 / D, EPS, ALU.mult, ALU.add).then_inc(sem("mean"), 1)

            def modulate(i):
                dve.wait_ge(sem("root"), i + 1)
                dve.reciprocal(ss[:, 3:4], ss[:, 2:3]).then_inc(sem("rstd"), 1)
                dve.wait_ge(sem("rstd"), i + 1)
                dve.scalar_tensor_tensor(fn[:], h[:, i - shift], ss[:, 3:4], rows[:, row_kind(i), 1], ALU.mult, ALU.mult
                                         ).then_inc(sem("fn_scaled"), 1)
                dve.wait_ge(sem("fn_scaled"), i + 1)
                dve.tensor_tensor(fn[:], fn[:], rows[:, row_kind(i), 0], ALU.add).then_inc(sem("fn"), 1)

            def route(i, hd, piece):
                links = (0, 4, 8, 13)[piece]

                def link(ins):
                    nonlocal links
                    links += 1
                    ins.then_inc(sem("link"), 1)
                    wait_apart(dve, sem("link"), (i * NH + hd) * R_LINKS + links)

                def top16(out, where, values):
                    link(dve.max(out[:, 0:8], values))
                    dve.max_index(where[:, 0:8], out[:, 0:8], values).then_inc(sem("places"), 1)
                    link(dve.match_replace(values, out[:, 0:8], values, TAKEN))
                    link(dve.max(out[:, 8:16], values))
                    link(dve.max_index(where[:, 8:16], out[:, 8:16], values))

                if piece == 0 and i is first and hd < 4:
                    wait_apart(dve, sem("first_s"), layer + 1)
                elif piece == 0:
                    wait_apart(dve, sem("s"), i + 1)
                if piece < 2:
                    top16(top[:, piece], topi[:, piece], sc[:, hd // 4, piece, hd % 4])
                    return
                if piece == 2:
                    dve.tensor_copy(topf[:], topi[:]).then_inc(sem("places"), 1)
                    link(dve.tensor_tensor(cand[:], top[:, 0].rearrange("p (a b) -> p a b", b=1).broadcast_to([P, TOPK, TOPK]),
                                           top[:, 1].rearrange("p (a b) -> p a b", a=1).broadcast_to([P, TOPK, TOPK]), ALU.add))
                    top16(cs[:, hd], ci, cand[:].rearrange("p a b -> p (a b)"))
                    dve.tensor_scalar(negm[:, hd:hd + 1], cs[:, hd, 0:1], -1.0, None, ALU.mult).then_inc(sem("negm"), 1)
                    return
                dve.tensor_scalar(ab[:, 0], ci[:], 4, None, ALU.logical_shift_right).then_inc(sem("places"), 1)
                link(dve.tensor_scalar(ab[:, 1], ci[:], 15, None, ALU.bitwise_and))
                link(dve.tensor_copy(abf[:], ab[:]))
                link(dve.tensor_tensor(hot[:], abf[:].rearrange("p c (k o) -> p c k o", o=1).broadcast_to([P, 2, TOPK, TOPK]),
                                       iota[:].rearrange("p (a b m) -> p a b m", a=1, b=1).broadcast_to([P, 2, TOPK, TOPK]), ALU.is_equal))
                link(dve.tensor_tensor(hot[:], hot[:], topf[:].rearrange("p c (o m) -> p c o m", o=1).broadcast_to([P, 2, TOPK, TOPK]),
                                       ALU.mult))
                link(dve.tensor_reduce(e12[:], hot[:], AX.X, ALU.add))
                link(dve.scalar_tensor_tensor(ef[:], e12[:, 0], float(NK), e12[:, 1], ALU.mult, ALU.add))
                dve.tensor_scalar(idx[:, hd], ef[:], float(layer * EXPERTS), None, ALU.add).then_inc(sem("idx"), 1)
                dve.wait_ge(sem("idx"), i * NH + hd + 1)
                assert links == R_LINKS, links

            def denominator(i, hd):
                dve.wait_ge(sem("gexp"), i * NH + hd + 1)
                dve.reciprocal(grec[:, hd:hd + 1], gsum[:, hd:hd + 1]).then_inc(sem("grec"), 1)

            def coefficients(i, g):
                hd, at = g // PAIRS, PAIR * (g % PAIRS)
                dve.wait_ge(sem("gelu"), i * PAIRS_T + g + 1)
                if g % PAIRS == 0:
                    dve.wait_ge(sem("grec"), i * NH + hd + 1)
                dve.scalar_tensor_tensor(coef[:, g % 4], gel[:, g % 4], grec[:, hd:hd + 1], gexp[:, hd, at:at + PAIR],
                                         ALU.mult, ALU.mult).then_inc(sem("coef"), 1)

            def head_sum(i, hd):
                dve.wait_ge(sem("slot_free"), i * TS + RING + (hd + 1) * TOPK)
                ps = PY[:, hd % 2].rearrange("p b n -> p (b n)")
                if hd == 0:
                    dve.tensor_copy(y[:], ps).then_inc(sem("y_free"), 1)
                else:
                    dve.tensor_tensor(y[:], y[:], ps, ALU.add).then_inc(sem("y_free"), 1)

            if layer == 0:
                dve.sem_inc(sem("y_free"), 2)
            dve.wait_ge(sem("rows"), 16 * rows_loads)
            mean(first)
            modulate(first)
            dve.wait_ge(sem("iota"), layer + 1)
            for hd in range(LAG):
                for piece in range(R_PIECES):
                    route(first, hd, piece)
            for hd in range(LAG):
                denominator(first, hd)

            def body(i, now, nxt):
                dve.wait_ge(sem("fn"), i + 1)
                dve.tensor_copy(f[:], fn[:]).then_inc(sem("f"), 1)
                dve.wait_ge(sem("f"), i + 1)
                for g in range(PAIRS_T):
                    for j in range(PAIR):
                        s = PAIR * g + j
                        dve.wait_ge(sem(f"landed{s % RING}"), 16 * (i * (TS // RING) + s // RING + 1))
                        x = ring[:, s % RING, 0:D]
                        dve.tensor_tensor_reduce(x, x, f[:], 1.0, 0.0, ALU.mult, ALU.add, u[:, g % 4, j:j + 1]).then_inc(sem("dot"), 1)
                        if j == 0 and g:
                            coefficients(i, g - 1)
                    if g % PAIRS == 3 and g >= PAIRS:
                        dve.wait_ge(sem("y_free"), i * NH + g // PAIRS + 1)
                        head_sum(i, g // PAIRS - 1)
                    for ahead, table in ((0, now), (1, nxt)):
                        for piece in range(R_PIECES):
                            for hd in heads_at(g - piece, table):
                                route(i + ahead, hd, piece)
                        for hd in heads_at(g - R_PIECES - 2, table):
                            denominator(i + ahead, hd)
                    if not nxt:
                        continue
                    if g == DVE_MEAN:
                        mean(i + 1)
                    if g == DVE_MOD:
                        modulate(i + 1)
                coefficients(i, PAIRS_T - 1)
                dve.wait_ge(sem("y_free"), i * NH + NH + 1)
                head_sum(i, NH - 1)
                dve.wait_ge(sem("y_free"), i * NH + NH + 2)
                if i is first:
                    dve.wait_ge(sem("gates"), 16 * rows_loads)
                dve.tensor_tensor(y[:], y[:], rows[:, row_kind(i), 2], ALU.mult).then_inc(sem("gated"), 1)
                dve.wait_ge(sem("gated"), i + 1)
                dve.tensor_tensor(h[:, i - shift], h[:, i - shift], y[:], ALU.add).then_inc(sem("h"), 1)
                dve.wait_ge(sem("h"), i + 1)
            tiles(dve, body)


def final_stage(nc, S, A, h, out):
    with ExitStack() as ctx:
        gain = ctx.enter_context(nc.sbuf_tensor("fin_gain", [P, D], F32))
        o = ctx.enter_context(nc.sbuf_tensor("fin_o", [P, LT, D], F32))
        ss = ctx.enter_context(nc.sbuf_tensor("fin_ss", [P, 4, LT], F32))
        block = ctx.enter_context(nc.Block())

        @block.sync
        def _(sp):
            sp.dma_start(gain[:], A["final_norm_g"].rearrange("(a n) -> a n", a=1).broadcast_to([P, D])).then_inc(S("fin_gain"), 16)
            for t in range(LT):
                sp.wait_ge(S("fin_o"), t + 1)
                sp.dma_start(out[0].rearrange("(t p) d -> p t d", p=P)[:, t], o[:, t]).then_inc(S("stored"), 16)
            sp.wait_ge(S("stored"), 16 * LT)

        @block.scalar
        def _(act):
            for t in range(LT):
                act.activation(o[:, t], h[:, CT + t], ACT.Square, accum_out=ss[:, 0, t:t + 1]).then_inc(S("fin_sq"), 1)
            act.wait_ge(S("fin_stats"), 1)
            act.activation(ss[:, 2], ss[:, 1], ACT.Sqrt).then_inc(S("fin_root"), 1)

        @block.vector
        def _(dve):
            dve.wait_ge(S("fin_sq"), LT)
            dve.tensor_scalar(ss[:, 1], ss[:, 0], 1.0 / D, EPS, ALU.mult, ALU.add).then_inc(S("fin_stats"), 1)
            dve.wait_ge(S("fin_root"), 1)
            dve.reciprocal(ss[:, 3], ss[:, 2]).then_inc(S("fin_stats"), 1)
            dve.wait_ge(S("fin_stats"), 2)
            dve.wait_ge(S("fin_gain"), 16)
            for t in range(LT):
                dve.scalar_tensor_tensor(o[:, t], h[:, CT + t], ss[:, 3, t:t + 1], gain[:], ALU.mult, ALU.mult
                                         ).then_inc(S("fin_o"), 1)


def backbone(nc, A, out):
    with ExitStack() as ctx:
        S = Sems(nc, ctx)
        mod_d = nc.dram_tensor("mod_rows", (DEPTH, 2, 2, 3, D), F32).ap()
        h = ctx.enter_context(nc.sbuf_tensor("h", [P, NT, D], F32))
        ident = ctx.enter_context(nc.sbuf_tensor("ident", [P, P], F32))
        arena = ctx.enter_context(nc.sbuf_tensor("arena", [P, KC * D + NH * NK], F32))
        rows_flat = ctx.enter_context(nc.sbuf_tensor("mod_rows_sb", [P, 2 * 3 * D], F32))
        rows = rows_flat[:].rearrange("p (a b n) -> p a b n", a=2, b=3)
        with nc.sbuf_tensor("strips", [P, RET_HEADS, SL + SC], F32) as strips:
            modulation_stage(nc, S, A, h, ident, mod_d, strips, arena, rows_flat)
            mixer0_stage(nc, S, A, h, ident, mod_d, strips, arena, rows)
        peer_stage(nc, S, A, h, ident, mod_d, arena, rows, 0, 0, 0, NT)
        mixer1_stage(nc, S, A, h, ident, mod_d, arena, rows)
        peer_stage(nc, S, A, h, ident, mod_d, arena, rows, 1, CT, NT, LT)
        final_stage(nc, S, A, h, out)


def _rope_tables():
    n = HD // 4
    rows, cols = np.divmod(np.arange(SEQ), GRID_W)
    inv = (np.float32(ROPE_BASE) ** (-np.arange(n, dtype=np.float32) / np.float32(n))).astype(np.float32)
    ang = np.stack([rows.astype(np.float32)[:, None] * inv, cols.astype(np.float32)[:, None] * inv], axis=1)
    cos, sin = np.cos(ang), np.sin(ang)
    return (np.stack([cos, cos], axis=2).reshape(SEQ, HD).astype(np.float32),
            np.stack([-sin, sin], axis=2).reshape(SEQ, HD).astype(np.float32))


def _lay_out(inputs):
    a = {k: np.asarray(v) for k, v in inputs.items()}
    a["rope_cos"], a["rope_sin"] = _rope_tables()
    a["gains"] = np.stack([a.pop("mix_norm_g"), a.pop("ffn_norm_g")], axis=1).reshape(DEPTH, 2 * D)
    a["conv_wT"] = a.pop("conv_w")[0].T
    keys = np.concatenate([a.pop("peer_keys1"), a.pop("peer_keys2")], axis=-1)
    a["keysT"] = keys.transpose(0, 3, 1, 2)
    a["uv"] = np.concatenate([a.pop("peer_u"), a.pop("peer_v")], axis=-1).reshape(DEPTH * EXPERTS, 2 * D)
    return {k: np.ascontiguousarray(v) for k, v in a.items()}


def kernel(**inputs):
    import concourse.bacc as _bacc
    from concourse.bass_utils import run_bass_kernel_spmd as _run

    nc = _bacc.Bacc("TRN2", target_bir_lowering=False, num_devices=1)
    arrays, args = {}, {}
    for name, a in _lay_out(inputs).items():
        arrays[f"in_{name}_dram"] = a
        args[name] = nc.dram_tensor(f"in_{name}_dram", a.shape, mybir.dt.from_np(a.dtype), kind="ExternalInput").ap()
    out = nc.dram_tensor("out_0_dram", (1, SEQ, D), F32, kind="ExternalOutput").ap()
    backbone(nc, args, out)
    r = _run(nc, [arrays], core_ids=[0])
    return r.results[0]["out_0_dram"]
```

```python
from contextlib import ExitStack

import numpy as np

import concourse.bass as bass
from concourse import mybir

ALU = mybir.AluOpType
ACT = mybir.ActivationFunctionType
AX = mybir.AxisListType
F32 = mybir.dt.float32
U32 = mybir.dt.uint32
F32R = mybir.dt.float32r

P = 128
D = 1024
KC = D // P
CTX, SEQ = 256, 512
CT, LT = CTX // P, SEQ // P
NT = CT + LT
TOK = CTX + SEQ
DEPTH = 2
EPS = 1e-6
HALF = 512
RET_HEADS, RET_V = 4, 128
HD = 64
ATT_HEADS, KV_HEADS = 16, 4
SCALE = HD ** -0.5
GRID_W, ROPE_BASE = 64, 10000.0
NEG = -1e30
NH, NK, TOPK = 8, 128, 16
EXPERTS = NK * NK
RING = 8
PAIR = 2
PAIRS = TOPK // PAIR
LAG = 2
TAKEN = -3.0e38


def kind(t):
    return int(t >= CT)


class Sems:

    def __init__(self, nc, ctx):
        self.nc, self.ctx, self.made = nc, ctx, {}

    def __call__(self, name):
        if name not in self.made:
            self.made[name] = self.ctx.enter_context(self.nc.semaphore(name))
        return self.made[name]


class Arena:

    def __init__(self, tensor):
        self.flat, self.at = tensor, 0

    def cut(self, *shape):
        size = int(np.prod(shape))
        assert self.at + size <= self.flat.shape[1], (self.at, size)
        part = self.flat[:, self.at:self.at + size]
        self.at += size
        if len(shape) == 1:
            return part
        names = "abcd"[:len(shape)]
        sizes = dict(zip(names[1:], shape[1:]))
        return part.rearrange(f"p ({' '.join(names)}) -> p {' '.join(names)}", **sizes)


def modulation_stage(nc, S, A, h, ident, mod_d, strips_d, arena, rows):
    n_chunk, ring = DEPTH * 12, 3
    with ExitStack() as ctx:
        def sb(name, shape, dt=F32):
            return ctx.enter_context(nc.sbuf_tensor(name, shape, dt))
        crow = sb("crow", [P, 2, KC])
        silu = sb("silu", [P, 2, KC])
        bufs, spare = Arena(arena[:]), Arena(rows[:])
        ada = [bufs.cut(KC, HALF), bufs.cut(KC, HALF), spare.cut(KC, HALF)]
        bias = sb("ada_bias", [2, DEPTH * 6 * D])
        gain = sb("norm_gain", [2, DEPTH * 2 * D])
        row = sb("mod_row", [2, 4, HALF])
        tmp = sb("mod_tmp", [2, 2, HALF])
        strips = sb("strips", [P, RET_HEADS, SL + SC])
        lg = sb("decay_log", [P, 5, 2 * RET_HEADS])
        dist = sb("distance", [P, 3, SL])
        cdist = sb("ctx_distance", [P, 2, SC])
        dec = sb("decays", [P, 2, SL])
        ps = ctx.enter_context(nc.psum_tensor("mod_ps", [2, 4, HALF], F32))
        block = ctx.enter_context(nc.Block())

        def chunk(n):
            layer, c = divmod(n, 12)
            return layer, c // 6, (c % 6) // 2, c % 2

        @block.sync
        def _(sp):
            sp.dma_start(crow[:, 0, :], A["c_ctx"].rearrange("(p k) -> p k", p=P)).then_inc(S("c_loaded"), 16)
            sp.dma_start(crow[:, 1, :], A["c"].rearrange("a (p k) -> p (a k)", p=P)).then_inc(S("c_loaded"), 16)
            sp.dma_start(lg[:, 0, 0:RET_HEADS], A["ret_decay_logit_f"].broadcast_to([P, RET_HEADS])).then_inc(S("logits"), 16)
            sp.dma_start(lg[:, 0, RET_HEADS:], A["ret_decay_logit_b"].broadcast_to([P, RET_HEADS])).then_inc(S("logits"), 16)
            sp.dma_start(bias[:], A["ada_b"].rearrange("(a l) n -> a (l n)", a=1).broadcast_to([2, DEPTH * 6 * D])
                         ).then_inc(S("rows_loaded"), 16)
            sp.dma_start(gain[:], A["gains"].rearrange("(a l) n -> a (l n)", a=1).broadcast_to([2, DEPTH * 2 * D])
                         ).then_inc(S("rows_loaded"), 16)
            for n in range(n_chunk):
                layer, half, sec, ch = chunk(n)
                if n >= ring:
                    sp.wait_ge(S("mod_mm"), n - ring + 1)
                col = ((half * 3 + sec) * 2 + ch) * HALF
                sp.dma_start(ada[n % ring], A["ada_w"][layer].rearrange("(p k) n -> p k n", p=P)[:, :, col:col + HALF]
                             ).then_inc(S(f"ada_loaded{n % ring}"), 16)
                if n == 4:
                    sp.dma_start(h[:, 0:CT], A["ctx"][0].rearrange("(t p) d -> p t d", p=P)).then_inc(S("h_loaded"), 16)
                    sp.dma_start(h[:, CT:NT], A["x"][0].rearrange("(t p) d -> p t d", p=P)).then_inc(S("h_loaded"), 16)
            sp.wait_ge(S("h_loaded"), 32)
            sp.wait_ge(S("strip"), 2 * RET_HEADS)
            sp.dma_start(strips_d, strips[:]).then_inc(S("strips_stored"), 16)
            sp.wait_ge(S("strips_stored"), 16)

        @block.gpsimd
        def _(pool):
            pool.memset(ident[:], 0.0).then_inc(S("ident"), 1)
            pool.wait_ge(S("ident"), 1)
            pool.affine_select(out=ident[:], in_=ident[:], compare_op=ALU.not_equal, fill=1.0, base=0,
                               pattern=[[-1, P]], channel_multiplier=1).then_inc(S("ident"), 1)
            few = dict(allow_small_or_imprecise_dtypes=True)
            pool.iota(dist[:, 0], [[1, SL]], base=-3 * P, channel_multiplier=-1, **few).then_inc(S("distances"), 1)
            pool.iota(cdist[:, 0], [[1, SC]], base=CTX - P, channel_multiplier=-1, **few).then_inc(S("distances"), 1)
            pool.iota(cdist[:, 1], [[-1, SC]], base=SEQ + P, channel_multiplier=1, **few).then_inc(S("distances"), 1)

        @block.scalar
        def _(act):
            act.wait_ge(S("c_loaded"), 32)
            act.activation(silu[:], crow[:], ACT.Silu).then_inc(S("silu_ready"), 1)
            act.wait_ge(S("logits_abs"), 1)
            act.activation(lg[:, 2], lg[:, 1], ACT.Exp, scale=-1.0).then_inc(S("logits_log"), 1)
            act.wait_ge(S("logits_log"), 1)
            act.activation(lg[:, 3], lg[:, 2], ACT.Ln, bias=1.0).then_inc(S("logits_log"), 1)
            act.wait_ge(S("log_gamma"), 1)
            act.wait_ge(S("distances"), 3)
            for m in range(2 * RET_HEADS):
                hd, cross = m // 2, m % 2
                for way in range(2):
                    if m:
                        act.wait_ge(S("strip"), m)
                    src = cdist[:, way] if cross else dist[:, 1 + way]
                    dst = dec[:, way, 0:SC] if cross else dec[:, way]
                    act.activation(dst, src, ACT.Exp, scale=lg[:, 4, way * RET_HEADS + hd:way * RET_HEADS + hd + 1]
                                   ).then_inc(S("decay"), 1)
            for n in range(n_chunk):
                layer, half, sec, ch = chunk(n)
                act.wait_ge(S("mod_row"), n + 1)
                act.dma_start(mod_d[layer, half, :, sec, ch * HALF:(ch + 1) * HALF], row[:, n % 4]
                              ).then_inc(S(f"mod_stored{n % 4}"), 16)
            for b in range(4):
                act.wait_ge(S(f"mod_stored{b}"), 16 * (n_chunk // 4))

        @block.tensor
        def _(pe):
            pe.wait_ge(S("silu_ready"), 1)
            for n in range(n_chunk):
                pe.wait_ge(S(f"ada_loaded{n % ring}"), 16 * (n // ring + 1))
                if n >= 4:
                    pe.wait_ge(S("mod_row"), n - 3)
                for k in range(KC):
                    ins = pe.matmul(ps[:, n % 4], silu[:, :, k], ada[n % ring][:, k], start=k == 0, stop=k == KC - 1)
                ins.then_inc(S("mod_mm"), 1)

        @block.vector
        def _(dve):
            dve.wait_ge(S("logits"), 32)
            dve.scalar_tensor_tensor(lg[:, 1], lg[:, 0], -1.0, lg[:, 0], ALU.mult, ALU.max).then_inc(S("logits_abs"), 1)
            dve.wait_ge(S("distances"), 3)
            dve.tensor_scalar(dist[:, 1], dist[:, 0], 0.0, None, ALU.max).then_inc(S("clamped"), 1)
            dve.tensor_scalar(dist[:, 2], dist[:, 0], -1.0, 0.0, ALU.mult, ALU.max).then_inc(S("clamped"), 1)
            dve.wait_ge(S("clamped"), 2)
            dve.wait_ge(S("logits_log"), 2)
            dve.scalar_tensor_tensor(lg[:, 4], lg[:, 0], 0.0, lg[:, 3], ALU.min, ALU.subtract).then_inc(S("log_gamma"), 1)
            for m in range(2 * RET_HEADS):
                hd, cross = m // 2, m % 2
                dve.wait_ge(S("decay"), 2 * (m + 1))
                if cross:
                    dve.tensor_tensor(strips[:, hd, SL:SL + SC], dec[:, 0, 0:SC], dec[:, 1, 0:SC], ALU.add).then_inc(S("strip"), 1)
                    continue
                for way, op in enumerate((ALU.is_ge, ALU.is_le)):
                    dve.scalar_tensor_tensor(dec[:, way], dist[:, 0], 0.0, dec[:, way], op, ALU.mult).then_inc(S("masked"), 1)
                dve.wait_ge(S("masked"), m + 2)
                dve.tensor_tensor(strips[:, hd, 0:SL], dec[:, 0], dec[:, 1], ALU.add).then_inc(S("strip"), 1)
            dve.wait_ge(S("rows_loaded"), 32)
            scaled = 0
            for n in range(n_chunk):
                layer, half, sec, ch = chunk(n)
                dve.wait_ge(S("mod_mm"), n + 1)
                if n >= 4:
                    dve.wait_ge(S(f"mod_stored{n % 4}"), 16 * (n // 4))
                b = bias[:, (layer * 12 + n % 12) * HALF:(layer * 12 + n % 12 + 1) * HALF]
                if sec != 1:
                    dve.tensor_tensor(row[:, n % 4], ps[:, n % 4], b, ALU.add).then_inc(S("mod_row"), 1)
                    continue
                g = gain[:, ((layer * 2 + half) * 2 + ch) * HALF:((layer * 2 + half) * 2 + ch + 1) * HALF]
                dve.tensor_tensor(tmp[:, ch], ps[:, n % 4], b, ALU.add).then_inc(S("mod_scale"), 1)
                scaled += 1
                dve.wait_ge(S("mod_scale"), scaled)
                dve.scalar_tensor_tensor(row[:, n % 4], tmp[:, ch], 1.0, g, ALU.add, ALU.mult).then_inc(S("mod_row"), 1)


def norm_squares(act, S, tag, h, junk, ss):
    for t in range(NT):
        act.activation(junk, h[:, t], ACT.Square, accum_out=ss[:, 0, t:t + 1]).then_inc(S(tag + "_squares"), 1)
        act.wait_ge(S(tag + "_squares"), t + 1)
    act.wait_ge(S(tag + "_stats"), 1)
    act.activation(ss[:, 2], ss[:, 1], ACT.Sqrt).then_inc(S(tag + "_squares"), 1)


def norm_modulate(dve, S, tag, h, a, ss, rows, PS, pairs, aTh, aTl, wh, wl):
    dve.wait_ge(S(tag + "_squares"), NT)
    dve.tensor_scalar(ss[:, 1], ss[:, 0], 1.0 / D, EPS, ALU.mult, ALU.add).then_inc(S(tag + "_stats"), 1)
    dve.wait_ge(S(tag + "_squares"), NT + 1)
    dve.reciprocal(ss[:, 3], ss[:, 2]).then_inc(S(tag + "_stats"), 1)
    dve.wait_ge(S(tag + "_stats"), 2)
    dve.wait_ge(S(tag + "_rows"), 32)
    for t in range(NT + 2):
        if t < NT:
            if t >= 2:
                dve.wait_ge(S(tag + "_aT_ps"), t - 1)
            dve.scalar_tensor_tensor(a[:, t % 2], h[:, t], ss[:, 3, t:t + 1], rows[:, kind(t), 1], ALU.mult, ALU.mult)\
                .then_inc(S(tag + "_scaled"), 1)
        if t >= 2:
            dve.wait_ge(S(tag + "_aT_high"), t - 1)
            tile = slice((t - 2) * P, (t - 1) * P)
            dve.tensor_tensor(aTl[:, :, tile], norm_banks(PS, pairs[t - 2]), aTh[:, :, tile].bitcast(F32), ALU.subtract
                              ).then_inc(S(tag + "_aT"), 1)
        if t == 2:
            split_low(dve, S, tag, wh, wl, 0)
    split_low(dve, S, tag, wh, wl, 1)


def norm_shift(pool, S, tag, a, rows):
    pool.wait_ge(S(tag + "_rows"), 32)
    for t in range(NT):
        pool.wait_ge(S(tag + "_scaled"), t + 1)
        pool.tensor_tensor(a[:, t % 2], a[:, t % 2], rows[:, kind(t), 0], ALU.add).then_inc(S(tag + "_a"), 1)


def norm_banks(PS, at):
    return PS[:, at:at + 2].rearrange("p b (k n) -> p (b k) n", k=4)


def norm_transpose(pe, S, tag, PS, pairs, a, ident, after):
    pe.wait_ge(S("ident"), 2)
    for t in range(NT + 2):
        if t < NT:
            last = max([x for x in range(t) if pairs[x] == pairs[t]], default=-1)
            if last >= 0:
                pe.wait_ge(S(tag + "_aT"), last + 1)
            pe.wait_ge(S(tag + "_a"), t + 1)
            for k in range(KC):
                ins = pe.transpose(norm_banks(PS, pairs[t])[:, k], a[:, t % 2, k * P:(k + 1) * P], ident[:])
            ins.then_inc(S(tag + "_aT_ps"), 1)
        if t >= 2:
            pe.wait_ge(S(tag + "_aT"), t - 1)
            after(t - 2)


def norm_evacuate(act, S, tag, PS, pairs, aTh, wh, wl):
    for t in range(NT):
        act.wait_ge(S(tag + "_aT_ps"), t + 1)
        act.activation(aTh[:, :, t * P:(t + 1) * P], norm_banks(PS, pairs[t]), ACT.Copy).then_inc(S(tag + "_aT_high"), 1)
        if t == 0:
            split_high(act, S, tag, wh, wl, 0)
    split_high(act, S, tag, wh, wl, 1)


KH = KC // 2


def twins(nc, ctx, name, shape):
    with nc.sbuf_tensor(name + "_plain", shape, F32) as plain:
        pass
    return plain, ctx.enter_context(nc.sbuf_tensor(name, shape, F32R))


def load_half(sp, S, tag, wl, src, j, cols):
    sp.dma_start(wl[0][:, j % 2], src.rearrange("(k p) n -> p k n", p=P)[:, (j % 2) * KH:(j % 2 + 1) * KH, cols]
                 ).then_inc(S(f"{tag}_w{j % 2}"), 16)


def split_high(act, S, tag, wh, wl, j):
    act.wait_ge(S(f"{tag}_w{j % 2}"), 16 * (j // 2 + 1))
    act.activation(wh[:, j % 2], wl[0][:, j % 2], ACT.Copy).then_inc(S(tag + "_w_high"), 1)


def split_low(dve, S, tag, wh, wl, j):
    dve.wait_ge(S(tag + "_w_high"), j + 1)
    dve.tensor_tensor(wl[1][:, j % 2], wl[0][:, j % 2], wh[:, j % 2].bitcast(F32), ALU.subtract).then_inc(S(tag + "_w_low"), 1)


def product(pe, out, x, y, j):
    for kl in range(KH):
        (xh, xl), (yh, yl) = x(kl), y(kl)
        for m, (l, r) in enumerate(((xh, yh), (xl, yh), (xh, yl))):
            ins = pe.matmul(out, l, r, start=j % 2 == 0 and kl == 0 and m == 0, stop=j % 2 == 1 and kl == KH - 1 and m == 2)
    return ins


def residual(dve, S, tag, h, PS, rows, tmp, tiles, bank, between):
    for n in range(2 * len(tiles)):
        if n == len(tiles):
            between()
        c, t = n // len(tiles), tiles[n % len(tiles)]
        dve.wait_ge(S(tag + "_out"), n + 1)
        if n >= 2:
            dve.wait_ge(S(tag + "_added"), n - 1)
        cols = slice(c * HALF, (c + 1) * HALF)
        dve.tensor_tensor(tmp[:, n % 2], PS[:, bank(n)], rows[:, kind(t), 2, cols], ALU.mult).then_inc(S(tag + "_out_read"), 1)
        dve.wait_ge(S(tag + "_out_read"), n + 1)
        dve.tensor_tensor(h[:, t, cols], h[:, t, cols], tmp[:, n % 2], ALU.add).then_inc(S(tag + "_added"), 1)


def rope(dve, S, tag, n, outs, ps, t1, t2, cos, sin, heads):
    w = heads * HD

    def halves(x):
        return x.rearrange("p (g a n) -> p g a n", g=2 * heads, a=2)

    def by_head(x):
        return x.rearrange("p (h n) -> p h n", h=heads)

    if n:
        dve.wait_ge(S(tag + "_rope_out"), n)
    dve.tensor_tensor(by_head(t1[:, 0:w]), by_head(ps), cos.rearrange("p (o n) -> p o n", o=1).broadcast_to([P, heads, HD]),
                      ALU.mult).then_inc(S(tag + "_rope"), 1)
    for a in range(2):
        table = sin.rearrange("p (x a n) -> p x a n", x=2, a=2)[:, :, a]
        for x in range(2):
            o = t2[:, 0:w].rearrange("p (h x a n) -> p h x a n", h=heads, x=2, a=2)[:, :, x, a]
            u = ps.rearrange("p (h x a n) -> p h x a n", h=heads, x=2, a=2)[:, :, x, 1 - a]
            s = table[:, x].rearrange("p (o n) -> p o n", o=1).broadcast_to([P, heads, 16])
            dve.tensor_tensor(o, u, s, ALU.mult).then_inc(S(tag + "_rope"), 1)
    dve.wait_ge(S(tag + "_rope"), 5 * (n + 1))
    for m, o in enumerate(outs):
        ins = dve.tensor_tensor(o, by_head(t1[:, 0:w]), by_head(t2[:, 0:w]), ALU.add)
    return ins.then_inc(S(tag + "_rope_out"), 1)


def load_rows(sp, S, mod_d, rows, layer, half, name, kinds=(0, 1), parts=slice(0, 3)):
    for kd in kinds:
        sp.dma_start(rows[:, kd, parts], mod_d[layer, half, kd, parts].rearrange("(o s) d -> o s d", o=1)
                     .broadcast_to([P, parts.stop - parts.start, D])).then_inc(S(name), 16)


def peer_kinds(layer):
    return (0, 1) if layer < DEPTH - 1 else (1,)


def peer_buffers(arena):
    cuts = Arena(arena[:])
    return cuts.cut(KC, D), cuts.cut(NH, NK)


def load_ahead_for_peer(sp, S, A, mod_d, arena, layer):
    wq, keys = peer_buffers(arena)
    sp.dma_start(wq, A["peer_wq"][layer].rearrange("(k p) n -> p k n", p=P)).then_inc(S("peer_wq"), 16)
    sp.dma_start(keys, A["keysT"][layer]).then_inc(S("peer_keys"), 16)


SL = 3 * P + SEQ
SC = P + SEQ


def mixer0_stage(nc, S, A, h, ident, mod_d, strips_d, arena, rows):
    n_in = 6
    with ExitStack() as ctx:
        def sb(name, shape, dt=F32):
            return ctx.enter_context(nc.sbuf_tensor("m0_" + name, shape, dt))
        plain_high, aTh = twins(nc, ctx, "m0_aT_high", [P, KC, TOK])
        plain_low, aTl = twins(nc, ctx, "m0_aT_low", [P, KC, TOK])
        wh = sb("w_high", [P, 2, KH, HALF], F32R)
        wl = twins(nc, ctx, "m0_w_low", [P, 2, KH, HALF])
        v, v_low = twins(nc, ctx, "m0_v", [P, NT, HALF])
        sg = sb("sg", [P, NT, HALF])
        cuts = Arena(arena[:])
        qT = cuts.cut(2, TOK)
        kT = cuts.cut(2, TOK)
        gb = cuts.cut(4, TOK)
        u = cuts.cut(4, TOK)
        cos = sb("cos", [P, LT, HD])
        sin = sb("sin", [P, LT, HD])
        cw = sb("cw", [P, 4, 3])
        tapped = sb("tapped", [P, TOK])
        ss = sb("ss", [P, 4, NT])
        hs = sb("hs", [P, 4, 2 * RET_HEADS, LT])
        a = sb("a", [P, 2, D])
        sq = sb("sq", [P, D])
        PS = ctx.enter_context(nc.psum_tensor("m0_ps", [P, 8, HALF], F32))
        block = ctx.enter_context(nc.Block())
        PT = a[:].rearrange("p a (b n) -> p (a b) n", b=2)
        strips = plain_high[:].rearrange("p k n -> p (k n)").rearrange("p (h n) -> p h n", h=RET_HEADS)
        yr = plain_low[:, 0:4].rearrange("p k n -> p (k n)").rearrange("p (t n) -> p t n", t=NT)
        yc = plain_low[:, 4:8]
        yrTl = v_low[:].rearrange("p t n -> p (t n)").rearrange("p (k n) -> p k n", k=4)
        T = "m0"
        n_tok, n_ch = 3 * NT, 8
        norm_pairs = (6, 4, 6, 4, 6, 6)
        yT_bank = (0, 1, 2, 3, 6, 7)

        items = []
        for hd in range(RET_HEADS):
            items += [(hd, 0, j) for j in range(CT)] + [(hd, 1, j) for j in range(NT)]

        @block.sync
        def _(sp):
            def load_peer():
                sp.wait_ge(S("m0_a"), NT)
                load_rows(sp, S, mod_d, rows, 0, 1, "peer_rows", parts=slice(0, 2))
                sp.wait_ge(S("m0_conv_out"), 4)
                sp.wait_ge(S("m0_S"), len(items))
                load_ahead_for_peer(sp, S, A, mod_d, arena, 0)

            load_rows(sp, S, mod_d, rows, 0, 0, "m0_rows", parts=slice(0, 2))
            for j in range(2 * (n_in + 2)):
                if j >= 2:
                    c = (j - 2) // 2
                    if j % 2 == 0:
                        sp.wait_ge(S("m0_w_used"), c + 1)
                    elif c < n_in:
                        sp.wait_ge(S("m0_proj"), NT * (c + 1) if c < 3 else n_tok + n_ch * (c - 2))
                    else:
                        sp.wait_ge(S("m0_out"), NT)
                if j == 2 * n_in + 1:
                    sp.dma_start(strips[:, 0], strips_d[:, 0]).then_inc(S("m0_strip0"), 16)
                    sp.dma_start(strips[:, 1:], strips_d[:, 1:]).then_inc(S("m0_strips"), 16)
                n = j // 2
                src = A["ev_w_in"][0] if n < n_in else A["ev_w_out"][0]
                c = (n if n < n_in else n - n_in) * HALF
                load_half(sp, S, T, wl, src, j, slice(c, c + HALF))
                if j == 1:
                    sp.dma_start(cos[:], A["rope_cos"].rearrange("(t p) n -> p t n", p=P)).then_inc(S("m0_tabs"), 16)
                    sp.dma_start(sin[:], A["rope_sin"].rearrange("(t p) n -> p t n", p=P)).then_inc(S("m0_tabs"), 16)
                    sp.dma_start(cw[:], A["conv_wT"].rearrange("(m p) i -> p m i", p=P)).then_inc(S("m0_tabs"), 16)
                    load_rows(sp, S, mod_d, rows, 0, 0, "m0_tabs", parts=slice(2, 3))
            load_peer()

        @block.gpsimd
        def _(pool):
            norm_shift(pool, S, T, a, rows)
            pool.wait_ge(S("m0_tabs"), 80)
            pool.wait_ge(S("m0_u"), n_ch)
            pool.wait_ge(S("m0_ev"), 2 * NT + 2 * n_ch)
            pool.wait_ge(S("m0_proj"), n_tok + 3 * n_ch)
            links = 0
            for m in range(4):
                y = yc[:, m]
                pool.tensor_scalar(y, u[:, m], cw[:, m, 1:2], None, ALU.mult).then_inc(S("m0_conv"), 1)
                links += 1
                for tap, out, src in ((0, slice(1, 0), slice(0, -1)), (2, slice(0, -1), slice(1, 0))):
                    pool.wait_ge(S("m0_conv"), links)
                    pool.tensor_scalar(tapped[:], u[:, m], cw[:, m, tap:tap + 1], None, ALU.mult).then_inc(S("m0_conv"), 1)
                    links += 1
                    pool.wait_ge(S("m0_conv"), links)
                    for lo, hi in ((0, CTX), (CTX, TOK)):
                        y_at, u_at = y[:, lo + out.start:hi + out.stop], tapped[:, lo + src.start:hi + src.stop]
                        pool.tensor_tensor(y_at, y_at, u_at, ALU.add).then_inc(S("m0_conv"), 1)
                    links += 2
                pool.wait_ge(S("m0_conv"), links)
                pool.tensor_tensor(y, y, gb[:, m], ALU.mult).then_inc(S("m0_conv_out"), 1)

        @block.scalar
        def _(act):
            norm_squares(act, S, T, h, sq[:], ss)
            norm_evacuate(act, S, T, PS, norm_pairs, aTh, wh, wl)
            split_high(act, S, T, wh, wl, 2)
            split_high(act, S, T, wh, wl, 3)
            for n in range(NT, n_tok):
                c, t = divmod(n, NT)
                if t == 0:
                    split_high(act, S, T, wh, wl, 2 * c + 2)
                act.wait_ge(S("m0_proj"), n + 1)
                dst = v if c == 1 else sg
                act.activation(dst[:, t], PS[:, n % 8], ACT.Copy if c == 1 else ACT.Silu).then_inc(S("m0_ev"), 1)
                if n == 2 * NT - 1:
                    for t in range(NT):
                        act.wait_ge(S("m0_qkT_ps"), t + 1)
                        blk = PS[:, 4 + t % 2].rearrange("p (b n) -> p b n", b=4)
                        act.activation(qT[:, :, t * P:(t + 1) * P], blk[:, 0:2], ACT.Copy).then_inc(S("m0_qT"), 1)
                        act.activation(kT[:, :, t * P:(t + 1) * P], blk[:, 2:4], ACT.Copy, scale=SCALE).then_inc(S("m0_qT"), 1)
                if n % NT == NT - 1:
                    split_high(act, S, T, wh, wl, 2 * c + 3)
            for i in range(2 * n_ch):
                n = n_tok + i
                m, th = divmod(i % n_ch, 2)
                if i % n_ch == 0:
                    split_high(act, S, T, wh, wl, 2 * (3 + i // n_ch) + 2)
                act.wait_ge(S("m0_proj"), n + 1)
                act.activation((gb if i < n_ch else u)[:, m, th * 3 * P:(th + 1) * 3 * P], PS[:, n % 8, 0:3 * P], ACT.Copy
                               ).then_inc(S("m0_ev"), 1)
                if i % n_ch == n_ch - 1:
                    split_high(act, S, T, wh, wl, 2 * (3 + i // n_ch) + 3)
            split_high(act, S, T, wh, wl, 2 * n_in)
            for g in range(2 * RET_HEADS):
                if g == 1:
                    split_high(act, S, T, wh, wl, 2 * n_in + 1)
                nt = LT if g % 2 else CT
                act.wait_ge(S("m0_pv"), g // 2 * (CT + NT) + (CT + NT if g % 2 else CT))
                if g:
                    act.wait_ge(S("m0_ret_ss"), 2 * g)
                act.activation(sq[:, 0:nt * P], PS[:, 4 + g % 2, 0:nt * P], ACT.Square).then_inc(S("m0_ret_sq"), 1)
                act.wait_ge(S("m0_ret_ss"), 2 * g + 2)
                act.activation(hs[:, 2, g, 0:nt], hs[:, 1, g, 0:nt], ACT.Sqrt).then_inc(S("m0_ret_sq"), 1)
            for t in range(NT):
                act.wait_ge(S("m0_yT_ps"), t + 1)
                act.activation(aTh[:, 0:4, t * P:(t + 1) * P], PS[:, yT_bank[t]].rearrange("p (b n) -> p b n", b=4), ACT.Copy
                               ).then_inc(S("m0_yT_high"), 1)
            act.wait_ge(S("m0_conv_out"), 4)
            act.activation(aTh[:, 4:8], yc, ACT.Copy).then_inc(S("m0_yT_high"), 1)
            for j in (2 * n_in + 2, 2 * n_in + 3):
                split_high(act, S, T, wh, wl, j)

        @block.tensor
        def _(pe):
            def bank_free(n):
                if n < NT:
                    pe.wait_ge(S("m0_qk"), n + 1)
                elif n < n_tok + 2 * n_ch:
                    pe.wait_ge(S("m0_ev"), n - NT + 1)
                else:
                    pe.wait_ge(S("m0_u"), n - n_tok - 2 * n_ch + 1)

            def unit(j, n):
                def a_rows(kl, cols):
                    k = (j % 2) * KH + kl
                    return aTh[:, k, cols], aTl[:, k, cols]

                def w_rows(kl, cols):
                    return wh[:, j % 2, kl, cols], wl[1][:, j % 2, kl, cols]

                if n < n_tok:
                    t = n % NT
                    return product(pe, PS[:, n % 8], lambda kl: a_rows(kl, slice(t * P, (t + 1) * P)),
                                   lambda kl: w_rows(kl, slice(0, HALF)), j)
                m, th = divmod((n - n_tok) % n_ch, 2)
                return product(pe, PS[:, n % 8, 0:3 * P], lambda kl: w_rows(kl, slice(m * P, (m + 1) * P)),
                               lambda kl: a_rows(kl, slice(th * 3 * P, (th + 1) * 3 * P)), j)

            def first_unit(t):
                if t == 0:
                    pe.wait_ge(S("m0_w_low"), 1)
                ins = unit(0, t)
                if t == NT - 1:
                    ins.then_inc(S("m0_w_used"), 1)

            norm_transpose(pe, S, T, PS, norm_pairs, a, ident, first_unit)
            for c in range(n_in):
                units = range(NT * c, NT * (c + 1)) if c < 3 else range(n_tok + n_ch * (c - 3), n_tok + n_ch * (c - 2))
                for j in (2 * c, 2 * c + 1):
                    if j == 0:
                        continue
                    pe.wait_ge(S("m0_w_low"), j + 1)
                    if c == 2 and j % 2 == 0:
                        pe.wait_ge(S("m0_qT"), 2 * NT)
                    for n in units:
                        if n >= 8 and j % 2 == 0:
                            bank_free(n - 8)
                        ins = unit(j, n)
                        if j % 2 == 1:
                            ins.then_inc(S("m0_proj"), 1)
                        elif n == units[-1]:
                            ins.then_inc(S("m0_w_used"), 1)
                if c == 1:
                    for t in range(NT):
                        pe.wait_ge(S("m0_qk"), NT)
                        if t >= 2:
                            pe.wait_ge(S("m0_qT"), 2 * (t - 1))
                        for m in range(4):
                            ins = pe.transpose(PS[:, 4 + t % 2, m * P:(m + 1) * P], sg[:, t, m * P:(m + 1) * P], ident[:])
                        ins.then_inc(S("m0_qkT_ps"), 1)
            n = n_tok + 3 * n_ch
            for m in range(n - 8, n):
                bank_free(m)
            pe.wait_ge(S("m0_qT"), 2 * NT)

            def scores(i):
                hd, kd, j = items[i]
                p0 = (hd % 2) * HD
                if i >= 2:
                    pe.wait_ge(S("m0_P"), i - 1)
                lo, hi = (CTX, TOK) if kd else (0, CTX)
                pe.matmul(PS[:, 2 + i % 2, 0:hi - lo], kT[p0:p0 + HD, hd // 2, j * P:(j + 1) * P],
                          qT[p0:p0 + HD, hd // 2, lo:hi], start=True, stop=True).then_inc(S("m0_S"), 1)

            def values(i):
                hd, kd, j = items[i]
                nt, last = (LT, NT - 1) if kd else (CT, CT - 1)
                pe.wait_ge(S("m0_P"), i + 1)
                if j == 0 and hd >= 1:
                    pe.wait_ge(S("m0_ret_y"), 2 * (hd - 1) + kd + 1)
                for it in range(nt):
                    ins = pe.matmul(PS[:, 4 + kd, it * P:(it + 1) * P], PT[:, i % 4, it * P:(it + 1) * P],
                                    v[:, j, hd * RET_V:(hd + 1) * RET_V], start=j == 0 and it == 0, stop=j == last,
                                    skip_group_check=True)
                ins.then_inc(S("m0_pv"), 1)

            for i in range(len(items)):
                scores(i)
                if i >= 1:
                    values(i - 1)
            values(len(items) - 1)
            pe.wait_ge(S("m0_ret_y"), 2 * RET_HEADS)
            for t in range(NT):
                for m in range(4):
                    ins = pe.transpose(PS[:, yT_bank[t], m * P:(m + 1) * P], yr[:, t, m * P:(m + 1) * P], ident[:])
                ins.then_inc(S("m0_yT_ps"), 1)
            pe.wait_ge(S("m0_yT"), NT)
            for j in range(4):
                pe.wait_ge(S("m0_w_low"), 2 * n_in + j + 1)
                if j == 1:
                    pe.wait_ge(S("m0_yT"), NT + 1)
                for t in range(NT):
                    n = (j // 2) * NT + t
                    if n >= 8 and j % 2 == 0:
                        pe.wait_ge(S("m0_out_read"), n - 7)

                    def y_cols(kl):
                        k = (j % 2) * KH + kl
                        cols = slice(t * P, (t + 1) * P)
                        return aTh[:, k, cols], yrTl[:, k, cols] if k < 4 else aTl[:, k, cols]

                    ins = product(pe, PS[:, n % 8], y_cols, lambda kl: (wh[:, j % 2, kl], wl[1][:, j % 2, kl]), j)
                    if j % 2 == 1:
                        ins.then_inc(S("m0_out"), 1)
                    elif t == NT - 1:
                        ins.then_inc(S("m0_w_used"), 1)

        @block.vector
        def _(dve):
            norm_modulate(dve, S, T, h, a, ss, rows, PS, norm_pairs, aTh, aTl, wh, wl)
            split_low(dve, S, T, wh, wl, 2)
            dve.wait_ge(S("m0_tabs"), 80)
            dve.wait_ge(S("m0_aT_ps"), NT)
            for t in range(NT):
                dve.wait_ge(S("m0_proj"), t + 1)
                if t < CT:
                    dve.tensor_copy(sg[:, t], PS[:, t % 8]).then_inc(S("m0_qk"), 1)
                else:
                    rope(dve, S, T, t - CT, [sg[:, t].rearrange("p (h n) -> p h n", h=8)], PS[:, t % 8], a[:, 0, 0:HALF],
                         a[:, 0, HALF:D], cos[:, t - CT], sin[:, t - CT], 8)
                    dve.wait_ge(S("m0_rope_out"), t - CT + 1)
                    dve.sem_inc(S("m0_qk"), 1)
            for j in range(3, 2 * n_in + 1):
                split_low(dve, S, T, wh, wl, j)
            for i in range(n_ch):
                n = n_tok + 2 * n_ch + i
                m, th = divmod(i, 2)
                dve.wait_ge(S("m0_proj"), n + 1)
                dve.wait_ge(S("m0_ev"), 2 * NT + n_ch + i + 1)
                seg = u[:, m, th * 3 * P:(th + 1) * 3 * P]
                dve.tensor_tensor(seg, seg, PS[:, n % 8, 0:3 * P], ALU.mult).then_inc(S("m0_u"), 1)
            links = 0

            def link(ins):
                nonlocal links
                links += 1
                ins.then_inc(S("m0_link"), 1)
                dve.wait_ge(S("m0_link"), links)

            def head_norm(hd, kd):
                g = 2 * hd + kd
                nt, t0 = (LT, CT) if kd else (CT, 0)
                dve.wait_ge(S("m0_ret_sq"), 2 * g + 1)
                dve.tensor_reduce(hs[:, 0, g, 0:nt], sq[:, 0:nt * P].rearrange("p (t n) -> p t n", t=nt), AX.X, ALU.add
                                  ).then_inc(S("m0_ret_ss"), 1)
                dve.wait_ge(S("m0_ret_ss"), 2 * g + 1)
                dve.tensor_scalar(hs[:, 1, g, 0:nt], hs[:, 0, g, 0:nt], 1.0 / RET_V, EPS, ALU.mult, ALU.add
                                  ).then_inc(S("m0_ret_ss"), 1)
                dve.wait_ge(S("m0_ret_sq"), 2 * g + 2)
                link(dve.reciprocal(hs[:, 3, g, 0:nt], hs[:, 2, g, 0:nt]))
                for it in range(nt):
                    cols = slice(hd * RET_V, (hd + 1) * RET_V)
                    ins = dve.scalar_tensor_tensor(yr[:, t0 + it, cols], PS[:, 4 + kd, it * P:(it + 1) * P], hs[:, 3, g, it:it + 1],
                                                   sg[:, t0 + it, cols], ALU.mult, ALU.mult)
                ins.then_inc(S("m0_ret_y"), 1)

            for i, (hd, kd, j) in enumerate(items):
                if i == 0:
                    dve.wait_ge(S("m0_strip0"), 16)
                if i == CT + NT:
                    split_low(dve, S, T, wh, wl, 2 * n_in + 1)
                    dve.wait_ge(S("m0_strips"), 16)
                dve.wait_ge(S("m0_S"), i + 1)
                if i >= 4:
                    dve.wait_ge(S("m0_pv"), i - 3)
                if kd == 0:
                    x, nq = 3 * P - j * P, CTX
                elif j < CT:
                    x, nq = SL + P - j * P, SEQ
                else:
                    x, nq = 3 * P - (j - CT) * P, SEQ
                dve.tensor_tensor(PT[:, i % 4, 0:nq], PS[:, 2 + i % 2, 0:nq], strips[:, hd, x:x + nq], ALU.mult
                                  ).then_inc(S("m0_P"), 1)
                if kd == 0 and j == CT - 1 and hd:
                    head_norm(hd - 1, 1)
                if kd == 1 and j == 2:
                    head_norm(hd, 0)
            head_norm(RET_HEADS - 1, 1)
            for t in range(NT):
                dve.wait_ge(S("m0_yT_high"), t + 1)
                tile = slice(t * P, (t + 1) * P)
                dve.tensor_tensor(yrTl[:, :, tile], PS[:, yT_bank[t]].rearrange("p (b n) -> p b n", b=4), aTh[:, 0:4, tile].bitcast(F32),
                                  ALU.subtract).then_inc(S("m0_yT"), 1)
            dve.wait_ge(S("m0_yT_high"), NT + 1)
            dve.tensor_tensor(aTl[:, 4:8], yc, aTh[:, 4:8].bitcast(F32), ALU.subtract).then_inc(S("m0_yT"), 1)
            split_low(dve, S, T, wh, wl, 2 * n_in + 2)
            dve.wait_ge(S("m0_P"), len(items))
            dve.wait_ge(S("m0_pv"), len(items))
            residual(dve, S, T, h, PS, rows, PT, list(range(NT)), lambda n: n % 8, lambda: split_low(dve, S, T, wh, wl, 2 * n_in + 3))


def mixer1_stage(nc, S, A, h, ident, mod_d, arena, rows):
    BAND = P + 2 * 128
    chunks = [("od_w_in", 0), ("od_w_in", 1), ("od_w_in", 2), ("od_w_out", 0), ("od_w_out", 1)]
    with ExitStack() as ctx:
        def sb(name, shape, dt=F32):
            return ctx.enter_context(nc.sbuf_tensor("m1_" + name, shape, dt))
        plain_high, aTh = twins(nc, ctx, "m1_aT_high", [P, KC * TOK])
        plain_low, aTl = twins(nc, ctx, "m1_aT_low", [P, KC * TOK])
        wh = sb("w_high", [P, 2, KH, HALF], F32R)
        wl = twins(nc, ctx, "m1_w_low", [P, 2, KH, HALF])
        cuts = Arena(arena[:])
        qT = sb("qT", [P, ATT_HEADS // 2, SEQ])
        kT = sb("kT", [P, KV_HEADS, TOK])
        v = sb("v", [P, NT, KV_HEADS, 2, HD])
        qtok = cuts.cut(4, HALF)
        ktok = cuts.cut(2, KV_HEADS, 2 * HD)
        cos = cuts.cut(LT, HD)
        sin = cuts.cut(LT, HD)
        ss = sb("ss", [P, 4, NT])
        a = cuts.cut(2, D)
        sq = cuts.cut(D)
        mask = sb("mask", [P, BAND])
        sink = sb("sink", [P, ATT_HEADS])
        PS = ctx.enter_context(nc.psum_tensor("m1_ps", [P, 8, HALF], F32))
        block = ctx.enter_context(nc.Block())
        T = "m1"
        n_oT, WIDE = KC * SEQ, CTX + BAND + 1
        oTh, oTl = (x[:, 0:n_oT].rearrange("p (k n) -> p k n", k=KC) for x in (aTh, aTl))
        high_rest, low_rest = (Arena(x[:, n_oT:]) for x in (plain_high, plain_low))
        pT = high_rest.cut(2, CTX + BAND)
        st = high_rest.cut(4, LT * ATT_HEADS)
        dg = high_rest.cut(2, P)
        pr = low_rest.cut(3, WIDE)
        aTh, aTl = (x[:].rearrange("p (k n) -> p k n", k=KC) for x in (aTh, aTl))
        norm_pairs = (0, 6) * (NT // 2)
        n_q = 2 * LT
        items = [(b, hd) for b in range(LT) for hd in range(ATT_HEADS)]

        def window(b):
            return max(b - 1, 0), min(b + 2, LT)

        def keys(b):
            lo, hi = window(b)
            return CTX + lo * P, (hi - lo) * P

        def key_tiles(b):
            lo, hi = window(b)
            return list(range(CT)) + [CT + j for j in range(lo, hi)]

        @block.sync
        def _(sp):
            load_rows(sp, S, mod_d, rows, 1, 0, "m1_rows", parts=slice(0, 2))
            for j in range(2 * len(chunks)):
                if j >= 2:
                    c = (j - 2) // 2
                    if j % 2 == 0:
                        sp.wait_ge(S("m1_w_used"), c + 1)
                    elif c < 3:
                        sp.wait_ge(S("m1_proj"), (LT, 2 * LT, 2 * LT + NT)[c])
                    else:
                        sp.wait_ge(S("m1_out"), LT)
                name, c = chunks[j // 2]
                load_half(sp, S, T, wl, A[name][0], j, slice(c * HALF, (c + 1) * HALF))
                if j == 1:
                    sp.dma_start(cos, A["rope_cos"].rearrange("(t p) n -> p t n", p=P)).then_inc(S("m1_tabs"), 16)
                    sp.dma_start(sin, A["rope_sin"].rearrange("(t p) n -> p t n", p=P)).then_inc(S("m1_tabs"), 16)
                    sp.dma_start(sink[:], A["attn_sinks"].broadcast_to([P, ATT_HEADS])).then_inc(S("m1_tabs"), 16)
                    load_rows(sp, S, mod_d, rows, 1, 0, "m1_tabs", parts=slice(2, 3))
            sp.wait_ge(S("m1_a"), NT)
            load_rows(sp, S, mod_d, rows, 1, 1, "peer_rows", peer_kinds(1), slice(0, 2))
            sp.wait_ge(S("m1_kT"), NT)
            sp.wait_ge(S("m1_v"), NT)
            load_ahead_for_peer(sp, S, A, mod_d, arena, 1)

        @block.gpsimd
        def _(pool):
            norm_shift(pool, S, T, a, rows)
            pool.memset(mask[:], 0.0).then_inc(S("m1_mask"), 1)
            pool.wait_ge(S("m1_mask"), 1)
            pool.affine_select(out=mask[:], in_=mask[:], compare_op=ALU.is_ge, fill=NEG, base=0, pattern=[[1, BAND]],
                               channel_multiplier=-1).then_inc(S("m1_mask"), 1)
            pool.wait_ge(S("m1_mask"), 2)
            pool.affine_select(out=mask[:], in_=mask[:], compare_op=ALU.is_ge, fill=NEG, base=2 * 128, pattern=[[-1, BAND]],
                               channel_multiplier=1).then_inc(S("m1_mask"), 1)

        @block.scalar
        def _(act):
            norm_squares(act, S, T, h, sq, ss)
            norm_evacuate(act, S, T, PS, norm_pairs, aTh, wh, wl)
            for n in range(n_q):
                if n % LT == 0:
                    for j in (2, 3) if n == 0 else (4, 5):
                        split_high(act, S, T, wh, wl, j)
                act.wait_ge(S("m1_qT_ps"), n + 1)
                c, t = divmod(n, LT)
                act.activation(qT[:, 4 * c:4 * c + 4, t * P:(t + 1) * P], PS[:, n % 2].rearrange("p (m n) -> p m n", m=4), ACT.Copy
                               ).then_inc(S("m1_qT"), 1)
            for t in range(NT):
                act.wait_ge(S("m1_kT_ps"), t + 1)
                act.activation(kT[:, :, t * P:(t + 1) * P], PS[:, t % 2].rearrange("p (m n) -> p m n", m=4), ACT.Copy
                               ).then_inc(S("m1_kT"), 1)

            def probs(i):
                b, hd = items[i]
                w_all = CTX + keys(b)[1] + 1
                act.wait_ge(S("m1_max"), 2 * i + 2)
                act.activation(pr[:, i % 3, 0:w_all], pr[:, i % 3, 0:w_all], ACT.Exp, bias=st[:, 1, i:i + 1],
                               accum_out=st[:, 2, i:i + 1]).then_inc(S("m1_probs"), 1)

            def inverse_sums(i):
                act.wait_ge(S("m1_recip"), i + 1)
                if i >= 2:
                    act.wait_ge(S("m1_pT_ps"), i - 1)
                act.activation(dg[:, i % 2], ident[:], ACT.Copy, scale=st[:, 3, i:i + 1]).then_inc(S("m1_diag"), 1)

            def transposed(i):
                b, hd = items[i]
                n = CTX + keys(b)[1]
                act.wait_ge(S("m1_pT_ps"), i + 1)
                if i >= 2:
                    act.wait_ge(S("m1_o"), i - 1)
                act.activation(pT[:, i % 2, 0:n], PS[:, 4:6].rearrange("p b n -> p (b n)")[:, 0:n], ACT.Copy).then_inc(S("m1_pT"), 1)

            def output_high(i):
                b, hd = items[i]
                p0 = (hd % 2) * HD
                act.wait_ge(S("m1_o"), i + 1)
                act.activation(oTh[p0:p0 + HD, hd // 2, b * P:(b + 1) * P], PS[p0:p0 + HD, 6 + i % 2, 0:P], ACT.Copy
                               ).then_inc(S("m1_oT_high"), 1)

            for i in range(len(items) + 4):
                if 1 <= i <= len(items):
                    inverse_sums(i - 1)
                if 2 <= i <= len(items) + 1:
                    transposed(i - 2)
                if i >= 4:
                    output_high(i - 4)
                if i < len(items):
                    probs(i)
                if i in (4, 8):
                    split_high(act, S, T, wh, wl, 5 + i // 4)
            for j in (8, 9):
                split_high(act, S, T, wh, wl, j)

        @block.tensor
        def _(pe):
            def q_transpose(n):
                pe.wait_ge(S("m1_rope_out"), n + 1)
                if n >= 2:
                    pe.wait_ge(S("m1_qT"), n - 1)
                for m in range(4):
                    ins = pe.transpose(PS[:, n % 2, m * P:(m + 1) * P], qtok[:, n % 4, m * P:(m + 1) * P], ident[:])
                ins.then_inc(S("m1_qT_ps"), 1)

            def k_transpose(t):
                pe.wait_ge(S("m1_k"), t + 1)
                if t >= 2:
                    pe.wait_ge(S("m1_kT"), t - 1)
                else:
                    pe.wait_ge(S("m1_qT"), n_q - 1 + t)
                for m in range(4):
                    ins = pe.transpose(PS[:, t % 2, m * P:(m + 1) * P], ktok[:, t % 2, m], ident[:])
                ins.then_inc(S("m1_kT_ps"), 1)

            def unit(j, n):
                t = CT + n % LT if n < n_q else n - n_q

                def a_tile(kl):
                    k = (j % 2) * KH + kl
                    return aTh[:, k, t * P:(t + 1) * P], aTl[:, k, t * P:(t + 1) * P]

                return product(pe, PS[:, 2 + n % 6], a_tile, lambda kl: (wh[:, j % 2, kl], wl[1][:, j % 2, kl]), j)

            def first_unit(t):
                if t == CT:
                    pe.wait_ge(S("m1_w_low"), 1)
                if t >= CT:
                    ins = unit(0, t - CT)
                if t == NT - 1:
                    ins.then_inc(S("m1_w_used"), 1)

            norm_transpose(pe, S, T, PS, norm_pairs, a, ident, first_unit)
            for j in range(1, 6):
                units = (range(0, LT), range(LT, n_q), range(n_q, n_q + NT))[j // 2]
                pe.wait_ge(S("m1_w_low"), j + 1)
                for n in units:
                    if n >= 6 and j % 2 == 0:
                        if n - 6 < n_q:
                            pe.wait_ge(S("m1_rope_out"), n - 5)
                        else:
                            pe.wait_ge(S("m1_v"), n - 6 - n_q + 1)
                    ins = unit(j, n)
                    if j % 2 == 1:
                        ins.then_inc(S("m1_proj"), 1)
                    elif n == units[-1]:
                        ins.then_inc(S("m1_w_used"), 1)
                    if j in (2, 4) and n - units[0] < LT:
                        q_transpose(n - LT)
                    if j == 5 and n > n_q:
                        k_transpose(n - n_q - 1)
            k_transpose(NT - 1)
            pe.wait_ge(S("m1_kT"), NT)
            pe.wait_ge(S("m1_v"), NT)

            def scores(i):
                b, hd = items[i]
                kv, p0, s0 = hd // (ATT_HEADS // KV_HEADS), (hd % 2) * HD, 2 * (i % 2)
                at, n = keys(b)
                if i >= 2:
                    pe.wait_ge(S("m1_logits"), i - 1)
                q = qT[p0:p0 + HD, hd // 2, b * P:(b + 1) * P]
                pe.matmul(PS[:, s0, 0:CTX], q, kT[p0:p0 + HD, kv, 0:CTX], start=True, stop=True)
                pe.matmul(PS[:, s0 + 1, 0:n], q, kT[p0:p0 + HD, kv, at:at + n], start=True, stop=True).then_inc(S("m1_S"), 1)

            def transposes(i):
                b, hd = items[i]
                pe.wait_ge(S("m1_probs"), i + 1)
                pe.wait_ge(S("m1_diag"), i + 1)
                if i >= 1:
                    pe.wait_ge(S("m1_pT"), i)
                for m in range(len(key_tiles(b))):
                    ins = pe.matmul(PS[:, 4 + m // 4, (m % 4) * P:(m % 4 + 1) * P], pr[:, i % 3, m * P:(m + 1) * P], dg[:, i % 2],
                                    start=True, stop=True, skip_group_check=True)
                ins.then_inc(S("m1_pT_ps"), 1)

            def values(i):
                b, hd = items[i]
                kv, tiles = hd // (ATT_HEADS // KV_HEADS), key_tiles(b)
                pe.wait_ge(S("m1_pT"), i + 1)
                if i >= 2:
                    pe.wait_ge(S("m1_oT"), i - 1)
                for m, t in enumerate(tiles):
                    ins = pe.matmul(PS[:, 6 + i % 2, 0:P], v[:, t, kv].rearrange("p a n -> p (a n)"), pT[:, i % 2, m * P:(m + 1) * P],
                                    start=m == 0, stop=m == len(tiles) - 1)
                ins.then_inc(S("m1_o"), 1)

            for i in range(len(items) + 3):
                if i < len(items):
                    scores(i)
                if 2 <= i <= len(items) + 1:
                    transposes(i - 2)
                if i >= 3:
                    values(i - 3)
            pe.wait_ge(S("m1_oT"), len(items))
            for j in range(6, 10):
                pe.wait_ge(S("m1_w_low"), j + 1)
                for t in range(LT):
                    n = (j // 2 - 3) * LT + t

                    def o_tile(kl):
                        k = (j % 2) * KH + kl
                        return oTh[:, k, t * P:(t + 1) * P], oTl[:, k, t * P:(t + 1) * P]

                    ins = product(pe, PS[:, n], o_tile, lambda kl: (wh[:, j % 2, kl], wl[1][:, j % 2, kl]), j)
                    if j % 2 == 1:
                        ins.then_inc(S("m1_out"), 1)
                    elif t == LT - 1:
                        ins.then_inc(S("m1_w_used"), 1)

        @block.vector
        def _(dve):
            norm_modulate(dve, S, T, h, a, ss, rows, PS, norm_pairs, aTh, aTl, wh, wl)
            split_low(dve, S, T, wh, wl, 2)
            dve.wait_ge(S("m1_tabs"), 80)
            dve.wait_ge(S("m1_aT_ps"), NT)
            t1, t2 = a[:, 0, 0:HALF], a[:, 0, HALF:D]
            for n in range(n_q):
                if n == LT:
                    split_low(dve, S, T, wh, wl, 3)
                    split_low(dve, S, T, wh, wl, 4)
                dve.wait_ge(S("m1_proj"), n + 1)
                if n >= 4:
                    dve.wait_ge(S("m1_qT_ps"), n - 3)
                rope(dve, S, T, n, [qtok[:, n % 4].rearrange("p (h n) -> p h n", h=8)], PS[:, 2 + n % 6], t1, t2,
                     cos[:, n % LT], sin[:, n % LT], 8)
            split_low(dve, S, T, wh, wl, 5)
            for t in range(NT):
                n = n_q + t
                ps = PS[:, 2 + n % 6]
                dve.wait_ge(S("m1_proj"), n + 1)
                if t >= 2:
                    dve.wait_ge(S("m1_kT_ps"), t - 1)
                outs = [ktok[:, t % 2, :, x * HD:(x + 1) * HD] for x in range(2)]
                if t < CT:
                    for x, o in enumerate(outs):
                        ins = dve.tensor_copy(o, ps[:, 0:KV_HEADS * HD].rearrange("p (h n) -> p h n", h=KV_HEADS))
                    ins.then_inc(S("m1_k"), 1)
                else:
                    rope(dve, S, T, n_q + t - CT, outs, ps[:, 0:KV_HEADS * HD], t1, t2, cos[:, t - CT], sin[:, t - CT], KV_HEADS)
                    dve.wait_ge(S("m1_rope_out"), n_q + t - CT + 1)
                    dve.sem_inc(S("m1_k"), 1)
                dve.tensor_copy(v[:, t], ps[:, KV_HEADS * HD:HALF].rearrange("p (h o n) -> p h o n", h=KV_HEADS, o=1)
                                .broadcast_to([P, KV_HEADS, 2, HD])).then_inc(S("m1_v"), 1)
            dve.wait_ge(S("m1_mask"), 3)

            def logits(i):
                b, hd = items[i]
                n = keys(b)[1]
                m0 = P if b == 0 else 0
                dve.wait_ge(S("m1_S"), i + 1)
                if i >= 3:
                    dve.wait_ge(S("m1_pT_ps"), i - 2)
                L = pr[:, i % 3]
                dve.tensor_scalar(L[:, 0:CTX], PS[:, 2 * (i % 2), 0:CTX], SCALE, None, ALU.mult)
                dve.tensor_copy(L[:, CTX + n:CTX + n + 1], sink[:, hd:hd + 1])
                dve.scalar_tensor_tensor(L[:, CTX:CTX + n], PS[:, 2 * (i % 2) + 1, 0:n], SCALE, mask[:, m0:m0 + n], ALU.mult, ALU.add
                                         ).then_inc(S("m1_logits"), 1)
                if i >= 1:
                    inverse(i - 1)
                dve.wait_ge(S("m1_logits"), i + 1)
                dve.tensor_reduce(st[:, 0, i:i + 1], L[:, 0:CTX + n + 1], AX.X, ALU.max).then_inc(S("m1_max"), 1)
                dve.wait_ge(S("m1_max"), 2 * i + 1)
                dve.tensor_scalar(st[:, 1, i:i + 1], st[:, 0, i:i + 1], -1.0, None, ALU.mult).then_inc(S("m1_max"), 1)

            def inverse(i):
                dve.wait_ge(S("m1_probs"), i + 1)
                dve.reciprocal(st[:, 3, i:i + 1], st[:, 2, i:i + 1]).then_inc(S("m1_recip"), 1)

            def output(i):
                b, hd = items[i]
                p0 = (hd % 2) * HD
                part = (slice(p0, p0 + HD), hd // 2, slice(b * P, (b + 1) * P))
                dve.wait_ge(S("m1_oT_high"), i + 1)
                dve.tensor_tensor(oTl[part], PS[p0:p0 + HD, 6 + i % 2, 0:P], oTh[part].bitcast(F32), ALU.subtract
                                  ).then_inc(S("m1_oT"), 1)

            for i in range(len(items) + 4):
                if i < len(items):
                    logits(i)
                if i == len(items):
                    inverse(i - 1)
                if i >= 4:
                    output(i - 4)
                if i in (4, 8):
                    split_low(dve, S, T, wh, wl, 5 + i // 4)
            split_low(dve, S, T, wh, wl, 8)
            residual(dve, S, T, h, PS, rows, qT[:, 0:2], [CT + t for t in range(LT)], lambda n: n, lambda: split_low(dve, S, T, wh, wl, 9))


R_LINKS = 19
R_PIECES = 4

PAIRS_T = NH * PAIRS
ACT_SQUARE, DVE_MEAN, ACT_ROOT, DVE_MOD = 1, 3, 4, 6
PE_F_T, ACT_F_T, PE_Q, ACT_Q, PE_Q_T, ACT_Q_T, PE_S, ACT_S = 8, 10, 12, 22, 24, 26, 28, 32
ROUTE_NOW = {3: 6, 8: 7}
ROUTE_FIRST = {4 * n: LAG + n for n in range(NH - LAG)}
ROUTE_NEXT = {33 + 4 * n: n for n in range(NH - LAG)}


def peer_stage(nc, S, A, h, ident, mod_d, arena, rows, layer, t0, first, n_tiles):
    T = f"peer{layer}_"
    TS = NH * TOPK
    with ExitStack() as ctx:
        def sb(name, shape, dt=F32):
            return ctx.enter_context(nc.sbuf_tensor(T + name, shape, dt))

        def sem(name):
            return S("peer_" + name)

        ring = sb("ring", [P, RING, 2 * D])
        wq, keys = peer_buffers(arena)
        f = sb("f", [P, D])
        fn = sb("fn", [P, D])
        fT = sb("fT", [P, KC, P])
        q = sb("q", [P, D])
        qT = sb("qT", [P, NH, P])
        sc = sb("scores", [P, 2, 2, NH // 2, NK])
        y = sb("y", [P, D])
        diag = sb("diag", [P, RING, P])
        ss = sb("ss", [P, 4])
        iota = sb("iota", [P, TOPK])
        top = sb("top", [P, 2, TOPK])
        topi = sb("topi", [P, 2, TOPK], U32)
        topf = sb("topf", [P, 2, TOPK])
        cand = sb("cand", [P, TOPK, TOPK])
        cs = sb("cs", [P, NH, TOPK])
        ci = sb("ci", [P, TOPK], U32)
        ab = sb("ab", [P, 2, TOPK], U32)
        abf = sb("abf", [P, 2, TOPK])
        hot = sb("hot", [P, 2, TOPK, TOPK])
        e12 = sb("e12", [P, 2, TOPK])
        ef = sb("ef", [P, TOPK])
        idx = sb("idx", [P, NH, TOPK], U32)
        negm = sb("negm", [P, NH])
        gexp = sb("gexp", [P, NH, TOPK])
        gsum = sb("gsum", [P, NH])
        grec = sb("grec", [P, NH])
        u = sb("u", [P, 4, PAIR])
        gel = sb("gel", [P, 4, PAIR])
        coef = sb("coef", [P, 4, PAIR])
        PY = ctx.enter_context(nc.psum_tensor(T + "py", [P, 2, 2, HALF], F32))
        PB = ctx.enter_context(nc.psum_tensor(T + "pb", [P, 4, HALF], F32))
        block = ctx.enter_context(nc.Block())

        rows_loads = sum(len(peer_kinds(l)) for l in range(layer + 1))
        shift = first - t0

        def wait_apart(eng, which, value):
            eng.wait_ge(which, value)
            eng.sem_inc(sem("passed_" + ("pool" if eng is nc.gpsimd else "dve")), 1)

        def row_kind(t):
            return (t - shift + CT) // LT if t0 < CT else 1

        def tiles(eng, body):
            body(first, ROUTE_FIRST, ROUTE_NEXT)
            with eng.Fori(first + 1, first + n_tiles - 1) as i:
                body(i, ROUTE_NOW, ROUTE_NEXT)
            body(first + n_tiles - 1, ROUTE_NOW, {})

        def heads_at(g, table):
            return [table[g]] if g in table else []

        @block.sync
        def _(sp):
            load_rows(sp, S, mod_d, rows, layer, 1, "peer_gates", peer_kinds(layer), slice(2, 3))

        @block.gpsimd
        def _(pool):
            pool.iota(iota[:], [[1, TOPK]], base=0, channel_multiplier=0, allow_small_or_imprecise_dtypes=True
                      ).then_inc(sem("iota"), 1)

            def body(i, now, nxt):
                for hd in range(NH):
                    pool.wait_ge(sem("idx"), i * NH + hd + 1)
                    for j in range(TOPK):
                        s = hd * TOPK + j
                        wait_apart(pool, sem("slot_free"), i * TS + s + 1)
                        pool.indirect_dma_start(ring[:, s % RING], None, A["uv"], bass.IndirectOffsetOnAxis(idx[:, hd, j:j + 1], 0)
                                                ).then_inc(sem(f"landed{s % RING}"), 16)
            tiles(pool, body)

        @block.scalar
        def _(act):
            def prep(i, step):
                if step == "square":
                    act.activation(q[:], h[:, i - shift], ACT.Square, accum_out=ss[:, 0:1]).then_inc(sem("square"), 1)
                elif step == "root":
                    act.wait_ge(sem("mean"), i + 1)
                    act.activation(ss[:, 2:3], ss[:, 1:2], ACT.Sqrt).then_inc(sem("root"), 1)
                elif step == "fT":
                    act.wait_ge(sem("fT_ps"), i + 1)
                    act.activation(fT[:], PB[:, 0:2].rearrange("p b (k n) -> p (b k) n", k=4), ACT.Copy).then_inc(sem("fT"), 1)
                elif step == "q":
                    act.wait_ge(sem("q_ps"), i + 1)
                    act.activation(q[:], PB[:, 2:4].rearrange("p b n -> p (b n)"), ACT.Copy).then_inc(sem("q"), 1)
                elif step == "qT":
                    act.wait_ge(sem("qT_ps"), i + 1)
                    act.activation(qT[:], PB[:, 0:2].rearrange("p b (k n) -> p (b k) n", k=4), ACT.Copy).then_inc(sem("qT"), 1)
                elif step == "s":
                    act.wait_ge(sem("s_ps"), i + 1)
                    if i is not first or first:
                        act.wait_ge(sem("idx"), i * NH)
                    act.activation(sc[:].rearrange("p g a h n -> p (g a h n)"), PB[:].rearrange("p b n -> p (b n)"), ACT.Copy
                                   ).then_inc(sem("s"), 1)

            def prep_first(part):
                cols, hds = slice(part * HALF, (part + 1) * HALF), slice(4 * part, 4 * part + 4)

                def ready(step, name):
                    if part:
                        act.wait_ge(sem(name + "_ps"), first + 1)
                    else:
                        act.wait_ge(sem("first_pe"), 3 * layer + step)

                def done(name):
                    return sem(name if part else "first_act")

                ready(1, "q")
                act.activation(q[:, cols], PB[:, 2 + part], ACT.Copy).then_inc(done("q"), 1)
                ready(2, "qT")
                act.activation(qT[:, hds], PB[:, 2 * part].rearrange("p (k n) -> p k n", k=4), ACT.Copy).then_inc(done("qT"), 1)
                ready(3, "s")
                if first:
                    act.wait_ge(sem("idx"), first * NH)
                act.activation(sc[:, part].rearrange("p g h n -> p (g h n)"), PB[:, 2 * part:2 * part + 2].rearrange("p b n -> p (b n)"),
                               ACT.Copy).then_inc(done("s"), 1)

            def gate(i, hd):
                act.wait_ge(sem("negm"), i * NH + hd + 1)
                act.activation(gexp[:, hd], cs[:, hd], ACT.Exp, bias=negm[:, hd:hd + 1], accum_out=gsum[:, hd:hd + 1]
                               ).then_inc(sem("gexp"), 1)

            for step in ("square", "root", "fT"):
                prep(first, step)
            for part in range(2):
                prep_first(part)
            for hd in range(LAG):
                gate(first, hd)

            def body(i, now, nxt):
                for g in range(PAIRS_T):
                    act.wait_ge(sem("dot"), i * TS + PAIR * (g + 1))
                    act.activation(gel[:, g % 4], u[:, g % 4], ACT.Gelu).then_inc(sem("gelu"), 1)
                    act.wait_ge(sem("coef"), i * PAIRS_T + g + 1)
                    for j in range(PAIR):
                        act.activation(diag[:, (PAIR * g + j) % RING], ident[:], ACT.Copy, scale=coef[:, g % 4, j:j + 1]
                                       ).then_inc(sem("diag"), 1)
                    for hd in heads_at(g - R_PIECES, now):
                        gate(i, hd)
                    for hd in heads_at(g - R_PIECES, nxt):
                        gate(i + 1, hd)
                    if not nxt:
                        continue
                    for at, step in ((ACT_SQUARE, "square"), (ACT_ROOT, "root"), (ACT_F_T, "fT"), (ACT_Q, "q"),
                                     (ACT_Q_T, "qT"), (ACT_S, "s")):
                        if g == at:
                            prep(i + 1, step)
            tiles(act, body)

        @block.tensor
        def _(pe):
            def f_transposes(i):
                pe.wait_ge(sem("fn"), i + 1)
                for k in range(KC):
                    ins = pe.transpose(PB[:, k // 4, (k % 4) * P:(k % 4 + 1) * P], fn[:, k * P:(k + 1) * P], ident[:])
                ins.then_inc(sem("fT_ps"), 1)

            def queries(i, k):
                if k == 0:
                    pe.wait_ge(sem("fT"), i + 1)
                for b in range(2):
                    ins = pe.matmul(PB[:, 2 + b], fT[:, k], wq[:, k, b * HALF:(b + 1) * HALF], start=k == 0, stop=k == KC - 1)
                if k == KC - 1:
                    ins.then_inc(sem("q_ps"), 1)

            def q_transposes(i):
                pe.wait_ge(sem("q"), i + 1)
                for k in range(KC):
                    ins = pe.transpose(PB[:, k // 4, (k % 4) * P:(k % 4 + 1) * P], q[:, k * P:(k + 1) * P], ident[:])
                ins.then_inc(sem("qT_ps"), 1)

            def scores(i, part):
                if part == 0 and i is not first:
                    pe.wait_ge(sem("qT"), i + 1)
                for hd in range(4 * part, 4 * part + 4):
                    for half in range(2):
                        rng = slice(half * 64, half * 64 + 64)
                        ins = pe.matmul(PB[:, 2 * part + half, (hd % 4) * NK:(hd % 4 + 1) * NK], qT[rng, hd], keys[rng, hd],
                                        start=True, stop=True, skip_group_check=True)
                if part == 1:
                    ins.then_inc(sem("s_ps"), 1)
                elif i is first:
                    ins.then_inc(sem("first_pe"), 1)

            if layer == 0:
                pe.sem_inc(sem("slot_free"), RING)
            pe.wait_ge(S("ident"), 2)
            f_transposes(first)
            pe.wait_ge(sem("wq"), 16 * (layer + 1))
            pe.wait_ge(sem("keys"), 16 * (layer + 1))
            pe.wait_ge(sem("fT"), first + 1)
            for part in range(2):
                for k in range(KC):
                    ins = pe.matmul(PB[:, 2 + part], fT[:, k], wq[:, k, part * HALF:(part + 1) * HALF], start=k == 0, stop=k == KC - 1)
                ins.then_inc(sem("q_ps" if part else "first_pe"), 1)
                if part:
                    pe.wait_ge(sem("q"), first + 1)
                else:
                    pe.wait_ge(sem("first_act"), 3 * layer + 1)
                for k in range(4):
                    ins = pe.transpose(PB[:, 2 * part, k * P:(k + 1) * P], q[:, part * HALF + k * P:part * HALF + (k + 1) * P], ident[:])
                ins.then_inc(sem("qT_ps" if part else "first_pe"), 1)
                if part:
                    pe.wait_ge(sem("qT"), first + 1)
                else:
                    pe.wait_ge(sem("first_act"), 3 * layer + 2)
                scores(first, part)

            def body(i, now, nxt):
                for g in range(PAIRS_T):
                    hd = g // PAIRS
                    if g % PAIRS == 0:
                        pe.wait_ge(sem("y_free"), i * NH + hd + 1)
                    for j in range(PAIR):
                        s = PAIR * g + j
                        pe.wait_ge(sem("diag"), i * TS + s + 1)
                        for b in range(2):
                            ins = pe.matmul(PY[:, hd % 2, b], diag[:, s % RING], ring[:, s % RING, D + b * HALF:D + (b + 1) * HALF],
                                            start=s % TOPK == 0, stop=s % TOPK == TOPK - 1)
                        ins.then_inc(sem("slot_free"), 1)
                    if not nxt:
                        continue
                    if g == PE_F_T:
                        f_transposes(i + 1)
                    if PE_Q <= g < PE_Q + KC:
                        queries(i + 1, g - PE_Q)
                    if g == PE_Q_T:
                        q_transposes(i + 1)
                    if PE_S <= g < PE_S + 2:
                        scores(i + 1, g - PE_S)
            tiles(pe, body)

        @block.vector
        def _(dve):
            def mean(i):
                dve.wait_ge(sem("square"), i + 1)
                dve.tensor_scalar(ss[:, 1:2], ss[:, 0:1], 1.0 / D, EPS, ALU.mult, ALU.add).then_inc(sem("mean"), 1)

            def modulate(i):
                dve.wait_ge(sem("root"), i + 1)
                dve.reciprocal(ss[:, 3:4], ss[:, 2:3]).then_inc(sem("rstd"), 1)
                dve.wait_ge(sem("rstd"), i + 1)
                dve.scalar_tensor_tensor(fn[:], h[:, i - shift], ss[:, 3:4], rows[:, row_kind(i), 1], ALU.mult, ALU.mult
                                         ).then_inc(sem("fn_scaled"), 1)
                dve.wait_ge(sem("fn_scaled"), i + 1)
                dve.tensor_tensor(fn[:], fn[:], rows[:, row_kind(i), 0], ALU.add).then_inc(sem("fn"), 1)

            def route(i, hd, piece):
                links = (0, 4, 8, 13)[piece]

                def link(ins):
                    nonlocal links
                    links += 1
                    ins.then_inc(sem("link"), 1)
                    wait_apart(dve, sem("link"), (i * NH + hd) * R_LINKS + links)

                def top16(out, where, values):
                    link(dve.max(out[:, 0:8], values))
                    dve.max_index(where[:, 0:8], out[:, 0:8], values).then_inc(sem("places"), 1)
                    link(dve.match_replace(values, out[:, 0:8], values, TAKEN))
                    link(dve.max(out[:, 8:16], values))
                    link(dve.max_index(where[:, 8:16], out[:, 8:16], values))

                if piece == 0 and i is first and hd < 4:
                    wait_apart(dve, sem("first_act"), 3 * layer + 3)
                elif piece == 0:
                    wait_apart(dve, sem("s"), i + 1)
                if piece < 2:
                    top16(top[:, piece], topi[:, piece], sc[:, hd // 4, piece, hd % 4])
                    return
                if piece == 2:
                    dve.tensor_copy(topf[:], topi[:]).then_inc(sem("places"), 1)
                    link(dve.tensor_tensor(cand[:], top[:, 0].rearrange("p (a b) -> p a b", b=1).broadcast_to([P, TOPK, TOPK]),
                                           top[:, 1].rearrange("p (a b) -> p a b", a=1).broadcast_to([P, TOPK, TOPK]), ALU.add))
                    top16(cs[:, hd], ci, cand[:].rearrange("p a b -> p (a b)"))
                    dve.tensor_scalar(negm[:, hd:hd + 1], cs[:, hd, 0:1], -1.0, None, ALU.mult).then_inc(sem("negm"), 1)
                    return
                dve.tensor_scalar(ab[:, 0], ci[:], 4, None, ALU.logical_shift_right).then_inc(sem("places"), 1)
                link(dve.tensor_scalar(ab[:, 1], ci[:], 15, None, ALU.bitwise_and))
                link(dve.tensor_copy(abf[:], ab[:]))
                link(dve.tensor_tensor(hot[:], abf[:].rearrange("p c (k o) -> p c k o", o=1).broadcast_to([P, 2, TOPK, TOPK]),
                                       iota[:].rearrange("p (a b m) -> p a b m", a=1, b=1).broadcast_to([P, 2, TOPK, TOPK]), ALU.is_equal))
                link(dve.tensor_tensor(hot[:], hot[:], topf[:].rearrange("p c (o m) -> p c o m", o=1).broadcast_to([P, 2, TOPK, TOPK]),
                                       ALU.mult))
                link(dve.tensor_reduce(e12[:], hot[:], AX.X, ALU.add))
                link(dve.scalar_tensor_tensor(ef[:], e12[:, 0], float(NK), e12[:, 1], ALU.mult, ALU.add))
                dve.tensor_scalar(idx[:, hd], ef[:], float(layer * EXPERTS), None, ALU.add).then_inc(sem("idx"), 1)
                dve.wait_ge(sem("idx"), i * NH + hd + 1)
                assert links == R_LINKS, links

            def denominator(i, hd):
                dve.wait_ge(sem("gexp"), i * NH + hd + 1)
                dve.reciprocal(grec[:, hd:hd + 1], gsum[:, hd:hd + 1]).then_inc(sem("grec"), 1)

            def coefficients(i, g):
                hd, at = g // PAIRS, PAIR * (g % PAIRS)
                dve.wait_ge(sem("gelu"), i * PAIRS_T + g + 1)
                if g % PAIRS == 0:
                    dve.wait_ge(sem("grec"), i * NH + hd + 1)
                dve.scalar_tensor_tensor(coef[:, g % 4], gel[:, g % 4], grec[:, hd:hd + 1], gexp[:, hd, at:at + PAIR],
                                         ALU.mult, ALU.mult).then_inc(sem("coef"), 1)

            def head_sum(i, hd):
                dve.wait_ge(sem("slot_free"), i * TS + RING + (hd + 1) * TOPK)
                ps = PY[:, hd % 2].rearrange("p b n -> p (b n)")
                if hd == 0:
                    dve.tensor_copy(y[:], ps).then_inc(sem("y_free"), 1)
                else:
                    dve.tensor_tensor(y[:], y[:], ps, ALU.add).then_inc(sem("y_free"), 1)

            if layer == 0:
                dve.sem_inc(sem("y_free"), 2)
            dve.wait_ge(sem("rows"), 16 * rows_loads)
            mean(first)
            modulate(first)
            dve.wait_ge(sem("iota"), layer + 1)
            for hd in range(LAG):
                for piece in range(R_PIECES):
                    route(first, hd, piece)
            for hd in range(LAG):
                denominator(first, hd)

            def body(i, now, nxt):
                dve.wait_ge(sem("fn"), i + 1)
                dve.tensor_copy(f[:], fn[:]).then_inc(sem("f"), 1)
                dve.wait_ge(sem("f"), i + 1)
                for g in range(PAIRS_T):
                    for j in range(PAIR):
                        s = PAIR * g + j
                        dve.wait_ge(sem(f"landed{s % RING}"), 16 * (i * (TS // RING) + s // RING + 1))
                        x = ring[:, s % RING, 0:D]
                        dve.tensor_tensor_reduce(x, x, f[:], 1.0, 0.0, ALU.mult, ALU.add, u[:, g % 4, j:j + 1]).then_inc(sem("dot"), 1)
                        if j == 0 and g:
                            coefficients(i, g - 1)
                    if g % PAIRS == 3 and g >= PAIRS:
                        dve.wait_ge(sem("y_free"), i * NH + g // PAIRS + 1)
                        head_sum(i, g // PAIRS - 1)
                    for ahead, table in ((0, now), (1, nxt)):
                        for piece in range(R_PIECES):
                            for hd in heads_at(g - piece, table):
                                route(i + ahead, hd, piece)
                        for hd in heads_at(g - R_PIECES - 2, table):
                            denominator(i + ahead, hd)
                    if not nxt:
                        continue
                    if g == DVE_MEAN:
                        mean(i + 1)
                    if g == DVE_MOD:
                        modulate(i + 1)
                coefficients(i, PAIRS_T - 1)
                dve.wait_ge(sem("y_free"), i * NH + NH + 1)
                head_sum(i, NH - 1)
                dve.wait_ge(sem("y_free"), i * NH + NH + 2)
                if i is first:
                    dve.wait_ge(sem("gates"), 16 * rows_loads)
                dve.tensor_tensor(y[:], y[:], rows[:, row_kind(i), 2], ALU.mult).then_inc(sem("gated"), 1)
                dve.wait_ge(sem("gated"), i + 1)
                dve.tensor_tensor(h[:, i - shift], h[:, i - shift], y[:], ALU.add).then_inc(sem("h"), 1)
                dve.wait_ge(sem("h"), i + 1)
            tiles(dve, body)


def final_stage(nc, S, A, h, out):
    with ExitStack() as ctx:
        gain = ctx.enter_context(nc.sbuf_tensor("fin_gain", [P, D], F32))
        o = ctx.enter_context(nc.sbuf_tensor("fin_o", [P, LT, D], F32))
        ss = ctx.enter_context(nc.sbuf_tensor("fin_ss", [P, 4, LT], F32))
        block = ctx.enter_context(nc.Block())

        @block.sync
        def _(sp):
            sp.dma_start(gain[:], A["final_norm_g"].rearrange("(a n) -> a n", a=1).broadcast_to([P, D])).then_inc(S("fin_gain"), 16)
            for t in range(LT):
                sp.wait_ge(S("fin_o"), 2 + t + 1)
                sp.dma_start(out[0].rearrange("(t p) d -> p t d", p=P)[:, t], o[:, t]).then_inc(S("stored"), 16)
            sp.wait_ge(S("stored"), 16 * LT)

        @block.scalar
        def _(act):
            for t in range(LT):
                act.activation(o[:, t], h[:, CT + t], ACT.Square, accum_out=ss[:, 0, t:t + 1]).then_inc(S("fin_sq"), 1)
            act.wait_ge(S("fin_o"), 1)
            act.activation(ss[:, 2], ss[:, 1], ACT.Sqrt).then_inc(S("fin_sq"), 1)

        @block.vector
        def _(dve):
            dve.wait_ge(S("fin_sq"), LT)
            dve.tensor_scalar(ss[:, 1], ss[:, 0], 1.0 / D, EPS, ALU.mult, ALU.add).then_inc(S("fin_o"), 1)
            dve.wait_ge(S("fin_sq"), LT + 1)
            dve.reciprocal(ss[:, 3], ss[:, 2]).then_inc(S("fin_o"), 1)
            dve.wait_ge(S("fin_o"), 2)
            dve.wait_ge(S("fin_gain"), 16)
            for t in range(LT):
                dve.scalar_tensor_tensor(o[:, t], h[:, CT + t], ss[:, 3, t:t + 1], gain[:], ALU.mult, ALU.mult
                                         ).then_inc(S("fin_o"), 1)


def backbone(nc, A, out):
    with ExitStack() as ctx:
        S = Sems(nc, ctx)
        mod_d = nc.dram_tensor("mod_rows", (DEPTH, 2, 2, 3, D), F32).ap()
        h = ctx.enter_context(nc.sbuf_tensor("h", [P, NT, D], F32))
        ident = ctx.enter_context(nc.sbuf_tensor("ident", [P, P], F32))
        arena = ctx.enter_context(nc.sbuf_tensor("arena", [P, KC * D + NH * NK], F32))
        rows_flat = ctx.enter_context(nc.sbuf_tensor("mod_rows_sb", [P, 2 * 3 * D], F32))
        rows = rows_flat[:].rearrange("p (a b n) -> p a b n", a=2, b=3)
        strips_d = nc.dram_tensor("decay_strips", (P, RET_HEADS, SL + SC), F32).ap()
        modulation_stage(nc, S, A, h, ident, mod_d, strips_d, arena, rows_flat)
        mixer0_stage(nc, S, A, h, ident, mod_d, strips_d, arena, rows)
        peer_stage(nc, S, A, h, ident, mod_d, arena, rows, 0, 0, 0, NT)
        mixer1_stage(nc, S, A, h, ident, mod_d, arena, rows)
        peer_stage(nc, S, A, h, ident, mod_d, arena, rows, 1, CT, NT, LT)
        final_stage(nc, S, A, h, out)


def _rope_tables():
    n = HD // 4
    rows, cols = np.divmod(np.arange(SEQ), GRID_W)
    inv = (np.float32(ROPE_BASE) ** (-np.arange(n, dtype=np.float32) / np.float32(n))).astype(np.float32)
    ang = np.stack([rows.astype(np.float32)[:, None] * inv, cols.astype(np.float32)[:, None] * inv], axis=1)
    cos, sin = np.cos(ang), np.sin(ang)
    return (np.stack([cos, cos], axis=2).reshape(SEQ, HD).astype(np.float32),
            np.stack([-sin, sin], axis=2).reshape(SEQ, HD).astype(np.float32))


def _lay_out(inputs):
    a = {k: np.asarray(v) for k, v in inputs.items()}
    a["rope_cos"], a["rope_sin"] = _rope_tables()
    a["gains"] = np.stack([a.pop("mix_norm_g"), a.pop("ffn_norm_g")], axis=1).reshape(DEPTH, 2 * D)
    a["conv_wT"] = a.pop("conv_w")[0].T
    keys = np.concatenate([a.pop("peer_keys1"), a.pop("peer_keys2")], axis=-1)
    a["keysT"] = keys.transpose(0, 3, 1, 2)
    a["uv"] = np.concatenate([a.pop("peer_u"), a.pop("peer_v")], axis=-1).reshape(DEPTH * EXPERTS, 2 * D)
    return {k: np.ascontiguousarray(v) for k, v in a.items()}


def kernel(**inputs):
    import concourse.bacc as _bacc
    from concourse.bass_utils import run_bass_kernel_spmd as _run

    nc = _bacc.Bacc("TRN2", target_bir_lowering=False, num_devices=1)
    arrays, args = {}, {}
    for name, a in _lay_out(inputs).items():
        arrays[f"in_{name}_dram"] = a
        args[name] = nc.dram_tensor(f"in_{name}_dram", a.shape, mybir.dt.from_np(a.dtype), kind="ExternalInput").ap()
    out = nc.dram_tensor("out_0_dram", (1, SEQ, D), F32, kind="ExternalOutput").ap()
    backbone(nc, args, out)
    r = _run(nc, [arrays], core_ids=[0])
    return r.results[0]["out_0_dram"]
```
